# Optimizing a Trainium2 kernel written in Bass

```python
import math
import jax
import jax.numpy as jnp
from jax import lax
import numpy as np
import jax, jax.numpy as jnp

D_MODEL = 1024
BATCH = 1
SEQ = 512
DEPTH = 1

CHUNK = 64
MAX_STREAM_CHUNKS = 64
POOL_WINDOWS = (2, 4, 8, 16)
POOL_GROUPS = len(POOL_WINDOWS)
D_POOL = D_MODEL // 2
POOL_GW = D_POOL // POOL_GROUPS
D_CONV = D_MODEL // 2
CONV_WIDTH = 31
N_HEADS = 8
QK_NOPE = 64
QK_ROPE = 32
V_HEAD = 64
Q_LORA = 384
KV_LORA = 256
ROPE_THETA = 10000.0
Q_BLOCK = 128
N_BRANCH = 3
OFF_CONV = D_POOL
OFF_Q = OFF_CONV + 2 * D_CONV
OFF_KV = OFF_Q + Q_LORA
OFF_KR = OFF_KV + KV_LORA
OFF_GATE = OFF_KR + QK_ROPE
D_IN = OFF_GATE + N_BRANCH * D_MODEL
IN_SPLITS = (OFF_CONV, OFF_Q, OFF_KV, OFF_KR, OFF_GATE)
N_EXPERTS = 16
N_GROUPS = 4
EXPERTS_PER_GROUP = N_EXPERTS // N_GROUPS
TOPK_GROUPS = 1
TOP_K = 2
D_EXPERT = 512
MOE_BLOCK = 128
D_PLE = 256
DEEPNORM_ALPHA = (2 * DEPTH) ** 0.25
DEEPNORM_BETA = (8 * DEPTH) ** -0.25
LN_EPS = 1e-5
RMS_EPS = 1e-6


def layer_norm(x, g, b):
    xf = x.astype(jnp.float32)
    mu = jnp.mean(xf, axis=-1, keepdims=True)
    xc = xf - mu
    var = jnp.mean(xc * xc, axis=-1, keepdims=True)
    return (xc * lax.rsqrt(var + LN_EPS) * g.astype(jnp.float32) + b.astype(jnp.float32)).astype(x.dtype)

def rms_norm(x, g):
    xf = x.astype(jnp.float32)
    ms = jnp.mean(xf * xf, axis=-1, keepdims=True)
    return (xf * lax.rsqrt(ms + RMS_EPS) * g.astype(jnp.float32)).astype(x.dtype)

def rope_tables(positions):
    inv_freq = jnp.power(ROPE_THETA, -jnp.arange(0, QK_ROPE, 2, dtype=jnp.float32) / QK_ROPE)
    ang = positions.astype(jnp.float32)[..., None] * inv_freq
    return jnp.cos(ang), jnp.sin(ang)

def apply_rope(x, cos, sin):
    cos = cos.astype(x.dtype)
    sin = sin.astype(x.dtype)
    x1, x2 = jnp.split(x, 2, axis=-1)
    return jnp.concatenate([x1 * cos - x2 * sin, x2 * cos + x1 * sin], axis=-1)

def pool_mixer(u, w_grp, scale):
    B, S, C = u.shape
    uf = u.astype(jnp.float32)
    cs = jnp.cumsum(uf, axis=1)
    t = jnp.arange(S)
    means = []
    for g, w in enumerate(POOL_WINDOWS):
        csg = cs[..., g * POOL_GW:(g + 1) * POOL_GW]
        lag = jnp.pad(csg[:, :S - w], ((0, 0), (w, 0), (0, 0)))
        cnt = jnp.minimum(t + 1, w).astype(jnp.float32)[None, :, None]
        means.append((csg - lag) / cnt)
    mixed = (jnp.concatenate(means, axis=-1) - uf).astype(u.dtype)
    mixed = jnp.einsum('bsgc,gcd->bsgd', mixed.reshape(B, S, POOL_GROUPS, POOL_GW), w_grp)
    return mixed.reshape(B, S, C) * scale

def conv_module(u2, dw, db, g, b):
    a, gate = jnp.split(u2, 2, axis=-1)
    z = a * jax.nn.sigmoid(gate)
    z = lax.conv_general_dilated(z, dw[:, None, :], window_strides=(1,),
                                 padding=[(CONV_WIDTH - 1, 0)],
                                 dimension_numbers=('NWC', 'WIO', 'NWC'),
                                 feature_group_count=D_CONV) + db
    return jax.nn.silu(layer_norm(z, g, b))

def chunk_causal_attention(q, k, v):
    B, S, H, Dk = q.shape
    nq = S // Q_BLOCK
    scale = Dk ** -0.5
    qb = q.reshape(B, nq, Q_BLOCK, H, Dk).transpose(1, 0, 2, 3, 4)
    key_chunk = jnp.arange(S) // CHUNK

    def block(args):
        qi, i = args
        s = jnp.einsum('bqhd,bkhd->bhqk', qi, k, preferred_element_type=jnp.float32) * scale
        q_chunk = (i * Q_BLOCK + jnp.arange(Q_BLOCK)) // CHUNK
        mask = key_chunk[None, :] <= q_chunk[:, None]
        pr = jax.nn.softmax(jnp.where(mask, s, -jnp.inf), axis=-1).astype(v.dtype)
        return jnp.einsum('bhqk,bkhd->bqhd', pr, v)

    o = lax.map(block, (qb, jnp.arange(nq)))
    return o.transpose(1, 0, 2, 3, 4).reshape(B, S, H, v.shape[-1])

def mla(c_q, c_kv, k_r, cos, sin, q_norm_g, w_uq, kv_norm_g, w_ukv):
    B, S, _ = c_q.shape
    q = jnp.matmul(rms_norm(c_q, q_norm_g), w_uq).reshape(B, S, N_HEADS, QK_NOPE + QK_ROPE)
    q_nope, q_rope = q[..., :QK_NOPE], q[..., QK_NOPE:]
    q_rope = apply_rope(q_rope, cos[:, :, None, :], sin[:, :, None, :])
    kv = jnp.matmul(rms_norm(c_kv, kv_norm_g), w_ukv).reshape(B, S, N_HEADS, QK_NOPE + V_HEAD)
    k_nope, v = kv[..., :QK_NOPE], kv[..., QK_NOPE:]
    k_rope = apply_rope(k_r, cos, sin)
    qf = jnp.concatenate([q_nope, q_rope], axis=-1)
    kf = jnp.concatenate([k_nope, jnp.broadcast_to(k_rope[:, :, None, :], (B, S, N_HEADS, QK_ROPE))], axis=-1)
    o = chunk_causal_attention(qf, kf, v)
    return o.reshape(B, S, N_HEADS * V_HEAD)

def mixer_sublayer(h, cos, sin, w_in, b_gate, pool_w, pool_scale, pool_proj, conv_dw, conv_b,
                   conv_ln_g, conv_ln_b, conv_proj, q_norm_g, w_uq, kv_norm_g, w_ukv, mla_proj, w_out):
    B, S, D = h.shape
    proj = jnp.matmul(h, w_in)
    u_pool, u_conv, c_q, c_kv, k_r, g_logits = jnp.split(proj, IN_SPLITS, axis=-1)
    gates = jax.nn.sigmoid(g_logits.reshape(B, S, N_BRANCH, D) + b_gate)
    y_pool = jnp.matmul(pool_mixer(u_pool, pool_w, pool_scale), pool_proj)
    y_conv = jnp.matmul(conv_module(u_conv, conv_dw, conv_b, conv_ln_g, conv_ln_b), conv_proj)
    y_mla = jnp.matmul(mla(c_q, c_kv, k_r, cos, sin, q_norm_g, w_uq, kv_norm_g, w_ukv), mla_proj)
    merged = gates[:, :, 0] * y_pool + gates[:, :, 1] * y_conv + gates[:, :, 2] * y_mla
    return jnp.matmul(merged, w_out)

def moe_ffn(h, w_router, router_bias, w_up, w_down):
    B, S, D = h.shape
    T = B * S
    A = T * TOP_K
    xt = h.reshape(T, D)
    aff = jax.nn.sigmoid(jnp.matmul(xt, w_router).astype(jnp.float32))
    sel = aff + router_bias.astype(jnp.float32)
    grp_score = jnp.sum(lax.top_k(sel.reshape(T, N_GROUPS, EXPERTS_PER_GROUP), TOP_K)[0], axis=-1)
    _, g_idx = lax.top_k(grp_score, TOPK_GROUPS)
    g_keep = jnp.any(jnp.arange(N_GROUPS)[None, None, :] == g_idx[:, :, None], axis=1)
    e_keep = jnp.repeat(g_keep, EXPERTS_PER_GROUP, axis=-1)
    _, e_idx = lax.top_k(jnp.where(e_keep, sel, -jnp.inf), TOP_K)
    w = jnp.take_along_axis(aff, e_idx, axis=-1)
    w = w / jnp.sum(w, axis=-1, keepdims=True)
    n_slots = ((A + N_EXPERTS * MOE_BLOCK + MOE_BLOCK - 1) // MOE_BLOCK) * MOE_BLOCK
    n_blocks = n_slots // MOE_BLOCK
    flat_e = e_idx.reshape(A)
    order = jnp.argsort(flat_e)
    s_e = flat_e[order]
    s_tok = (order // TOP_K).astype(jnp.int32)
    s_w = w.reshape(A)[order]
    counts = jnp.bincount(flat_e, length=N_EXPERTS)
    start = jnp.cumsum(counts) - counts
    padded = (counts + MOE_BLOCK - 1) // MOE_BLOCK * MOE_BLOCK
    pad_end = jnp.cumsum(padded)
    pad_start = pad_end - padded
    dest = pad_start[s_e] + jnp.arange(A) - start[s_e]
    slot_tok = jnp.full((n_slots,), T, jnp.int32).at[dest].set(s_tok)
    slot_w = jnp.zeros((n_slots,), jnp.float32).at[dest].set(s_w)
    blk_e = jnp.minimum(jnp.searchsorted(pad_end, jnp.arange(n_blocks) * MOE_BLOCK, side='right'),
                        N_EXPERTS - 1)
    xs = jnp.concatenate([xt, jnp.zeros((1, D), xt.dtype)], axis=0)[slot_tok]
    xs = xs.reshape(n_blocks, MOE_BLOCK, D)

    def expert_block(args):
        xb, e = args
        gate, up = jnp.split(jnp.matmul(xb, w_up[e]), 2, axis=-1)
        return jnp.matmul(jax.nn.silu(gate) * up, w_down[e])

    ys = lax.map(expert_block, (xs, blk_e)).reshape(n_slots, D)
    out = jnp.zeros((T + 1, D), h.dtype).at[slot_tok].add(ys * slot_w[:, None].astype(ys.dtype))
    return out[:T].reshape(B, S, D)

def first_inputs(seed: int = 0) -> dict:
    key = jax.random.key(seed)
    ks = iter(jax.random.split(key, 40))
    f32 = jnp.float32
    L, D = DEPTH, D_MODEL

    def dense(shape, fan_in, gain=1.0):
        return jax.random.normal(next(ks), shape, f32) * (gain * fan_in ** -0.5)

    def norm_gain(shape):
        return 1.0 + 0.05 * jax.random.normal(next(ks), shape, f32)

    def small(shape, s=0.02):
        return s * jax.random.normal(next(ks), shape, f32)

    x = jax.random.normal(next(ks), (BATCH, SEQ, D), f32)
    p = jax.random.normal(next(ks), (L, BATCH, SEQ, D_PLE), f32)
    offset = jax.random.randint(next(ks), (BATCH, 1), 0, MAX_STREAM_CHUNKS) * CHUNK
    positions = (offset + jnp.arange(SEQ, dtype=jnp.int32)[None, :]).astype(jnp.int32)
    return {
        'x': x,
        'p': p,
        'positions': positions,
        'ln_in_g': norm_gain((D,)),
        'ln_in_b': small((D,)),
        'w_in': dense((L, D, D_IN), D),
        'b_gate': small((L, N_BRANCH, D), 0.1),
        'pool_w': dense((L, POOL_GROUPS, POOL_GW, POOL_GW), POOL_GW),
        'pool_scale': norm_gain((L, D_POOL)),
        'pool_proj': dense((L, D_POOL, D), D_POOL),
        'conv_dw': dense((L, CONV_WIDTH, D_CONV), CONV_WIDTH),
        'conv_b': small((L, D_CONV)),
        'conv_ln_g': norm_gain((L, D_CONV)),
        'conv_ln_b': small((L, D_CONV)),
        'conv_proj': dense((L, D_CONV, D), D_CONV),
        'q_norm_g': norm_gain((L, Q_LORA)),
        'w_uq': dense((L, Q_LORA, N_HEADS * (QK_NOPE + QK_ROPE)), Q_LORA),
        'kv_norm_g': norm_gain((L, KV_LORA)),
        'w_ukv': dense((L, KV_LORA, N_HEADS * (QK_NOPE + V_HEAD)), KV_LORA),
        'mla_proj': dense((L, N_HEADS * V_HEAD, D), N_HEADS * V_HEAD),
        'w_out': dense((L, D, D), D, DEEPNORM_BETA),
        'ln1_g': norm_gain((L, D)),
        'ln1_b': small((L, D)),
        'w_router': dense((D, N_EXPERTS), D),
        'router_bias': small((N_EXPERTS,), 0.01),
        'exp_w_up': dense((L, N_EXPERTS, D, 2 * D_EXPERT), D),
        'exp_w_down': dense((L, N_EXPERTS, D_EXPERT, D), D_EXPERT, DEEPNORM_BETA),
        'ple_proj': dense((L, D_PLE, D), D_PLE, DEEPNORM_BETA),
        'ple_gate': dense((L, D, D), D),
        'ln2_g': norm_gain((L, D)),
        'ln2_b': small((L, D)),
    }

def first_block(x, p, positions, ln_in_g, ln_in_b, w_in, b_gate, pool_w, pool_scale, pool_proj,
              conv_dw, conv_b, conv_ln_g, conv_ln_b, conv_proj, q_norm_g, w_uq, kv_norm_g, w_ukv,
              mla_proj, w_out, ln1_g, ln1_b, w_router, router_bias, exp_w_up, exp_w_down,
              ple_proj, ple_gate, ln2_g, ln2_b):
    cos, sin = rope_tables(positions)
    h = layer_norm(x, ln_in_g, ln_in_b)
    for i in range(DEPTH):
        y = mixer_sublayer(h, cos, sin, w_in[i], b_gate[i], pool_w[i], pool_scale[i], pool_proj[i],
                           conv_dw[i], conv_b[i], conv_ln_g[i], conv_ln_b[i], conv_proj[i],
                           q_norm_g[i], w_uq[i], kv_norm_g[i], w_ukv[i], mla_proj[i], w_out[i])
        h = layer_norm(DEEPNORM_ALPHA * h + y, ln1_g[i], ln1_b[i])
        e = jnp.matmul(p[i], ple_proj[i]) * jax.nn.sigmoid(jnp.matmul(h, ple_gate[i]))
        m = moe_ffn(h, w_router, router_bias, exp_w_up[i], exp_w_down[i])
        h = layer_norm(DEEPNORM_ALPHA * h + m + e, ln2_g[i], ln2_b[i])
    return h


DEPTH_2 = 2

N_EVEN = (DEPTH_2 + 1) // 2
N_ODD = DEPTH_2 // 2
ALPHA = (2 * DEPTH_2) ** 0.25
BETA = (8 * DEPTH_2) ** -0.25

SC_WIDTH = D_MODEL
SC_KERNEL = 3

SSM_INNER = D_MODEL
SSM_HEADDIM = 64
SSM_HEADS = SSM_INNER // SSM_HEADDIM
SSM_GROUPS = 2
SSM_STATE = 128
SSM_CONV = 4
SSM_CHUNK = 128
SSM_XBC = SSM_INNER + 2 * SSM_GROUPS * SSM_STATE
MIX0_IN = 3 * SC_WIDTH + SSM_INNER + SSM_XBC + SSM_HEADS
MIX0_OUT = SC_WIDTH + SSM_INNER

FOX_HEADS = 16
FOX_HEADDIM = D_MODEL // FOX_HEADS
FOX_WIDTH = FOX_HEADS * FOX_HEADDIM
FOX_IN = 3 * FOX_WIDTH + FOX_HEADS
FOX_BLOCK = 128

D_FF = 2816
FFN_KERNEL = 3


def _split(h, sizes):
    idx = np.cumsum(sizes)[:-1].tolist()
    return jnp.split(h, idx, axis=-1)

def causal_dwconv(x, w, b=None):
    k, c = w.shape
    y = lax.conv_general_dilated(x, w[:, None, :].astype(x.dtype), window_strides=(1,), padding=[(k - 1, 0)], dimension_numbers=('NWC', 'WIO', 'NWC'), feature_group_count=c)
    return y if b is None else y + b.astype(y.dtype)

def layer_norm_2(x, g, b):
    xf = x.astype(jnp.float32)
    mu = jnp.mean(xf, -1, keepdims=True)
    var = jnp.mean(jnp.square(xf - mu), -1, keepdims=True)
    return ((xf - mu) * lax.rsqrt(var + LN_EPS) * g + b).astype(x.dtype)

def gated_rmsnorm(y, z, g):
    bsz, l, _ = y.shape
    u = (y.astype(jnp.float32) * jax.nn.silu(z.astype(jnp.float32))).reshape(bsz, l, SSM_GROUPS, -1)
    u = u * lax.rsqrt(jnp.mean(jnp.square(u), -1, keepdims=True) + LN_EPS)
    return (u.reshape(bsz, l, SSM_INNER) * g).astype(y.dtype)

def ssd_chunked(xs, dt, a, bm, cm):
    bsz, l = xs.shape[:2]
    nc, q, r = l // SSM_CHUNK, SSM_CHUNK, SSM_HEADS // SSM_GROUPS
    x = xs.astype(jnp.float32).reshape(bsz, nc, q, SSM_GROUPS, r, SSM_HEADDIM)
    dtc = dt.reshape(bsz, nc, q, SSM_GROUPS, r)
    xdt = x * dtc[..., None]
    bc = bm.astype(jnp.float32).reshape(bsz, nc, q, SSM_GROUPS, SSM_STATE)
    cc = cm.astype(jnp.float32).reshape(bsz, nc, q, SSM_GROUPS, SSM_STATE)
    a_cs = jnp.cumsum((dtc * a.reshape(SSM_GROUPS, r)).transpose(0, 1, 3, 4, 2), axis=-1)
    causal = jnp.tril(jnp.ones((q, q), dtype=bool))
    seg = jnp.exp(jnp.where(causal, a_cs[..., :, None] - a_cs[..., None, :], -jnp.inf))
    cb = jnp.einsum('bctgn,bcsgn->bcgts', cc, bc)
    y_diag = jnp.einsum('bcgts,bcgrts,bcsgrp->bctgrp', cb, seg, xdt)
    decay_to_end = jnp.exp(a_cs[..., -1:] - a_cs)
    chunk_states = jnp.einsum('bcsgn,bcgrs,bcsgrp->bcgrpn', bc, decay_to_end, xdt)
    chunk_decay = jnp.exp(a_cs[..., -1])

    def step(h, inp):
        st, dec = inp
        return h * dec[..., None, None] + st, h

    h0 = jnp.zeros((bsz, SSM_GROUPS, r, SSM_HEADDIM, SSM_STATE), jnp.float32)
    _, prev = lax.scan(step, h0, (jnp.moveaxis(chunk_states, 1, 0), jnp.moveaxis(chunk_decay, 1, 0)))
    prev = jnp.moveaxis(prev, 0, 1)
    y_off = jnp.einsum('bctgn,bcgrpn,bcgrt->bctgrp', cc, prev, jnp.exp(a_cs))
    return (y_diag + y_off).reshape(bsz, l, SSM_HEADS, SSM_HEADDIM)

def sconv_ssd_mixer(x, w_in, sc_conv_w, ssm_conv_w, ssm_conv_b, dt_bias, a_log, d_skip, norm_g, w_out):
    bsz, l, _ = x.shape
    h = x @ w_in
    sc_b, sc_c, sc_h, z, xbc, dt_raw = _split(h, [SC_WIDTH, SC_WIDTH, SC_WIDTH, SSM_INNER, SSM_XBC, SSM_HEADS])
    y_a = sc_b * causal_dwconv(sc_c * sc_h, sc_conv_w)
    xbc = jax.nn.silu(causal_dwconv(xbc, ssm_conv_w, ssm_conv_b))
    xs, bm, cm = _split(xbc, [SSM_INNER, SSM_GROUPS * SSM_STATE, SSM_GROUPS * SSM_STATE])
    xs = xs.reshape(bsz, l, SSM_HEADS, SSM_HEADDIM)
    dt = jax.nn.softplus(dt_raw.astype(jnp.float32) + dt_bias.astype(jnp.float32))
    a = -jnp.exp(a_log.astype(jnp.float32))
    y = ssd_chunked(xs, dt, a, bm.reshape(bsz, l, SSM_GROUPS, SSM_STATE), cm.reshape(bsz, l, SSM_GROUPS, SSM_STATE))
    y = y + d_skip.astype(jnp.float32)[:, None] * xs.astype(jnp.float32)
    y_b = gated_rmsnorm(y.reshape(bsz, l, SSM_INNER).astype(x.dtype), z, norm_g)
    return jnp.concatenate([y_a, y_b], axis=-1) @ w_out

def fox_mixer(x, w_in, b_f, w_out):
    bsz, l, _ = x.shape
    nb = l // FOX_BLOCK
    h = x @ w_in
    q, k, v, f_logit = _split(h, [FOX_WIDTH, FOX_WIDTH, FOX_WIDTH, FOX_HEADS])
    heads = lambda t: t.reshape(bsz, l, FOX_HEADS, FOX_HEADDIM).transpose(0, 2, 1, 3)
    q, k, v = heads(q), heads(k), heads(v)
    log_f = jax.nn.log_sigmoid(f_logit.astype(jnp.float32) + b_f.astype(jnp.float32))
    cum = jnp.cumsum(log_f, axis=1).transpose(0, 2, 1)
    scale = FOX_HEADDIM ** -0.5
    key_pos = jnp.arange(l)

    def block(args):
        q_blk, cum_blk, i = args
        qpos = i * FOX_BLOCK + jnp.arange(FOX_BLOCK)
        s = jnp.einsum('bhqd,bhkd->bhqk', q_blk, k).astype(jnp.float32) * scale + cum_blk[..., None] - cum[:, :, None, :]
        s = jnp.where(key_pos[None, :] <= qpos[:, None], s, -jnp.inf)
        p = jax.nn.softmax(s, axis=-1)
        return jnp.einsum('bhqk,bhkd->bhqd', p.astype(v.dtype), v)

    q_blocks = q.reshape(bsz, FOX_HEADS, nb, FOX_BLOCK, FOX_HEADDIM).transpose(2, 0, 1, 3, 4)
    cum_blocks = cum.reshape(bsz, FOX_HEADS, nb, FOX_BLOCK).transpose(2, 0, 1, 3)
    o = lax.map(block, (q_blocks, cum_blocks, jnp.arange(nb)))
    o = o.transpose(1, 0, 3, 2, 4).reshape(bsz, l, FOX_WIDTH)
    return o @ w_out

def conv_ffn(x, w_up, conv_w, conv_b, w_down):
    h = causal_dwconv(x @ w_up, conv_w, conv_b)
    u, g = _split(h, [D_FF, D_FF])
    return (u * jax.nn.silu(g)) @ w_down

def second_inputs(seed: int = 0) -> dict:
    key = jax.random.key(seed)
    ks = jax.random.split(key, 21)
    f32 = jnp.float32

    def nrm(k, shape, scale):
        return jax.random.normal(k, shape, f32) * scale

    x = nrm(ks[0], (BATCH, SEQ, D_MODEL), 1.0)
    sc_ssm_w_in = nrm(ks[1], (N_EVEN, D_MODEL, MIX0_IN), D_MODEL ** -0.5)
    sc_conv_w = nrm(ks[2], (N_EVEN, SC_KERNEL, SC_WIDTH), SC_KERNEL ** -0.5)
    ssm_conv_w = nrm(ks[3], (N_EVEN, SSM_CONV, SSM_XBC), SSM_CONV ** -0.5)
    ssm_conv_b = nrm(ks[4], (N_EVEN, SSM_XBC), 0.02)
    dt0 = jnp.exp(jax.random.uniform(ks[5], (N_EVEN, SSM_HEADS), f32, minval=math.log(1e-3), maxval=math.log(1e-1)))
    ssm_dt_bias = dt0 + jnp.log(-jnp.expm1(-dt0))
    ssm_a_log = jnp.log(jax.random.uniform(ks[6], (N_EVEN, SSM_HEADS), f32, minval=1.0, maxval=16.0))
    ssm_d = 1.0 + nrm(ks[7], (N_EVEN, SSM_HEADS), 0.1)
    ssm_norm_g = 1.0 + nrm(ks[8], (N_EVEN, SSM_INNER), 0.02)
    sc_ssm_w_out = nrm(ks[9], (N_EVEN, MIX0_OUT, D_MODEL), BETA * MIX0_OUT ** -0.5)
    col_scale = jnp.concatenate([jnp.ones((2 * FOX_WIDTH,), f32), jnp.full((FOX_WIDTH,), BETA, f32), jnp.ones((FOX_HEADS,), f32)])
    fox_w_in = nrm(ks[10], (N_ODD, D_MODEL, FOX_IN), D_MODEL ** -0.5) * col_scale
    fox_b_f = jax.random.uniform(ks[11], (N_ODD, FOX_HEADS), f32, minval=1.0, maxval=4.0)
    fox_w_out = nrm(ks[12], (N_ODD, FOX_WIDTH, D_MODEL), BETA * FOX_WIDTH ** -0.5)
    ffn_w_up = nrm(ks[13], (DEPTH_2, D_MODEL, 2 * D_FF), BETA * D_MODEL ** -0.5)
    ffn_conv_w = nrm(ks[14], (DEPTH_2, FFN_KERNEL, 2 * D_FF), FFN_KERNEL ** -0.5)
    ffn_conv_b = nrm(ks[15], (DEPTH_2, 2 * D_FF), 0.02)
    ffn_w_down = nrm(ks[16], (DEPTH_2, D_FF, D_MODEL), BETA * D_FF ** -0.5)
    ln_mix_g = 1.0 + nrm(ks[17], (DEPTH_2, D_MODEL), 0.02)
    ln_mix_b = nrm(ks[18], (DEPTH_2, D_MODEL), 0.02)
    ln_ffn_g = 1.0 + nrm(ks[19], (DEPTH_2, D_MODEL), 0.02)
    ln_ffn_b = nrm(ks[20], (DEPTH_2, D_MODEL), 0.02)
    return {'x': x, 'sc_ssm_w_in': sc_ssm_w_in, 'sc_conv_w': sc_conv_w, 'ssm_conv_w': ssm_conv_w, 'ssm_conv_b': ssm_conv_b, 'ssm_dt_bias': ssm_dt_bias, 'ssm_a_log': ssm_a_log, 'ssm_d': ssm_d, 'ssm_norm_g': ssm_norm_g, 'sc_ssm_w_out': sc_ssm_w_out, 'fox_w_in': fox_w_in, 'fox_b_f': fox_b_f, 'fox_w_out': fox_w_out, 'ffn_w_up': ffn_w_up, 'ffn_conv_w': ffn_conv_w, 'ffn_conv_b': ffn_conv_b, 'ffn_w_down': ffn_w_down, 'ln_mix_g': ln_mix_g, 'ln_mix_b': ln_mix_b, 'ln_ffn_g': ln_ffn_g, 'ln_ffn_b': ln_ffn_b}

def second_block(x, sc_ssm_w_in, sc_conv_w, ssm_conv_w, ssm_conv_b, ssm_dt_bias, ssm_a_log, ssm_d, ssm_norm_g, sc_ssm_w_out, fox_w_in, fox_b_f, fox_w_out, ffn_w_up, ffn_conv_w, ffn_conv_b, ffn_w_down, ln_mix_g, ln_mix_b, ln_ffn_g, ln_ffn_b):
    for i in range(DEPTH_2):
        j = i // 2
        if i % 2 == 0:
            mix = sconv_ssd_mixer(x, sc_ssm_w_in[j], sc_conv_w[j], ssm_conv_w[j], ssm_conv_b[j], ssm_dt_bias[j], ssm_a_log[j], ssm_d[j], ssm_norm_g[j], sc_ssm_w_out[j])
        else:
            mix = fox_mixer(x, fox_w_in[j], fox_b_f[j], fox_w_out[j])
        x = layer_norm_2(ALPHA * x + mix, ln_mix_g[i], ln_mix_b[i])
        x = layer_norm_2(ALPHA * x + conv_ffn(x, ffn_w_up[i], ffn_conv_w[i], ffn_conv_b[i], ffn_w_down[i]), ln_ffn_g[i], ln_ffn_b[i])
    return x


def setup_inputs(seed=0):
    out = dict(first_inputs(seed))
    for name, value in second_inputs(seed + 1).items():
        if name != "x":
            out[name + "_2"] = value
    return out


def reference(
    x, p, positions, ln_in_g, ln_in_b, w_in, b_gate, pool_w, pool_scale, pool_proj, conv_dw,
    conv_b, conv_ln_g, conv_ln_b, conv_proj, q_norm_g, w_uq, kv_norm_g, w_ukv, mla_proj, w_out,
    ln1_g, ln1_b, w_router, router_bias, exp_w_up, exp_w_down, ple_proj, ple_gate, ln2_g, ln2_b,
    sc_ssm_w_in_2, sc_conv_w_2, ssm_conv_w_2, ssm_conv_b_2, ssm_dt_bias_2, ssm_a_log_2, ssm_d_2,
    ssm_norm_g_2, sc_ssm_w_out_2, fox_w_in_2, fox_b_f_2, fox_w_out_2, ffn_w_up_2, ffn_conv_w_2,
    ffn_conv_b_2, ffn_w_down_2, ln_mix_g_2, ln_mix_b_2, ln_ffn_g_2, ln_ffn_b_2,
):
    x = first_block(
        x, p, positions, ln_in_g, ln_in_b, w_in, b_gate, pool_w, pool_scale, pool_proj, conv_dw,
        conv_b, conv_ln_g, conv_ln_b, conv_proj, q_norm_g, w_uq, kv_norm_g, w_ukv, mla_proj,
        w_out, ln1_g, ln1_b, w_router, router_bias, exp_w_up, exp_w_down, ple_proj, ple_gate,
        ln2_g, ln2_b,
    )
    return second_block(
        x, sc_ssm_w_in_2, sc_conv_w_2, ssm_conv_w_2, ssm_conv_b_2, ssm_dt_bias_2, ssm_a_log_2,
        ssm_d_2, ssm_norm_g_2, sc_ssm_w_out_2, fox_w_in_2, fox_b_f_2, fox_w_out_2, ffn_w_up_2,
        ffn_conv_w_2, ffn_conv_b_2, ffn_w_down_2, ln_mix_g_2, ln_mix_b_2, ln_ffn_g_2,
        ln_ffn_b_2,
    )


_drawn_inputs = setup_inputs


def setup_inputs(seed=0):
    import zlib

    import numpy as np

    out = dict(_drawn_inputs(seed))
    spreads = {}
    factors = {'conv_ln_b': 3.173,
     'q_norm_g': 5.097,
     'kv_norm_g': 4.255,
     'ssm_conv_b_2': 8.0,
     'ssm_d_2': 3.714,
     'ssm_norm_g_2': 8.0,
     'ffn_conv_b_2': 8.0}
    for name, (base, spread) in spreads.items():
        noise = np.random.default_rng([zlib.crc32(name.encode()), seed]).standard_normal(out[name].shape)
        drawn = base * np.exp(spread * noise) if base else spread * noise
        out[name] = jnp.asarray(drawn.astype(out[name].dtype))
    for name, factor in factors.items():
        out[name] = (out[name] * factor).astype(out[name].dtype)
    return out
```

```python
from contextlib import ExitStack

import numpy as np

import concourse.bass as bass
from concourse import mybir

F32 = mybir.dt.float32
I32 = mybir.dt.int32
ALU = mybir.AluOpType
ACT = mybir.ActivationFunctionType
AX = mybir.AxisListType

P = 128
S = 512
D = 1024
C8 = D // P
NT = S // P
NS = 4
SLAB = 8

POOL_W = (2, 4, 8, 16)
TAPS = 31
HEADS1, NOPE, ROPE, VH = 8, 64, 32, 64
QL, KVL = 384, 256
EXPERTS, FE = 16, 512
ALPHA1 = 2.0 ** 0.25
ALPHA2 = 4.0 ** 0.25
SSM_H, SSM_P, SSM_N = 16, 64, 128
FOX_H = 16
FF = 2816
FT = FF // P
NEG = -1e30
TWO_PI = 2.0 * np.pi
MAGIC = 1.5 * 2.0 ** 23

STAGES = [("in", 19, 19), ("uq", 3, 8), ("uk", 1, 4), ("uv", 1, 4), ("att", 0, 4 * HEADS1),
          ("branch", 36, 48), ("wout", 8, 8), ("pg", 8, 8), ("pp", 2, 8), ("moe", 12 * EXPERTS, 16 * EXPERTS),
          ("s_in", 44, 44), ("sout", 16, 8), ("up0", 44, 44), ("down0", 22, 8), ("fqk", 16, 16), ("fv", 8, 8),
          ("fatt", 0, 4 * FOX_H), ("fout", 8, 8), ("up1", 44, 44), ("down1", 22, 8)]
AUX = [("ln_in", 2), ("qrms", 1), ("kvrms", 1), ("poolw", 4), ("att", 4 * HEADS1), ("convln", 2), ("ln1", 2),
       ("route", 1), ("wt", 1), ("ln2", 2), ("dt", 1), ("acst", 1), ("btok", 2), ("xtok", 8), ("cb", 2),
       ("state", 6), ("head", 24), ("grms0", 1), ("grms1", 1), ("lnm0", 2), ("lnf0", 2), ("f", 1),
       ("fatt", 4 * FOX_H), ("lnm1", 2), ("lnf1", 2)]


def starts(rows, k):
    out, at = {}, 0
    for row in rows:
        out[row[0]] = at
        at += row[k]
    return out, at


SLAB0, NSLABS = starts(STAGES, 1)
T0, _ = starts(STAGES, 2)
A0, _ = starts(AUX, 1)

PAR = [("ln_in_g", 8), ("ln_in_b", 8), ("b_gate", 24), ("pool_scale", 4), ("conv_dw", 4 * TAPS), ("conv_b", 4),
       ("conv_ln_g", 4), ("conv_ln_b", 4), ("q_norm_g", 3), ("kv_norm_g", 2), ("ln1_g", 8), ("ln1_b", 8),
       ("ln2_g", 8), ("ln2_b", 8), ("sc_conv", 24), ("ssm_conv", 48), ("ssm_conv_b", 12), ("ssm_d", 8),
       ("ssm_norm_g", 8), ("ffn_conv0", 132), ("ffn_conv1", 132), ("ffn_b0", 44), ("ffn_b1", 44),
       ("lnm0_g", 8), ("lnm0_b", 8), ("lnm1_g", 8), ("lnm1_b", 8), ("lnf0_g", 8), ("lnf0_b", 8),
       ("lnf1_g", 8), ("lnf1_b", 8), ("dt_bias", 1), ("a_log", 1), ("b_f", 1), ("router_bias", 16),
       ("router", 128), ("w_dt", 128), ("w_f", 128), ("pool_w", 512)]
PAR0, NPAR = starts(PAR, 1)
CST = [("ident", 128), ("ones", 128), ("mask_fox", 128), ("mask_mla", 128), ("mask_ssd", 128), ("invcnt", 64),
       ("invfreq", 1), ("sign", 1), ("ln_eps", 1), ("rms_eps", 1), ("zero", 1), ("one", 1), ("halfpi", 1)]
CST0, NCST = starts(CST, 1)

MIX = dict(ZB=0, ZP=6144, UP=8320, PW=10432, CQ=11488, CKV=13024, KT=14048, KR=15072, COS=15584,
           SIN=16096, QH=16608, KH=20704, V=24800, RT=26848, QB=27872, VB=28896, PTS=29408, SG=30688, MG=16608)
MOE = dict(WB=0, ACTV=8192, SG=10240, PG=11264, SEL=15360, WT=16128, PLE=31712)
SSM = dict(ZS=0, XBC=4096, Y=10240, T=18432, BT=18432, XDT=19456, ONE=23568, CB=25616, DT=26640,
           DTV=29712, DTE=30224, ACS=30736, TK=31248)
FFN = dict(G=0, PAD=11264, T=13320)
FOX = dict(QH=0, KH=8192, V=16384, O=20480, PTS=24576, QB=25856, VB=26880, F=27392)
ARENA = 33300


class Count:

    def __init__(self, sem):
        self.sem, self.n, self.i, self.per = sem, 0, None, 0

    def inc(self, ins):
        ins.then_inc(self.sem, 1)
        self.n += 1

    def now(self, back=0):
        return self.n - back if self.i is None else self.i * self.per + (self.n - back)

    def enter(self, i, per):
        self.i, self.per, self.base = i, per, self.n

    def leave(self, rounds):
        assert self.n == self.base + self.per, (self.n - self.base, self.per)
        self.n, self.i = self.base + self.per * rounds, None


def lin(i, per, base):
    return base if i is None else i * per + base


def one(ap):
    return ap.rearrange("p o n -> p (o n)")


def build(nc, w_stream, x, p, positions, par, cst, sel16, w_scratch, out):
    with ExitStack() as ctx:
        def sb(name, cols, dt=F32):
            return ctx.enter_context(nc.sbuf_tensor(name, [P, cols], dt))

        def sem(name):
            return ctx.enter_context(nc.semaphore(name))

        ring = sb("ring", NS * SLAB * P)
        Xt, Rt, SQt = sb("X", C8 * S), sb("R", C8 * S), sb("SQ", C8 * S)
        X, R, SQ = (t[:, :].rearrange("p (c s) -> p c s", s=S) for t in (Xt, Rt, SQt))
        part = sb("part", NPAR)
        cstt = sb("cstt", NCST)
        STD, RSTD = sb("STD", S), sb("RSTD", S)
        stat = sb("stat", 64)
        arena = sb("arena", ARENA)
        bank = [ctx.enter_context(nc.psum_tensor(f"bank{i}", [P, S], F32)) for i in range(8)]

        slab_full = [sem(f"slab_full{i}") for i in range(NS)]
        slab_used = sem("slab_used")
        m_full, a_full = sem("m_full"), sem("a_full")
        m_out = [sem(f"m_out{i}") for i in range(4)]
        a_out = [sem(f"a_out{i}") for i in range(4)]
        loaded, p_loaded, sel_loaded = sem("loaded"), sem("p_loaded"), sem("sel_loaded")
        dve_step, act_step, pool_step = sem("dve_step"), sem("act_step"), sem("pool_step")
        ln_centred, ln_rstd, ln_scaled = sem("ln_centred"), sem("ln_rstd"), sem("ln_scaled")
        ln_squared, ln_std, ln_done = sem("ln_squared"), sem("ln_std"), sem("ln_done")
        conv_in, pads_zero, pool_mixed, rope_q, k_rope, k_rope_in = (
            sem("conv_in"), sem("pads_zero"), sem("pool_mixed"), sem("rope_q"), sem("k_rope"), sem("k_rope_in"))
        att_q, att_v, att_masked, att_max, att_nm, att_rs, att_prob = (
            sem(n) for n in ("att_q", "att_v", "att_masked", "att_max", "att_nm", "att_rs", "att_prob"))
        merged, resid = sem("merged"), sem("resid")
        routed, wt_sent, wb_loaded = sem("routed"), sem("wt_sent"), sem("wb_loaded")
        moe_mul, moe_act = sem("moe_mul"), sem("moe_act")
        sc_y, xbc_conv, xbc_done, dt_e, dt_ln, a_neg, dt_ready = (
            sem(n) for n in ("sc_y", "xbc_conv", "xbc_done", "dt_e", "dt_ln", "a_neg", "dt_ready"))
        ssd_dx, ssd_prev, ssd_l, ssd_e, ssd_m, ssd_d, ssd_u, dte = (
            sem(n) for n in ("ssd_dx", "ssd_prev", "ssd_l", "ssd_e", "ssd_m", "ssd_d", "ssd_u", "dte"))
        ffn_conv, ffn_g, ffn_silu = sem("ffn_conv"), sem("ffn_g"), sem("ffn_silu")
        f_e, f_ln, f_cum, f_rows, f_ones = (sem(n) for n in ("f_e", "f_ln", "f_cum", "f_rows", "f_ones"))
        out_done = sem("out_done")

        def pc(name, j=0, rows=slice(0, P)):
            return part[rows, PAR0[name] + j:PAR0[name] + j + 1]

        def pmat(name, k, w):
            return part[:, PAR0[name] + k * w:PAR0[name] + (k + 1) * w]

        def cm(name, w=P, rows=slice(0, P)):
            return cstt[rows, CST0[name]:CST0[name] + w]

        def ar(at, n, w=S, rows=slice(0, P)):
            return arena[rows, at:at + n * w].rearrange("p (c s) -> p c s", s=w)

        ident, ones = cm("ident"), cm("ones")
        _m, _o, _s, _x, _f = MIX, MOE, SSM, FOX, FFN
        ZB = ar(_m["ZB"], 12)
        ZP = ar(_m["ZP"], 4, 544)
        UP = ar(_m["UP"], 4, 528)
        PW = ar(_m["PW"], 2, 528)
        CQ, CKV, KT = ar(_m["CQ"], 3), ar(_m["CKV"], 2), ar(_m["KT"], 2)
        KR, COS, SIN = (arena[:, _m[n]:_m[n] + S] for n in ("KR", "COS", "SIN"))
        RT, MSG, MG = ar(_m["RT"], 2), ar(_m["SG"], 2), ar(_m["MG"], 8)
        H0 = TAPS - 1
        WB, ACTV, ESG, PG = ar(_o["WB"], 16), ar(_o["ACTV"], 4), ar(_o["SG"], 2), ar(_o["PG"], 8)
        PLE = ar(_o["PLE"], 2)
        SEL, AFF, CMP, RANK, KEEP, GSC, WTOK = (
            arena[:, _o["SEL"] + a:_o["SEL"] + b] for a, b in
            ((0, 128), (128, 256), (256, 512), (512, 576), (576, 640), (640, 656), (656, 720)))
        ZS, XBC, BT, CBS = ar(_s["ZS"], 8), ar(_s["XBC"], 12), ar(_s["BT"], 2), ar(_s["CB"], 2)
        XDT, DX, SEL16 = ar(_s["XDT"], 4, 1024), R[:, 0:6], arena[:, _s["ONE"]:_s["ONE"] + 2048]
        YY = ar(_s["Y"], 16)
        DTB = ar(_s["DT"], 6)
        DT, DTE, ACS, TK = (arena[:, _s[n]:_s[n] + S] for n in ("DTV", "DTE", "ACS", "TK"))
        CS, CHP, CT = ar(_s["T"], 2), ar(_s["T"] + 1024, 2, 514), ar(_s["T"] + 2052, 2)
        XP, XA = ar(_s["T"] + 3076, 2, 515), ar(_s["T"] + 4106, 2)
        EB, LB, MB, CSB = R[:, 0:2], R[:, 2:4], R[:, 4:6], R[:, 6:8]
        G, FP, TF = ar(_f["G"], FT), ar(_f["PAD"], 4, 514), ar(_f["T"], 4)
        FB, F8 = ar(_x["F"], 6), ar(_x["F"] + 3072, 2)

        def head_tile(h):
            return A0["head"] + (h if h < 2 else 3 * (h // 2) - 1 + h % 2)

        def pair_tile(j):
            return A0["head"] + (3 * j + 4 if j < 7 else 23)

        WT = arena[:, _o["WT"]:_o["WT"] + S]
        ATT = {
            "att": dict(n=HEADS1, K=NOPE + ROPE, QH=ar(_m["QH"], 8), KH=ar(_m["KH"], 8), V=ar(_m["V"], 4, 512),
                        O=ZB[:, 4:8], PR=R, PTS=arena[:, _m["PTS"]:_m["PTS"] + 1280],
                        QB=ar(_m["QB"], 2), VB=ar(_m["VB"], 8, 64), scale=float((NOPE + ROPE) ** -0.5),
                        mask=cm("mask_mla"), h0=0),
            "fatt": dict(n=FOX_H, K=66, QH=ar(_x["QH"], 16), KH=ar(_x["KH"], 16), V=ar(_x["V"], 4, 1024),
                         O=ar(_x["O"], 8), PR=R, PTS=arena[:, _x["PTS"]:_x["PTS"] + 1280],
                         QB=ar(_x["QB"], 2), VB=ar(_x["VB"], 8, 64), scale=0.125, mask=cm("mask_fox"), h0=HEADS1),
        }
        NORMS = {}
        total = dict(centred=0, n=0, scaled=0, squared=0)

        def norm(name, c, src, dst, g, b, eps, fn=ACT.Identity):
            NORMS[name] = dict(c=c, src=src, dst=dst, g=g, b=b, eps=eps, fn=fn, ln=b is not None, **total)
            total["centred"] += c if b is not None else 0
            total["n"] += 1
            total["scaled"] += c
            total["squared"] += c

        norm("ln_in", 8, X, X, "ln_in_g", "ln_in_b", "ln_eps")
        norm("qrms", 3, CQ, CQ, "q_norm_g", None, "rms_eps")
        norm("kvrms", 2, CKV, CKV, "kv_norm_g", None, "rms_eps")
        norm("convln", 4, ZB[:, 8:12], ZB[:, 8:12], "conv_ln_g", "conv_ln_b", "ln_eps", ACT.Silu)
        norm("ln1", 8, R, X, "ln1_g", "ln1_b", "ln_eps")
        norm("ln2", 8, R, X, "ln2_g", "ln2_b", "ln_eps")
        norm("grms0", 4, YY[:, 8:12], YY[:, 8:12], "ssm_norm_g", None, "ln_eps")
        norm("grms1", 4, YY[:, 12:16], YY[:, 12:16], "ssm_norm_g", None, "ln_eps")
        norm("lnm0", 8, R, X, "lnm0_g", "lnm0_b", "ln_eps")
        norm("lnf0", 8, R, X, "lnf0_g", "lnf0_b", "ln_eps")
        norm("lnm1", 8, R, X, "lnm1_g", "lnm1_b", "ln_eps")
        norm("lnf1", 8, R, X, "lnf1_g", "lnf1_b", "ln_eps")

        def norm_done(name):
            return NORMS[name]["scaled"] + NORMS[name]["c"]

        block = ctx.enter_context(nc.Block())

        def m_ready(eng, t, i=None, per=0):
            eng.wait_ge(m_full, lin(i, per, t + 1))

        def a_ready(eng, t, i=None, per=0):
            eng.wait_ge(a_full, lin(i, per, t + 1))

        def m_read(eng, t, i=None, per=0):
            eng.wait_ge(m_out[t % 4], lin(i, per // 4, t // 4 + 1))

        def a_read(eng, t, i=None, per=0):
            eng.wait_ge(a_out[t % 4], lin(i, per // 4, t // 4 + 1))

        def mbank(t):
            return bank[t % 4]

        def abank(t):
            return bank[4 + t % 4]

        @block.sync
        def _(sp):
            sp.dma_start(X, x.rearrange("(c p) s -> p c s", p=P)).then_inc(loaded, 16)
            sp.dma_start(part[:, :], par).then_inc(loaded, 16)
            sp.dma_start(cstt[:, :], cst).then_inc(loaded, 16)
            sp.dma_start(KR.bitcast(I32), positions).then_inc(loaded, 16)

            def load(slab, i=None):
                src = w_stream[slab] if i is None else w_stream[bass.ds(i * NS + slab, 1)].rearrange("o p n -> p (o n)")
                sp.dma_start(ring[:, (slab % NS) * SLAB * P:(slab % NS + 1) * SLAB * P], src)\
                    .then_inc(slab_full[slab % NS], 16)

            for slab in range(NS):
                load(slab)
            sp.dma_start(PLE, p.rearrange("(c p) s -> p c s", p=P)).then_inc(p_loaded, 16)
            with sp.Fori(0, NSLABS // NS - 1) as i:
                for slab in range(NS, 2 * NS):
                    sp.wait_ge(slab_used, i * NS + (slab - NS + 1))
                    load(slab, i)
            for slab in range(NSLABS // NS * NS, NSLABS):
                sp.wait_ge(slab_used, slab - NS + 1)
                load(slab)
            for k in range(C8):
                sp.wait_ge(ln_done, norm_done("lnf1") - C8 + k + 1)
                sp.dma_start(out[k * P:(k + 1) * P, :], X[:, k]).then_inc(out_done, 16)
            sp.wait_ge(out_done, 16 * C8)

        @block.tensor
        def _(pe):
            st = dict(n=0, b=0, pending=False)

            def weights(width=1, i=None, per=0):
                if st["b"] == 0:
                    slab = st["n"]
                    pe.wait_ge(slab_full[slab % NS], lin(i, 16 * per // NS, 16 * (slab // NS + 1)))
                    st["pending"] = slab > 0
                at = ((st["n"] % NS) * SLAB + st["b"]) * P
                st["b"] += width
                if st["b"] == SLAB:
                    st["b"], st["n"] = 0, st["n"] + 1
                return ring[:, at:at + width * P]

            def signal(ins, final=None):
                if final is not None:
                    ins.then_inc(final, 1)
                elif st["pending"]:
                    ins.then_inc(slab_used, 1)
                    st["pending"] = False

            def tile(t, rhs, i=None, per_t=0, per_s=0):
                if t >= 4:
                    m_read(pe, t - 4, i, per_t)
                for k, r in enumerate(rhs):
                    w = weights(1, i, per_s)
                    mm = pe.matmul(mbank(t)[:, :], w, r, start=(k == 0), stop=(k == len(rhs) - 1))
                    signal(mm, m_full if k == len(rhs) - 1 else None)

            def loop(rounds, tiles, slabs, body):
                n0 = st["n"]
                with pe.Fori(0, rounds) as i:
                    body(i)
                assert st["n"] == n0 + slabs and st["b"] == 0
                st["n"] = n0 + slabs * rounds

            def stats(name, waits=()):
                n = NORMS[name]
                t = A0[name]
                for s, v in waits:
                    pe.wait_ge(s, v)
                if n["ln"]:
                    if t >= 4:
                        a_read(pe, t - 4)
                    for k in range(n["c"]):
                        mm = pe.matmul(abank(t)[:, :], ones, n["src"][:, k], start=(k == 0), stop=(k == n["c"] - 1))
                    mm.then_inc(a_full, 1)
                    t += 1
                if t >= 4:
                    a_read(pe, t - 4)
                for k in range(n["c"]):
                    pe.wait_ge(ln_squared, n["squared"] + k + 1)
                    mm = pe.matmul(abank(t)[:, :], ones, SQ[:, k], start=(k == 0), stop=(k == n["c"] - 1))
                mm.then_inc(a_full, 1)

            def attention(name):
                a = ATT[name]
                K = a["K"]

                def scores(h, i=None):
                    per = 4 * 2
                    pe.wait_ge(att_q, lin(i, 2, a["h0"] + h + 1))
                    for q in range(NT):
                        t = T0[name] + 4 * h + q
                        m_read(pe, t - 4, i, per)
                        k = a["KH"][0:K, h, 0:(q + 1) * P] if i is None else \
                            one(a["KH"][0:K, bass.ds(i * 2 + h, 1), 0:(q + 1) * P])
                        pe.matmul(mbank(t)[:, 0:(q + 1) * P], a["QB"][0:K, h % 2, q * P:(q + 1) * P], k,
                                  start=True, stop=True).then_inc(m_full, 1)

                def values(h, i=None):
                    per = 4 * 2
                    pe.wait_ge(att_prob, lin(i, 8, 4 * (a["h0"] + h + 1)))
                    t = A0[name] + 4 * h
                    for n, blocks in enumerate((((0, 0), (1, 0), (2, 0), (3, 0)), ((1, 1), (2, 1), (3, 1)),
                                                ((2, 2), (3, 2), (3, 3)))):
                        a_read(pe, t + n - 4, i, per)
                        for m, (q, k) in enumerate(blocks):
                            tr = pe.transpose(abank(t + n)[:, m * P:(m + 1) * P],
                                              a["PR"][:, 4 * (h % 2) + q, k * P:(k + 1) * P], ident)
                        tr.then_inc(a_full, 1)
                    a_read(pe, t - 1, i, per)
                    pe.wait_ge(att_v, lin(i, 2, a["h0"] + h + 1))
                    for k, at in enumerate((0, 512, 896, 1152)):
                        if k < 3:
                            a_read(pe, t + k, i, per)
                        mm = pe.matmul(abank(t + 3)[0:64, k * P:S], a["VB"][:, 4 * (h % 2) + k, :],
                                       a["PTS"][:, at:at + (NT - k) * P], start=(k == 0), stop=(k == NT - 1))
                    mm.then_inc(a_full, 1)

                scores(0)
                with pe.Fori(0, a["n"] // 2 - 1) as i:
                    scores(1, i)
                    values(0, i)
                    scores(2, i)
                    values(1, i)
                scores(a["n"] - 1)
                values(a["n"] - 2)
                values(a["n"] - 1)

            Xr = [X[:, k] for k in range(C8)]
            pe.wait_ge(loaded, 64)
            stats("ln_in")
            for n in range(19):
                if n == 0:
                    pe.wait_ge(ln_done, norm_done("ln_in"))
                tile(T0["in"] + n, Xr)
            stats("qrms")
            for n in range(8):
                if n == 0:
                    pe.wait_ge(ln_done, norm_done("qrms"))
                tile(T0["uq"] + n, [CQ[:, k] for k in range(3)])
            stats("kvrms")
            pe.wait_ge(ln_done, norm_done("kvrms"))
            for n in range(4):
                tile(T0["uk"] + n, [CKV[:, k] for k in range(2)])
            for t in range(4):
                m_read(pe, T0["uv"] + t - 4)
            for k in range(2):
                w = weights(4)
                for t in range(NT):
                    mm = pe.matmul(mbank(T0["uv"] + t)[:, :], CKV[:, k, t * P:(t + 1) * P], w,
                                   start=(k == 0), stop=(k == 1))
                    signal(mm, m_full if k == 1 else None)
            for g in range(4):
                t = A0["poolw"] + g
                pe.wait_ge(pool_mixed, g + 1)
                a_read(pe, t - 4)
                pe.matmul(abank(t)[:, :], pmat("pool_w", g, P), UP[:, g, 16:16 + S], start=True, stop=True)\
                    .then_inc(a_full, 1)
            pe.wait_ge(k_rope, HEADS1)
            for j in range(4):
                m_read(pe, T0["uv"] + j)
            attention("att")
            def branch(i, b):
                for m in range(C8):
                    t = T0["branch"] + (16 * b if i is None else 0) + 2 * m
                    tile(t, Xr, i, 16, 12)
                    z = [one(ZB[:, bass.ds(i * 4 + k, 1), :]) if i is not None else ZB[:, 4 * b + k] for k in range(4)]
                    tile(t + 1, z, i, 16, 12)

            for t in range(A0["att"] + 4 * HEADS1 - 4, A0["att"] + 4 * HEADS1):
                a_read(pe, t)
            loop(2, 32, 12, lambda i: branch(i, 0))
            stats("convln", [(merged, 1)])
            pe.wait_ge(ln_done, norm_done("convln"))
            branch(None, 2)
            pe.wait_ge(merged, 2)
            for m in range(C8):
                tile(T0["wout"] + m, [MG[:, k] for k in range(C8)])
            stats("ln1", [(resid, 1)])
            pe.wait_ge(ln_done, norm_done("ln1"))
            for m in range(C8):
                tile(T0["pg"] + m, Xr)
            pe.wait_ge(p_loaded, 16)
            for m in range(C8):
                tile(T0["pp"] + m, [PLE[:, k] for k in range(2)])
            t = A0["route"]
            a_read(pe, t - 4)
            for q in range(NT):
                for k in range(C8):
                    mm = pe.matmul(abank(t)[:, 16 * q:16 * q + 16], X[:, k, q * P:(q + 1) * P],
                                   pmat("router", k, 16), start=(k == 0), stop=(k == C8 - 1))
            mm.then_inc(a_full, 1)
            t = A0["wt"]
            pe.wait_ge(routed, 1)
            a_read(pe, t - 4)
            for q in range(NT):
                mm = pe.transpose(abank(t)[0:16, q * P:(q + 1) * P], WTOK[:, 16 * q:16 * q + 16], ident)
            mm.then_inc(a_full, 1)

            def expert(i):
                for n in range(8):
                    tile(T0["moe"] + n, Xr, i, 16, 12)
                for m in range(C8):
                    if m == 0:
                        pe.wait_ge(moe_act, i * 4 + 4)
                    tile(T0["moe"] + 8 + m, [ACTV[:, k] for k in range(4)], i, 16, 12)

            loop(EXPERTS, 16, 12, expert)
            stats("ln2", [(resid, 2)])
            pe.wait_ge(ln_done, norm_done("ln2"))
            t = A0["dt"]
            a_read(pe, t - 4)
            for k in range(C8):
                mm = pe.matmul(abank(t)[0:16, :], pmat("w_dt", k, 16), X[:, k], start=(k == 0), stop=(k == C8 - 1))
            mm.then_inc(a_full, 1)

            def four(base, n):
                def body(i):
                    for j in range(4):
                        tile(base + j, Xr, i, 4, 4)
                loop(n // 4, 4, 4, body)

            def twelve(i):
                for j in range(12):
                    tile(T0["s_in"] + j, Xr, i, 12, 12)
            loop(2, 12, 12, twelve)
            four(T0["s_in"] + 24, 8)
            four(T0["s_in"] + 32, 12)
            t = A0["acst"]
            pe.wait_ge(dt_ready, 1)
            a_read(pe, t - 4)
            for n, src in enumerate((ACS, DT, DTE)):
                for c in range(NT):
                    tr = pe.transpose(abank(t)[:, 64 * n + 16 * c:64 * n + 16 * c + 16],
                                      src[0:16, c * P:(c + 1) * P], ident[0:16, 0:16])
            tr.then_inc(a_full, 1)
            pe.wait_ge(xbc_done, 12)
            for g in range(2):
                t = A0["btok"] + g
                a_read(pe, t - 4)
                for c in range(NT):
                    tr = pe.transpose(abank(t)[:, c * P:(c + 1) * P], XBC[:, 8 + g, c * P:(c + 1) * P], ident)
                tr.then_inc(a_full, 1)
            for c in range(NT):
                for g in range(2):
                    t = A0["xtok"] + 2 * c + g
                    a_read(pe, t - 4)
                    for j in range(4):
                        tr = pe.transpose(abank(t)[:, j * P:(j + 1) * P], XBC[:, 4 * g + j, c * P:(c + 1) * P], ident)
                    tr.then_inc(a_full, 1)
            for g in range(2):
                t = A0["cb"] + g
                a_read(pe, t - 4)
                for c in range(NT):
                    cs = slice(c * P, (c + 1) * P)
                    mm = pe.matmul(abank(t)[:, cs], XBC[:, 8 + g, cs], XBC[:, 10 + g, cs], start=True, stop=True)
                mm.then_inc(a_full, 1)
            a_read(pe, A0["btok"])
            a_read(pe, A0["btok"] + 1)
            for c in range(NT - 1):
                for g in range(2):
                    t = A0["state"] + 2 * c + g
                    pe.wait_ge(ssd_dx, 2 * c + g + 1)
                    a_read(pe, t - 4)
                    pe.matmul(abank(t)[:, :], BT[:, g, c * P:(c + 1) * P], DX[:, 2 * c + g],
                              start=True, stop=True).then_inc(a_full, 1)

            def decays(h):
                t = head_tile(h)
                a_read(pe, t - 4)
                pe.matmul(abank(t)[:, :], SEL16[0:16, h * P:(h + 1) * P], ACS[0:16, :], start=True, stop=True)\
                    .then_inc(a_full, 1)

            pe.wait_ge(sel_loaded, 16)
            decays(0)
            decays(1)
            for c in range(NT):
                for g in range(2):
                    a_read(pe, A0["xtok"] + 2 * c + g)
            for j in range(C8):
                if j < C8 - 1:
                    decays(2 * j + 2)
                    decays(2 * j + 3)
                t = pair_tile(j)
                a_read(pe, t - 4)
                pe.wait_ge(ssd_m, 2 * j + 2)
                pe.wait_ge(ssd_e, 2 * j + 2)
                pe.wait_ge(ssd_prev, 4 * j + 4)
                for h in (2 * j, 2 * j + 1):
                    r = slice(64 * (h % 2), 64 * (h % 2) + 64)
                    f = slice((h % 8) * 64, (h % 8) * 64 + 64)
                    for c in range(NT):
                        cs = slice(c * P, (c + 1) * P)
                        mm = pe.matmul(abank(t)[r, cs], XDT[:, c, h * 64:h * 64 + 64], MB[:, h % 2, cs],
                                       start=True, stop=(c == 0))
                        if c:
                            mm = pe.matmul(abank(t)[r, cs], SQ[:, 2 * (c - 1) + h // 8, f], CSB[:, h % 2, cs],
                                           start=False, stop=True)
                mm.then_inc(a_full, 1)
            stats("grms0")
            stats("grms1")
            for t in range(T0["sout"] - 4, T0["sout"]):
                m_read(pe, t)
            pe.wait_ge(ln_done, norm_done("grms1"))
            for m in range(C8):
                tile(T0["sout"] + m, [YY[:, k] for k in range(16)])
            stats("lnm0", [(resid, 3)])

            def ffn(layer, first, last, resid_n):
                pe.wait_ge(ln_done, norm_done(first))
                four(T0[f"up{layer}"], 2 * FT)
                pe.wait_ge(ffn_g, FT * (layer + 1))
                for m in range(C8):
                    tile(T0[f"down{layer}"] + m, [G[:, k] for k in range(FT)])
                stats(last, [(resid, resid_n)])

            ffn(0, "lnm0", "lnf0", 4)
            pe.wait_ge(ln_done, norm_done("lnf0"))
            t = A0["f"]
            a_read(pe, t - 4)
            for k in range(C8):
                mm = pe.matmul(abank(t)[0:16, :], pmat("w_f", k, 16), X[:, k], start=(k == 0), stop=(k == C8 - 1))
            mm.then_inc(a_full, 1)
            four(T0["fqk"], 16)
            for half in range(2):
                for q in range(NT):
                    m_read(pe, T0["fv"] + 4 * half + q - 4)
                for k in range(C8):
                    w = weights(4)
                    for q in range(NT):
                        mm = pe.matmul(mbank(T0["fv"] + 4 * half + q)[:, :], X[:, k, q * P:(q + 1) * P], w,
                                       start=(k == 0), stop=(k == C8 - 1))
                        signal(mm, m_full if k == C8 - 1 else None)
            pe.wait_ge(f_rows, 32)
            for q in range(NT):
                m_read(pe, T0["fv"] + 4 + q)
            attention("fatt")
            for t in range(A0["fatt"] + 4 * FOX_H - 4, A0["fatt"] + 4 * FOX_H):
                a_read(pe, t)
            for m in range(C8):
                tile(T0["fout"] + m, [ATT["fatt"]["O"][:, k] for k in range(C8)])
            stats("lnm1", [(resid, 5)])
            ffn(1, "lnm1", "lnf1", 6)

        @block.scalar
        def _(act):
            step = Count(act_step)

            def norm_act(name, waits=()):
                n = NORMS[name]
                t = A0[name] + n["ln"]
                for s, v in waits:
                    act.wait_ge(s, v)
                for k in range(n["c"]):
                    if n["ln"]:
                        act.wait_ge(ln_centred, n["centred"] + k + 1)
                    act.activation(SQ[:, k], n["src"][:, k], ACT.Square).then_inc(ln_squared, 1)
                a_ready(act, t)
                act.activation(STD[:, :], abank(t)[:, :], ACT.Sqrt, bias=cm(n["eps"], 1),
                               scale=1.0 / (n["c"] * P)).then_inc(a_out[t % 4], 1)
                for k in range(n["c"]):
                    act.wait_ge(ln_scaled, n["scaled"] + k + 1)
                    b = pc(n["b"], k) if n["ln"] else cm("zero", 1)
                    gk = k + (4 if name == "grms1" else 0)
                    act.activation(n["dst"][:, k], n["src"][:, k], n["fn"], bias=b, scale=pc(n["g"], gk))\
                        .then_inc(ln_done, 1)

            def attention(name):
                a = ATT[name]

                def exps(h, i=None):
                    act.wait_ge(att_nm, lin(i, 2, a["h0"] + h + 1))
                    if h >= 2:
                        a_ready(act, A0[name] + 4 * (h - 2) + 2, i, 8)
                    elif i is not None:
                        act.wait_ge(a_full, i * 8 + (A0[name] + 4 * (h - 2) + 3))
                    for q in range(NT):
                        t = T0[name] + 4 * h + q
                        c = 8 * (h % 2) + q
                        act.activation(a["PR"][:, 4 * (h % 2) + q, 0:(q + 1) * P], mbank(t)[:, 0:(q + 1) * P], ACT.Exp,
                                       bias=stat[:, c:c + 1], scale=a["scale"],
                                       accum_out=stat[:, c + 4:c + 5]).then_inc(m_out[t % 4], 1)

                def evacuate(h, i=None):
                    t = A0[name] + 4 * h
                    a_ready(act, t, i, 8)
                    act.activation(a["PTS"][:, 0:S], abank(t)[:, :], ACT.Copy).then_inc(a_out[t % 4], 1)
                    a_ready(act, t + 3, i, 8)
                    r = slice(64 * (h % 2), 64 * (h % 2) + 64)
                    o = a["O"][r, h // 2] if i is None else one(a["O"][r, bass.ds(i + h // 2, 1), :])
                    act.activation(o, abank(t + 3)[0:64, :], ACT.Copy).then_inc(a_out[(t + 3) % 4], 1)

                exps(0)
                with act.Fori(0, a["n"] // 2 - 1) as i:
                    exps(1, i)
                    evacuate(0, i)
                    exps(2, i)
                    evacuate(1, i)
                exps(a["n"] - 1)
                evacuate(a["n"] - 2)
                evacuate(a["n"] - 1)

            act.wait_ge(loaded, 64)
            norm_act("ln_in")
            act.wait_ge(rope_q, 1)
            act.activation(SIN, RT[:, 0], ACT.Sin, bias=cm("zero", 1)).then_inc(act_step, 1)
            act.activation(COS, RT[:, 1], ACT.Sin, bias=cm("zero", 1)).then_inc(act_step, 1)
            step.n = 2
            for k in range(4):
                t = T0["in"] + 2 * k + 1
                if k >= 2:
                    act.wait_ge(conv_in, k - 1)
                m_ready(act, t)
                act.activation(MSG[:, k % 2], mbank(t)[:, :], ACT.Sigmoid).then_inc(m_out[t % 4], 1)
            for k in range(3):
                t = T0["in"] + 8 + k
                m_ready(act, t)
                act.activation(CQ[:, k], mbank(t)[:, :], ACT.Copy).then_inc(m_out[t % 4], 1)
            for k in range(2):
                t = T0["in"] + 11 + k
                m_ready(act, t)
                act.activation(CKV[:, k], mbank(t)[:, :], ACT.Copy).then_inc(m_out[t % 4], 1)
            act.wait_ge(pads_zero, 2)
            for g in range(4):
                t = T0["in"] + 15 + g
                m_ready(act, t)
                act.activation(UP[:, g, 16:16 + S], mbank(t)[:, :], ACT.Copy).then_inc(m_out[t % 4], 1)
            m_read(act, T0["in"] + 8)
            m_read(act, T0["in"] + 9)
            m_read(act, T0["in"] + 10)
            norm_act("qrms")

            def split_heads(dst, t, j):
                m_ready(act, t)
                act.activation(dst[0:64, 2 * j], mbank(t)[0:64, :], ACT.Copy).then_inc(act_step, 1)
                act.activation(dst[0:64, 2 * j + 1], mbank(t)[64:128, :], ACT.Copy).then_inc(m_out[t % 4], 1)

            for j in range(4):
                split_heads(ATT["att"]["QH"], T0["uq"] + j, j)
            m_read(act, T0["in"] + 11)
            m_read(act, T0["in"] + 12)
            norm_act("kvrms")
            for j in range(4):
                split_heads(ATT["att"]["KH"], T0["uk"] + j, j)
            for k in range(4):
                t = T0["uv"] + k
                m_ready(act, t)
                act.activation(ATT["att"]["V"][:, k], mbank(t)[:, :], ACT.Copy).then_inc(m_out[t % 4], 1)
            for g in range(4):
                t = A0["poolw"] + g
                a_ready(act, t)
                act.activation(ZB[:, g], abank(t)[:, :], ACT.Identity, bias=cm("zero", 1),
                               scale=pc("pool_scale", g)).then_inc(a_out[t % 4], 1)
            attention("att")

            def branch(i, b):
                for m in range(C8):
                    t = T0["branch"] + (16 * b if i is None else 0) + 2 * m
                    m_read(act, t + 1 - 4, i, 16)
                    m_ready(act, t, i, 16)
                    bias = pc("b_gate", 8 * b + m) if i is None else \
                        part[:, bass.ds(i * 8 + (PAR0["b_gate"] + m), 1)]
                    act.activation(MSG[:, m % 2], mbank(t)[:, :], ACT.Sigmoid, bias=bias).then_inc(m_out[t % 4], 1)

            with act.Fori(0, 2) as i:
                branch(i, 0)
            norm_act("convln")
            branch(None, 2)
            norm_act("ln1")
            for m in range(C8):
                t = T0["pg"] + m
                m_ready(act, t)
                act.activation(PG[:, m], mbank(t)[:, :], ACT.Sigmoid).then_inc(m_out[t % 4], 1)
            t = A0["route"]
            a_ready(act, t)
            act.activation(AFF[:, 0:64], abank(t)[:, 0:64], ACT.Sigmoid).then_inc(a_out[t % 4], 1)
            t = A0["wt"]
            a_ready(act, t)
            act.activation(WT[0:16, :], abank(t)[0:16, :], ACT.Copy).then_inc(a_out[t % 4], 1)
            a_read(act, t)
            act.dma_start(w_scratch, WT[0:16, :]).then_inc(wt_sent, 16)
            act.wait_ge(wt_sent, 16)
            act.dma_start(WB, w_scratch.rearrange("(o e) s -> o e s", o=1).to_broadcast([P, EXPERTS, S]))\
                .then_inc(wb_loaded, 16)

            with act.Fori(0, EXPERTS) as i:
                for j in range(4):
                    t = T0["moe"] + 2 * j
                    m_read(act, t + 1 - 4 if j >= 2 else t + 1 - 12, i, 16)
                    m_ready(act, t, i, 16)
                    act.activation(ESG[:, j % 2], mbank(t)[:, :], ACT.Silu).then_inc(m_out[t % 4], 1)
            norm_act("ln2")
            def log1p_act(b, src_tile, bias):
                t = A0[src_tile]
                a_ready(act, t)
                act.activation(b[0:16, 0], abank(t)[0:16, :], ACT.Identity, bias=pc(bias, 0, slice(0, 16)))\
                    .then_inc(a_out[t % 4], 1)
                n = 1 if src_tile == "f" else 0
                act.wait_ge(dt_ln, 2 * n + 1)
                act.activation(b[0:16, 2], b[0:16, 1], ACT.Exp, scale=-1.0).then_inc(dt_e, 1)
                act.wait_ge(dt_ln, 2 * n + 2)
                act.activation(b[0:16, 4], b[0:16, 3], ACT.Ln).then_inc(dt_e, 1)

            act.activation(stat[0:16, 50:51], pc("a_log", 0, slice(0, 16)), ACT.Exp).then_inc(a_neg, 1)
            log1p_act(DTB, "dt", "dt_bias")
            act.wait_ge(dte, 1)
            for c in range(NT):
                last = ACS[0:16, (c + 1) * P - 1:(c + 1) * P]
                ins = act.activation(DTE[0:16, c * P:(c + 1) * P], ACS[0:16, c * P:(c + 1) * P], ACT.Exp,
                                     bias=last, scale=-1.0)
            ins.then_inc(a_neg, 1)
            with act.Fori(0, 2) as i:
                for m in range(4):
                    t = T0["s_in"] + 3 * m
                    m_read(act, t - 5, i, 12)
                    m_ready(act, t, i, 12)
                    act.activation(CS[:, m % 2], mbank(t)[:, :], ACT.Copy).then_inc(m_out[t % 4], 1)
            with act.Fori(0, 2) as i:
                for m in range(4):
                    t = T0["s_in"] + 24 + m
                    m_ready(act, t, i, 4)
                    act.activation(one(ZS[:, bass.ds(i * 4 + m, 1), :]), mbank(t)[:, :], ACT.Silu)\
                        .then_inc(m_out[t % 4], 1)
            with act.Fori(0, 3) as i:
                for m in range(4):
                    t = T0["s_in"] + 32 + m
                    m_ready(act, t, i, 4)
                    act.wait_ge(xbc_conv, i * 4 + (m + 1))
                    act.activation(XP[:, m % 2, 3:3 + S], mbank(t)[:, :], ACT.Copy).then_inc(m_out[t % 4], 1)
                    act.wait_ge(xbc_conv, i * 4 + (m + 3))
                    act.activation(one(XBC[:, bass.ds(i * 4 + m, 1), :]), XA[:, m % 2], ACT.Silu,
                                   bias=part[:, bass.ds(i * 4 + (PAR0["ssm_conv_b"] + m), 1)]).then_inc(xbc_done, 1)
            t = A0["acst"]
            a_ready(act, t)
            act.activation(TK[:, 0:192], abank(t)[:, 0:192], ACT.Copy).then_inc(a_out[t % 4], 1)
            for g in range(2):
                t = A0["btok"] + g
                a_ready(act, t)
                act.activation(BT[:, g], abank(t)[:, :], ACT.Copy).then_inc(a_out[t % 4], 1)
            for g in range(2):
                t = A0["cb"] + g
                a_ready(act, t)
                act.activation(CBS[:, g], abank(t)[:, :], ACT.Copy).then_inc(a_out[t % 4], 1)
            for n in range(6):
                t = A0["state"] + n
                a_ready(act, t)
                act.activation(SQ[:, n], abank(t)[:, :], ACT.Copy).then_inc(a_out[t % 4], 1)
            for h in range(SSM_H):
                t = head_tile(h)
                if h >= 2:
                    act.wait_ge(ssd_e, h - 1)
                    act.wait_ge(ssd_prev, 2 * (h - 2) + 2)
                a_ready(act, t)
                act.activation(EB[:, h % 2], abank(t)[:, :], ACT.Exp).then_inc(ssd_u, 1)
                act.wait_ge(ssd_d, 4 * h + 4)
                act.activation(LB[:, h % 2], LB[:, h % 2], ACT.Exp).then_inc(ssd_l, 1)
            norm_act("grms0", [(sc_y, 8)])
            norm_act("grms1")
            norm_act("lnm0")

            def ffn(layer, last):
                with act.Fori(0, FT // 2) as i:
                    for k in range(4):
                        t = T0[f"up{layer}"] + k
                        m_ready(act, t, i, 4)
                        act.wait_ge(ffn_conv, i * 4 + (48 * layer + k + 1))
                        act.activation(FP[:, k, 2:2 + S], mbank(t)[:, :], ACT.Copy).then_inc(m_out[t % 4], 1)
                        if k % 2:
                            act.wait_ge(ffn_conv, i * 4 + (48 * layer + k + 5))
                            act.activation(TF[:, k], TF[:, k], ACT.Silu).then_inc(ffn_silu, 1)
                norm_act(last)

            ffn(0, "lnf0")
            log1p_act(FB, "f", "b_f")
            QK = ar(_x["QH"], 32)
            with act.Fori(0, 4) as i:
                for j in range(4):
                    t = T0["fqk"] + j
                    m_ready(act, t, i, 4)
                    for h in range(2):
                        ins = act.activation(one(QK[0:64, bass.ds(i * 8 + (2 * j + h), 1), :]),
                                             mbank(t)[64 * h:64 * h + 64, :], ACT.Copy)
                    ins.then_inc(m_out[t % 4], 1)
            for half in range(2):
                for q in range(NT):
                    t = T0["fv"] + 4 * half + q
                    m_ready(act, t)
                    act.activation(ATT["fatt"]["V"][:, q, half * S:half * S + S], mbank(t)[:, :], ACT.Copy)\
                        .then_inc(m_out[t % 4], 1)
            attention("fatt")
            norm_act("lnm1")
            ffn(1, "lnf1")

        @block.vector
        def _(dve):
            step = Count(dve_step)

            def sync():
                dve.wait_ge(dve_step, step.now())

            def norm_dve(name):
                n = NORMS[name]
                t = A0[name]
                if n["ln"]:
                    a_ready(dve, t)
                    for k in range(n["c"]):
                        ins = dve.scalar_tensor_tensor(out=n["src"][:, k], in0=abank(t)[:, :],
                                                       scalar=-1.0 / (n["c"] * P), in1=n["src"][:, k],
                                                       op0=ALU.mult, op1=ALU.add)
                        ins.then_inc(ln_centred, 1)
                    dve.wait_ge(ln_centred, n["centred"] + n["c"])
                    dve.engine_nop().then_inc(a_out[t % 4], 1)
                    t += 1
                a_read(dve, t)
                dve.reciprocal(RSTD[:, :], STD[:, :]).then_inc(ln_rstd, 1)
                dve.wait_ge(ln_rstd, n["n"] + 1)
                for k in range(n["c"]):
                    if not n["ln"]:
                        dve.wait_ge(ln_squared, n["squared"] + k + 1)
                    dve.tensor_tensor(n["src"][:, k], n["src"][:, k], RSTD[:, :], ALU.mult).then_inc(ln_scaled, 1)

            def attention(name, h_nm):
                a = ATT[name]

                def maxima(h, i=None):
                    for q in range(NT):
                        t = T0[name] + 4 * h + q
                        m_ready(dve, t, i, 8)
                        dve.tensor_tensor(mbank(t)[:, q * P:(q + 1) * P], mbank(t)[:, q * P:(q + 1) * P],
                                          a["mask"], ALU.add).then_inc(att_masked, 1)
                    for q in range(NT):
                        t = T0[name] + 4 * h + q
                        c = 8 * (h % 2) + q
                        dve.wait_ge(att_masked, lin(i, 8, 4 * (a["h0"] + h) + q + 1))
                        dve.tensor_reduce(stat[:, 16 + c:17 + c], mbank(t)[:, 0:(q + 1) * P], AX.X, ALU.max,
                                          negate=True).then_inc(att_max, 1)
                    c = 8 * (h % 2)
                    dve.wait_ge(att_max, lin(i, 8, 4 * (a["h0"] + h + 1)))
                    dve.tensor_scalar(stat[:, c:c + 4], stat[:, 16 + c:20 + c], a["scale"], None, ALU.mult)\
                        .then_inc(att_nm, 1)

                def probabilities(h, i=None):
                    c = 8 * (h % 2) + 4
                    for q in range(NT):
                        m_read(dve, T0[name] + 4 * h + q, i, 8)
                    dve.reciprocal(stat[:, 28 + c:32 + c], stat[:, c:c + 4]).then_inc(att_rs, 1)
                    dve.wait_ge(att_rs, lin(i, 2, a["h0"] + h + 1))
                    for q in range(NT):
                        pr = a["PR"][:, 4 * (h % 2) + q, 0:(q + 1) * P]
                        dve.tensor_scalar(pr, pr, stat[:, 28 + c + q:29 + c + q], None, ALU.mult).then_inc(att_prob, 1)
                    t = A0[name] + 4 * h
                    for n, (at, w) in ((1, (512, 384)), (2, (896, 384))):
                        a_ready(dve, t + n, i, 8)
                        dve.tensor_copy(a["PTS"][:, at:at + w], abank(t + n)[:, 0:w]).then_inc(a_out[(t + n) % 4], 1)

                maxima(0)
                with dve.Fori(0, a["n"] // 2 - 1) as i:
                    maxima(1, i)
                    probabilities(0, i)
                    maxima(2, i)
                    probabilities(1, i)
                maxima(a["n"] - 1)
                probabilities(a["n"] - 2)
                probabilities(a["n"] - 1)

            def res_tiles(stage, alpha, n_done):
                for m in range(C8):
                    t = T0[stage] + m
                    m_ready(dve, t)
                    dve.scalar_tensor_tensor(out=R[:, m], in0=X[:, m], scalar=alpha, in1=mbank(t)[:, :],
                                             op0=ALU.mult, op1=ALU.add).then_inc(m_out[t % 4], 1)
                for t in range(T0[stage] + 4, T0[stage] + 8):
                    m_read(dve, t)
                dve.engine_nop().then_inc(resid, 1)

            dve.wait_ge(loaded, 64)
            norm_dve("ln_in")
            A, B = KT[:, 0], KT[:, 1]
            step.inc(dve.tensor_copy(A, KR.bitcast(I32)))
            sync()
            step.inc(dve.tensor_scalar(A, A, cm("invfreq", 1), None, ALU.mult))
            sync()
            step.inc(dve.tensor_scalar(B, A, float(1.0 / TWO_PI), MAGIC, ALU.mult, ALU.add))
            sync()
            step.inc(dve.tensor_scalar(B, B, MAGIC, None, ALU.subtract))
            c1 = 6.28125
            c2 = float(np.float32(TWO_PI - c1).view(np.uint32).__and__(0xFFFFF000).view(np.float32))
            c3 = float(TWO_PI - c1 - c2)
            for c in (c1, c2, c3):
                sync()
                step.inc(dve.scalar_tensor_tensor(out=A, in0=B, scalar=-c, in1=A, op0=ALU.mult, op1=ALU.add))
            sync()
            lim = 3.1415925
            step.inc(dve.tensor_scalar(RT[:, 1], A, float(np.pi / 2), None, ALU.add))
            sync()
            step.inc(dve.tensor_scalar(B, RT[:, 1], float(np.pi), -TWO_PI, ALU.is_gt, ALU.mult))
            sync()
            step.inc(dve.tensor_tensor(RT[:, 1], RT[:, 1], B, ALU.add))
            sync()
            step.inc(dve.tensor_scalar(RT[:, 1], RT[:, 1], lim, -lim, ALU.min, ALU.max))
            step.inc(dve.tensor_scalar(A, A, lim, -lim, ALU.min, ALU.max))
            sync()
            dve.tensor_scalar(RT[:, 0], A, cm("sign", 1), None, ALU.mult).then_inc(rope_q, 1)
            dve.memset(ZP[:, :, 0:H0], 0.0).then_inc(pads_zero, 1)
            dve.memset(UP[:, :, 0:16], 0.0).then_inc(pads_zero, 1)
            for k in range(4):
                t = T0["in"] + 2 * k
                m_read(dve, t + 1)
                dve.tensor_tensor(ZP[:, k, H0:H0 + S], mbank(t)[:, :], MSG[:, k % 2], ALU.mult).then_inc(conv_in, 1)
                dve.wait_ge(conv_in, k + 1)
                dve.engine_nop().then_inc(m_out[t % 4], 1)
            dve.wait_ge(act_step, 2)
            t = T0["in"] + 13
            m_ready(dve, t)
            dve.tensor_tensor(KT[:, 0], mbank(t)[:, :], COS, ALU.mult).then_inc(m_out[t % 4], 1)
            m_ready(dve, t + 1)
            dve.tensor_tensor(KT[:, 1], mbank(t + 1)[:, :], SIN, ALU.mult).then_inc(m_out[(t + 1) % 4], 1)
            m_read(dve, t)
            m_read(dve, t + 1)
            dve.tensor_tensor(KR, KT[:, 0], KT[:, 1], ALU.add).then_inc(k_rope_in, 1)
            for g in range(4):
                m_read(dve, T0["in"] + 15 + g)
                src = UP[:, g]
                lo = 0
                for r in range(g + 1):
                    w = 1 << r
                    lo += w
                    dst = PW[:, r % 2]
                    step.inc(dve.tensor_tensor(dst[:, lo:528], src[:, lo:528], src[:, lo - w:528 - w], ALU.add))
                    sync()
                    src = dst
                step.inc(dve.tensor_scalar(PW[:, (g + 1) % 2, 16:16 + S], src[:, 16:16 + S], 1.0 / POOL_W[g], None, ALU.mult))
                sync()
                mean = PW[:, (g + 1) % 2]
                ic = cstt[:, CST0["invcnt"] + 16 * g:CST0["invcnt"] + 16 * g + 16]
                step.inc(dve.tensor_tensor(mean[:, 16:32], src[:, 16:32], ic, ALU.mult))
                sync()
                dve.tensor_tensor(UP[:, g, 16:16 + S], mean[:, 16:16 + S], UP[:, g, 16:16 + S], ALU.subtract)\
                    .then_inc(pool_mixed, 1)
                dve.wait_ge(pool_mixed, g + 1)
            norm_dve("qrms")
            QH = ATT["att"]["QH"]
            for r in range(2):
                t = T0["uq"] + 4 + 2 * r
                m_ready(dve, t)
                dve.tensor_tensor(RT[:, 0], mbank(t)[:, :], COS, ALU.mult).then_inc(m_out[t % 4], 1)
                m_ready(dve, t + 1)
                dve.tensor_tensor(RT[:, 1], mbank(t + 1)[:, :], SIN, ALU.mult).then_inc(m_out[(t + 1) % 4], 1)
                m_read(dve, t)
                m_read(dve, t + 1)
                for j in range(4):
                    q = slice(32 * j, 32 * j + 32)
                    dve.tensor_tensor(QH[64:96, 4 * r + j], RT[q, 0], RT[q, 1], ALU.add).then_inc(rope_q, 1)
                dve.wait_ge(rope_q, 4 * r + 5)
            norm_dve("kvrms")
            attention("att", 0)
            dve.memset(MG, 0.0).then_inc(dve_step, 1)
            step.n += 1
            sync()

            def merge(i, b, conv):
                acc = ZB
                for m in range(C8):
                    t = T0["branch"] + (16 * b if i is None else 0) + 2 * m
                    m_ready(dve, t + 1, i, 16)
                    m_read(dve, t, i, 16)
                    sync()
                    dve.tensor_tensor(RT[:, m % 2], mbank(t + 1)[:, :], MSG[:, m % 2], ALU.mult)\
                        .then_inc(m_out[(t + 1) % 4], 1)
                    m_read(dve, t + 1, i, 16)
                    step.inc(dve.tensor_tensor(MG[:, m], MG[:, m], RT[:, m % 2], ALU.add))
                    if conv:
                        for j in range(4 * m, min(4 * m + 4, TAPS)):
                            for c in range(2):
                                o = one(acc[:, bass.ds(i * 2 + (8 + c), 1), :])
                                z = one(ZP[:, bass.ds(i * 2 + c, 1), j:j + S])
                                w = part[:, bass.ds(i * (2 * TAPS) + (PAR0["conv_dw"] + c * TAPS + j), 1)]
                                if j == 0:
                                    bb = part[:, bass.ds(i * 2 + (PAR0["conv_b"] + c), 1)]
                                    step.inc(dve.tensor_scalar(o, z, w, bb, ALU.mult, ALU.add))
                                else:
                                    dve.wait_ge(dve_step, step.now(1))
                                    step.inc(dve.scalar_tensor_tensor(out=o, in0=z, scalar=w, in1=o,
                                                                      op0=ALU.mult, op1=ALU.add))

            with dve.Fori(0, 2) as i:
                step.enter(i, C8 + 2 * TAPS)
                merge(i, 0, True)
            step.leave(2)
            sync()
            dve.engine_nop().then_inc(merged, 1)
            norm_dve("convln")
            merge(None, 2, False)
            sync()
            dve.engine_nop().then_inc(merged, 1)
            res_tiles("wout", ALPHA1, 1)
            norm_dve("ln1")
            for m in range(C8):
                t = T0["pp"] + m
                m_read(dve, T0["pg"] + m)
                m_ready(dve, t)
                dve.tensor_tensor(PG[:, m], PG[:, m], mbank(t)[:, :], ALU.mult).then_inc(m_out[t % 4], 1)
                m_read(dve, t)
                step.inc(dve.scalar_tensor_tensor(out=R[:, m], in0=X[:, m], scalar=ALPHA1, in1=PG[:, m],
                                                  op0=ALU.mult, op1=ALU.add))
            a_read(dve, A0["route"])
            rb = part[:, PAR0["router_bias"]:PAR0["router_bias"] + 16]
            for q in range(NT):
                c = slice(16 * q, 16 * q + 16)
                step.inc(dve.tensor_tensor(SEL[:, c], AFF[:, c], rb, ALU.add))
            step.inc(dve.memset(CMP[:, :], 0.0))

            def order(src, n):
                s4 = src.rearrange("p (g e) -> p g e", e=4)
                c4 = CMP[:, 0:16 * n].rearrange("p (g e j) -> p g e j", e=4, j=4)
                sync()
                for j in range(4):
                    for lo, hi, op in ((0, j, ALU.is_gt), (j + 1, 4, ALU.is_ge)):
                        if hi > lo:
                            b = s4[:, :, j:j + 1].to_broadcast([P, n, hi - lo])
                            step.inc(dve.tensor_tensor(c4[:, :, lo:hi, j], b, s4[:, :, lo:hi], op))
                sync()
                step.inc(dve.tensor_reduce(RANK[:, 0:4 * n], c4, AX.X, ALU.add))
                sync()

            order(SEL[:, 0:64], 16)
            step.inc(dve.tensor_scalar(KEEP[:, 0:64], RANK[:, 0:64], 2.0, None, ALU.is_lt))
            sync()
            step.inc(dve.tensor_tensor(SEL[:, 64:128], SEL[:, 0:64], KEEP[:, 0:64], ALU.mult))
            step.inc(dve.tensor_tensor(AFF[:, 64:128], AFF[:, 0:64], KEEP[:, 0:64], ALU.mult))
            sync()
            step.inc(dve.tensor_reduce(GSC[:, 0:16], SEL[:, 64:128].rearrange("p (g e) -> p g e", e=4), AX.X, ALU.add))
            order(GSC[:, 0:16], 4)
            step.inc(dve.tensor_scalar(KEEP[:, 0:16], RANK[:, 0:16], 1.0, None, ALU.is_lt))
            sync()
            k3 = KEEP[:, 0:16].rearrange("p (g o) -> p g o", o=1).to_broadcast([P, 16, 4])
            step.inc(dve.tensor_tensor(AFF[:, 0:64].rearrange("p (g e) -> p g e", e=4),
                                       AFF[:, 64:128].rearrange("p (g e) -> p g e", e=4), k3, ALU.mult))
            sync()
            step.inc(dve.tensor_reduce(GSC[:, 0:4], AFF[:, 0:64].rearrange("p (q e) -> p q e", e=16), AX.X, ALU.add))
            sync()
            step.inc(dve.reciprocal(GSC[:, 4:8], GSC[:, 0:4]))
            sync()
            for q in range(NT):
                c = slice(16 * q, 16 * q + 16)
                step.inc(dve.tensor_scalar(WTOK[:, c], AFF[:, c], GSC[:, 4 + q:5 + q], None, ALU.mult))
            sync()
            dve.engine_nop().then_inc(routed, 1)

            dve.wait_ge(wb_loaded, 16)
            with dve.Fori(0, EXPERTS) as i:
                for j in range(4):
                    t = T0["moe"] + 2 * j + 1
                    m_read(dve, t - 1, i, 16)
                    m_ready(dve, t, i, 16)
                    dve.tensor_tensor(ACTV[:, j], mbank(t)[:, :], ESG[:, j % 2], ALU.mult).then_inc(m_out[t % 4], 1)
                    m_read(dve, t, i, 16)
                    dve.tensor_tensor(ACTV[:, j], ACTV[:, j], one(WB[:, bass.ds(i, 1), :]), ALU.mult)\
                        .then_inc(moe_act, 1)
                for m in range(C8):
                    t = T0["moe"] + 8 + m
                    m_ready(dve, t, i, 16)
                    m_read(dve, t - 4, i, 16)
                    dve.tensor_tensor(R[:, m], R[:, m], mbank(t)[:, :], ALU.add).then_inc(m_out[t % 4], 1)
            for t in range(T0["s_in"] - 4, T0["s_in"]):
                m_read(dve, t)
            dve.engine_nop().then_inc(resid, 1)
            norm_dve("ln2")
            def log1p_dve(b, n):
                x_, ab, e, u, ln, o = (b[0:16, k] for k in range(6))
                a_read(dve, A0["f" if n else "dt"])
                step.inc(dve.tensor_scalar(ab, x_, -1.0, None, ALU.mult))
                sync()
                dve.tensor_tensor(ab, ab, x_, ALU.max).then_inc(dt_ln, 1)
                dve.wait_ge(dt_e, 2 * n + 1)
                dve.tensor_scalar(u, e, 1.0, None, ALU.add).then_inc(dt_ln, 1)
                dve.wait_ge(dt_ln, 2 * n + 2)
                step.inc(dve.tensor_scalar(o, u, -1.0, None, ALU.add))
                sync()
                step.inc(dve.tensor_tensor(o, e, o, ALU.subtract))
                step.inc(dve.reciprocal(ab, u))
                sync()
                step.inc(dve.tensor_tensor(o, o, ab, ALU.mult))
                sync()
                dve.wait_ge(dt_e, 2 * n + 2)
                step.inc(dve.tensor_tensor(o, o, ln, ALU.add))
                sync()

            x_, ab, e, u, ln, o = (DTB[0:16, k] for k in range(6))
            log1p_dve(DTB, 0)
            step.inc(dve.tensor_scalar(x_, x_, 0.0, None, ALU.max))
            sync()
            step.inc(dve.tensor_tensor(DT[0:16, :], x_, o, ALU.add))
            sync()
            dve.wait_ge(a_neg, 1)
            step.inc(dve.tensor_scalar(ab, DT[0:16, :], stat[0:16, 50:51], -1.0, ALU.mult, ALU.mult))
            sync()
            for c in range(NT):
                cs = slice(c * P, (c + 1) * P)
                ins = dve.tensor_tensor_scan(ACS[0:16, cs], ones[0:16, :], ab[:, cs], 0.0, ALU.mult, ALU.add)
            ins.then_inc(dte, 1)
            step.inc(dve.memset(CHP[:, :, 0:2], 0.0))
            for m in range(2):
                dve.memset(XP[:, m, 0:3], 0.0).then_inc(xbc_conv, 1)
            sync()
            dve.wait_ge(a_neg, 2)
            dve.tensor_tensor(DTE[0:16, :], DTE[0:16, :], DT[0:16, :], ALU.mult).then_inc(dt_ready, 1)

            with dve.Fori(0, 2) as i:
                step.enter(i, 4 * 3)
                for m in range(4):
                    t = T0["s_in"] + 3 * m
                    m_read(dve, t, i, 12)
                    m_ready(dve, t + 1, i, 12)
                    dve.tensor_tensor(CHP[:, m % 2, 2:2 + S], mbank(t + 1)[:, :], CS[:, m % 2], ALU.mult)\
                        .then_inc(m_out[(t + 1) % 4], 1)
                    m_read(dve, t + 1, i, 12)
                    if m == 0:
                        sync()

                    def w(j):
                        return part[:, bass.ds(i * 12 + (PAR0["sc_conv"] + 3 * m + j), 1)]
                    step.inc(dve.tensor_scalar(CT[:, m % 2], CHP[:, m % 2, 2:2 + S], w(2), None, ALU.mult))
                    for j in (1, 0):
                        sync()
                        step.inc(dve.scalar_tensor_tensor(out=CT[:, m % 2], in0=CHP[:, m % 2, j:j + S], scalar=w(j),
                                                          in1=CT[:, m % 2], op0=ALU.mult, op1=ALU.add))
                    sync()
                    m_ready(dve, t + 2, i, 12)
                    dve.tensor_tensor(one(YY[:, bass.ds(i * 4 + m, 1), :]), mbank(t + 2)[:, :], CT[:, m % 2],
                                      ALU.mult).then_inc(m_out[(t + 2) % 4], 1)
                    m_read(dve, t + 2, i, 12)
            step.leave(2)
            with dve.Fori(0, 3) as i:
                step.enter(i, 4 * 3)
                for m in range(4):
                    t = T0["s_in"] + 32 + m
                    m_read(dve, t, i, 4)

                    def w(j):
                        return part[:, bass.ds(i * 16 + (PAR0["ssm_conv"] + 4 * m + j), 1)]
                    step.inc(dve.tensor_scalar(XA[:, m % 2], XP[:, m % 2, 3:3 + S], w(3), None, ALU.mult))
                    for j in (2, 1, 0):
                        sync()
                        ins = dve.scalar_tensor_tensor(out=XA[:, m % 2], in0=XP[:, m % 2, j:j + S], scalar=w(j),
                                                       in1=XA[:, m % 2], op0=ALU.mult, op1=ALU.add)
                        if j:
                            step.inc(ins)
                        else:
                            ins.then_inc(xbc_conv, 1)
            step.leave(3)
            a_read(dve, A0["acst"])
            for c in range(NT):
                for g in range(2):
                    t = A0["xtok"] + 2 * c + g
                    a_ready(dve, t)
                    src = abank(t)[:, :].rearrange("p (h f) -> p h f", f=64)

                    def by_head(n):
                        a = 64 * n + 16 * c + 8 * g
                        return TK[:, a:a + 8].rearrange("p (h o) -> p h o", o=1).to_broadcast([P, 8, 64])
                    if c < NT - 1:
                        dve.tensor_tensor(DX[:, 2 * c + g].rearrange("p (h f) -> p h f", f=64), src, by_head(2),
                                          ALU.mult).then_inc(ssd_dx, 1)
                    dve.tensor_tensor(XDT[:, c, g * 512:g * 512 + 512].rearrange("p (h f) -> p h f", f=64), src,
                                      by_head(1), ALU.mult).then_inc(a_out[t % 4], 1)
            a_read(dve, A0["cb"])
            a_read(dve, A0["cb"] + 1)
            for n in range(6):
                a_read(dve, A0["state"] + n)

            def finish_pair(j):
                t = pair_tile(j)
                a_ready(dve, t)
                dve.scalar_tensor_tensor(out=YY[:, 8 + j], in0=XBC[:, j], scalar=pc("ssm_d", j), in1=abank(t)[:, :],
                                         op0=ALU.mult, op1=ALU.add).then_inc(a_out[t % 4], 1)
                a_read(dve, t)
                dve.tensor_tensor(YY[:, 8 + j], YY[:, 8 + j], ZS[:, j], ALU.mult).then_inc(sc_y, 1)

            for j in range(C8):
                for h in (2 * j, 2 * j + 1):
                    t = head_tile(h)
                    dve.wait_ge(ssd_u, h + 1)
                    for c in range(NT):
                        cs = slice(c * P, (c + 1) * P)
                        if h >= 2 and c == 0:
                            dve.wait_ge(ssd_m, h - 1)
                        dve.scalar_tensor_tensor(out=LB[:, h % 2, cs], in0=abank(t)[:, cs],
                                                 scalar=TK[:, 16 * c + h:16 * c + h + 1], in1=cm("mask_ssd"),
                                                 op0=ALU.subtract, op1=ALU.add).then_inc(ssd_d, 1)
                    dve.wait_ge(ssd_d, 4 * h + 4)
                    dve.engine_nop().then_inc(a_out[t % 4], 1)
                if j:
                    finish_pair(j - 1)
                for h in (2 * j, 2 * j + 1):
                    g = h // 8
                    dve.wait_ge(ssd_l, h + 1)
                    dve.tensor_tensor(MB[:, h % 2], LB[:, h % 2], CBS[:, g], ALU.mult).then_inc(ssd_m, 1)
                    f = slice((h % 8) * 64, (h % 8) * 64 + 64)
                    for c in (1, 2):
                        dve.scalar_tensor_tensor(out=SQ[:, 2 * c + g, f], in0=SQ[:, 2 * (c - 1) + g, f],
                                                 scalar=EB[:, h % 2, (c + 1) * P - 1:(c + 1) * P],
                                                 in1=SQ[:, 2 * c + g, f], op0=ALU.mult, op1=ALU.add)\
                            .then_inc(ssd_prev, 1)
                        dve.wait_ge(ssd_prev, 2 * h + c)
            finish_pair(C8 - 1)
            norm_dve("grms0")
            norm_dve("grms1")
            res_tiles("sout", ALPHA2, 1)
            norm_dve("lnm0")

            def ffn(layer, last):
                for k in range(4):
                    dve.memset(FP[:, k, 0:2], 0.0).then_inc(ffn_conv, 1)
                dve.wait_ge(ffn_conv, 48 * layer + 4)
                with dve.Fori(0, FT // 2) as i:
                    step.enter(i, 8)

                    def conv(k):
                        t = T0[f"up{layer}"] + k
                        m_read(dve, t, i, 4)
                        c = k // 2 + (FT if k % 2 else 0)

                        def w(j):
                            return part[:, bass.ds(i * 6 + (PAR0[f"ffn_conv{layer}"] + 3 * c + j), 1)]
                        b = part[:, bass.ds(i * 2 + (PAR0[f"ffn_b{layer}"] + c), 1)]
                        step.inc(dve.tensor_scalar(TF[:, k], FP[:, k, 2:2 + S], w(2), b, ALU.mult, ALU.add))
                        sync()
                        step.inc(dve.scalar_tensor_tensor(out=TF[:, k], in0=FP[:, k, 1:1 + S], scalar=w(1),
                                                          in1=TF[:, k], op0=ALU.mult, op1=ALU.add))
                        sync()
                        dve.scalar_tensor_tensor(out=TF[:, k], in0=FP[:, k, 0:S], scalar=w(0), in1=TF[:, k],
                                                 op0=ALU.mult, op1=ALU.add).then_inc(ffn_conv, 1)

                    def gate(r):
                        dve.wait_ge(ffn_silu, i * 2 + (FT * layer + r + 1))
                        dve.tensor_tensor(one(G[:, bass.ds(i * 2 + r, 1), :]), TF[:, 2 * r], TF[:, 2 * r + 1],
                                          ALU.mult).then_inc(ffn_g, 1)
                        dve.wait_ge(ffn_g, i * 2 + (FT * layer + r + 1))

                    conv(0)
                    conv(1)
                    conv(2)
                    gate(0)
                    conv(3)
                    gate(1)
                step.leave(FT // 2)
                res_tiles(f"down{layer}", ALPHA2, 1)
                norm_dve(last)

            ffn(0, "lnf0")
            dve.memset(ar(_x["QH"], 32)[64:66], 1.0).then_inc(f_ones, 1)
            log1p_dve(FB, 1)
            x_, ab, o = FB[0:16, 0], FB[0:16, 1], FB[0:16, 5]
            step.inc(dve.tensor_scalar(x_, x_, 0.0, None, ALU.min))
            sync()
            step.inc(dve.tensor_tensor(x_, x_, o, ALU.subtract))
            sync()
            for c in range(NT):
                cs = slice(c * P, (c + 1) * P)
                init = ab[:, c * P - 1:c * P] if c else 0.0
                step.inc(dve.tensor_tensor_scan(ab[:, cs], ones[0:16, :], x_[:, cs], init, ALU.mult, ALU.add))
                sync()
            dve.tensor_scalar(F8[0:16, 0], ab, 8.0, None, ALU.mult).then_inc(f_cum, 1)
            dve.tensor_scalar(F8[0:16, 1], ab, -8.0, None, ALU.mult).then_inc(f_cum, 1)
            attention("fatt", 0)
            res_tiles("fout", ALPHA2, 1)
            norm_dve("lnm1")
            ffn(1, "lnf1")

        @block.gpsimd
        def _(pool):
            def attention(name):
                a = ATT[name]

                def copies(h, i=None):
                    if h >= 2 or i is not None:
                        pool.wait_ge(m_full, lin(i, 8, T0[name] + 4 * (h - 2) + 4))
                    q = a["QH"][0:a["K"], h] if i is None else one(a["QH"][0:a["K"], bass.ds(i * 2 + h, 1), :])
                    pool.tensor_copy(a["QB"][0:a["K"], h % 2], q).then_inc(att_q, 1)
                    pool.wait_ge(att_q, lin(i, 2, a["h0"] + h + 1))
                    if h >= 2 or i is not None:
                        pool.wait_ge(a_full, lin(i, 8, A0[name] + 4 * (h - 2) + 4))
                    at = h * 64 if i is None else None
                    v = a["V"][:, :, at:at + 64] if i is None else a["V"][:, :, bass.ds(i * 128 + h * 64, 64)]
                    pool.tensor_copy(a["VB"][:, 4 * (h % 2):4 * (h % 2) + 4, :], v).then_inc(att_v, 1)
                    pool.wait_ge(att_v, lin(i, 2, a["h0"] + h + 1))

                for h in range(2):
                    copies(h)
                with pool.Fori(0, a["n"] // 2 - 1) as i:
                    copies(2, i)
                    copies(3, i)

            pool.wait_ge(k_rope_in, 1)
            for h in range(HEADS1):
                pool.tensor_copy(ATT["att"]["KH"][64:96, h], KR[64:96, :]).then_inc(k_rope, 1)
                pool.wait_ge(k_rope, h + 1)
            pool.wait_ge(rope_q, 9)
            for j in range(4):
                m_read(pool, T0["uv"] + j)
            attention("att")
            pool.wait_ge(m_full, T0["s_in"])
            pool.dma_start(SEL16[0:16, :], sel16).then_inc(sel_loaded, 16)
            pool.wait_ge(xbc_done, 12)
            for h in range(SSM_H):
                pool.wait_ge(ssd_u, h + 1)
                if h >= 2:
                    a_ready(pool, pair_tile(h // 2 - 1))
                pool.tensor_tensor(CSB[:, h % 2], EB[:, h % 2], XBC[:, 10 + h // 8], ALU.mult).then_inc(ssd_e, 1)
                pool.wait_ge(ssd_e, h + 1)
            pool.wait_ge(f_ones, 1)
            pool.wait_ge(f_cum, 2)
            pool.dma_start(ATT["fatt"]["QH"][65:66], F8[0:16, 0]).then_inc(f_rows, 16)
            pool.dma_start(ATT["fatt"]["KH"][64:65], F8[0:16, 1]).then_inc(f_rows, 16)
            for q in range(NT):
                m_read(pool, T0["fv"] + 4 + q)
            pool.wait_ge(f_rows, 32)
            attention("fatt")


def _blocks(w, cols):
    k = w.shape[0] // P
    return [w[i * P:(i + 1) * P, c:c + P] for c in cols for i in range(k)]


def _tiles(w, a=0, b=None):
    return _blocks(w, range(a, w.shape[1] if b is None else b, P))


def _wide(w, width):
    k = w.shape[0] // P
    return [w[i * P:(i + 1) * P, c + j:c + j + P]
            for c in range(0, w.shape[1], width) for i in range(k) for j in range(0, width, P)]


def _stream(a):
    w_in = a["w_in"][0]
    off = np.cumsum([0, 512, 512, 512, QL, KVL, ROPE])
    kr = w_in[:, off[5]:off[6]]
    krs = np.concatenate([kr[:, 16:], kr[:, :16]], 1)
    b = []
    for j in range(4):
        b += _blocks(w_in, [off[1] + j * P]) + _blocks(w_in, [off[2] + j * P])
    b += _tiles(w_in, off[3], off[5])
    b += _tiles(np.concatenate([kr] * 4, 1)) + _tiles(np.concatenate([krs] * 4, 1))
    b += _tiles(w_in, 0, 512)
    uq = a["w_uq"][0].reshape(QL, HEADS1, NOPE + ROPE)
    b += _tiles(uq[:, :, :NOPE].reshape(QL, -1))
    for r in range(2):
        rope = uq[:, 4 * r:4 * r + 4, NOPE:]
        b += _tiles(rope.reshape(QL, -1)) + _tiles(np.concatenate([rope[..., 16:], rope[..., :16]], -1).reshape(QL, -1))
    ukv = a["w_ukv"][0].reshape(KVL, HEADS1, NOPE + VH)
    b += _tiles(ukv[:, :, :NOPE].reshape(KVL, -1)) + _wide(ukv[:, :, NOPE:].reshape(KVL, -1), 512)
    for g, name in ((0, "pool_proj"), (2, "mla_proj"), (1, "conv_proj")):
        for m in range(C8):
            b += _blocks(w_in, [off[6] + g * D + m * P]) + _blocks(a[name][0], [m * P])
    b += _tiles(a["w_out"][0]) + _tiles(a["ple_gate"][0]) + _tiles(a["ple_proj"][0])
    for e in range(EXPERTS):
        up = a["exp_w_up"][0, e]
        for j in range(4):
            b += _blocks(up, [j * P, FE + j * P])
        b += _tiles(a["exp_w_down"][0, e])
    s = a["sc_ssm_w_in_2"][0]
    for m in range(C8):
        b += _blocks(s, [D + m * P, 2 * D + m * P, m * P])
    b += _tiles(s, 3 * D, 4 * D + 1536)
    b += _tiles(a["sc_ssm_w_out_2"][0])

    def ffn(i):
        up = a["ffn_w_up_2"][i]
        r = []
        for m in range(FT):
            r += _blocks(up, [m * P, FF + m * P])
        return r + _tiles(a["ffn_w_down_2"][i])

    b += ffn(0)
    fox = a["fox_w_in_2"][0]
    b += _tiles(fox, 0, 2 * D) + _wide(fox[:, 2 * D:3 * D], 512) + _tiles(a["fox_w_out_2"][0])
    b += ffn(1)
    assert len(b) == NSLABS * SLAB, (len(b), NSLABS * SLAB)
    out = np.empty((NSLABS, P, SLAB, P), np.float32)
    for n, x in enumerate(b):
        out[n // SLAB, :, n % SLAB] = x
    return out.reshape(NSLABS, P, SLAB * P)


def _params(a):
    part = np.zeros((P, NPAR), np.float32)

    def put(name, v):
        part[:v.shape[0], PAR0[name]:PAR0[name] + v.shape[1]] = v

    def col(v):
        return v.reshape(-1, P).T

    def taps(w):
        return w.T.reshape(w.shape[1] // P, P, w.shape[0]).transpose(1, 0, 2).reshape(P, -1)

    for name, key in (("ln_in_g", "ln_in_g"), ("ln_in_b", "ln_in_b")):
        put(name, col(a[key]))
    put("b_gate", col(a["b_gate"][0][[0, 2, 1]].reshape(-1)))
    for name, key in (("pool_scale", "pool_scale"), ("conv_b", "conv_b"), ("conv_ln_g", "conv_ln_g"),
                      ("conv_ln_b", "conv_ln_b"), ("q_norm_g", "q_norm_g"), ("kv_norm_g", "kv_norm_g"),
                      ("ln1_g", "ln1_g"), ("ln1_b", "ln1_b"), ("ln2_g", "ln2_g"), ("ln2_b", "ln2_b"),
                      ("ssm_conv_b", "ssm_conv_b_2"), ("ssm_norm_g", "ssm_norm_g_2")):
        put(name, col(a[key][0]))
    put("conv_dw", taps(a["conv_dw"][0]))
    put("sc_conv", taps(a["sc_conv_w_2"][0]))
    put("ssm_conv", taps(a["ssm_conv_w_2"][0]))
    put("ssm_d", col(np.repeat(a["ssm_d_2"][0], SSM_P)))
    for i in range(2):
        put(f"ffn_conv{i}", taps(a["ffn_conv_w_2"][i]))
        put(f"ffn_b{i}", col(a["ffn_conv_b_2"][i]))
        for k, key in (("lnm", "ln_mix"), ("lnf", "ln_ffn")):
            put(f"{k}{i}_g", col(a[f"{key}_g_2"][i]))
            put(f"{k}{i}_b", col(a[f"{key}_b_2"][i]))
    put("dt_bias", a["ssm_dt_bias_2"][0][:, None])
    put("a_log", a["ssm_a_log_2"][0][:, None])
    put("b_f", a["fox_b_f_2"][0][:, None])
    put("router_bias", np.broadcast_to(a["router_bias"], (P, EXPERTS)))

    def rows(w):
        return w.reshape(-1, P, w.shape[1]).transpose(1, 0, 2).reshape(P, -1)

    put("router", rows(a["w_router"]))
    put("w_dt", rows(a["sc_ssm_w_in_2"][0][:, 4 * D + 1536:]))
    put("w_f", rows(a["fox_w_in_2"][0][:, 3 * D:]))
    put("pool_w", a["pool_w"][0].transpose(1, 0, 2).reshape(P, -1))
    return part


def _constants():
    c = np.zeros((P, NCST), np.float32)
    q, k = np.meshgrid(np.arange(P), np.arange(P), indexing="ij")

    def put(name, v):
        c[:, CST0[name]:CST0[name] + v.shape[1]] = v

    put("ident", np.eye(P))
    put("ones", np.ones((P, P)))
    put("mask_fox", np.where(k <= q, 0, NEG))
    put("mask_mla", np.where(k // 64 <= q // 64, 0, NEG))
    put("mask_ssd", np.where(q <= k, 0, NEG))
    put("invcnt", np.broadcast_to(np.concatenate([1.0 / np.minimum(np.arange(16) + 1, w) for w in POOL_W]), (P, 64)))
    j = np.arange(P) % 16
    put("invfreq", (np.float32(10000.0) ** (-(2 * j).astype(np.float32) / np.float32(ROPE)))[:, None])
    put("sign", np.where(np.arange(P) % 32 < 16, -1.0, 1.0)[:, None])
    for name, v in (("ln_eps", 1e-5), ("rms_eps", 1e-6), ("zero", 0.0), ("one", 1.0), ("halfpi", np.pi / 2)):
        put(name, np.full((P, 1), v))
    sel = np.zeros((16, 16, P), np.float32)
    sel[np.arange(16), np.arange(16)] = 1.0
    return c, sel.reshape(16, -1)


def kernel(**inputs):
    from concourse import bacc
    from concourse.bass_utils import run_bass_kernel_spmd

    a = {k: np.asarray(v) for k, v in inputs.items()}
    cst, sel = _constants()
    arrays = {
        "w_stream": _stream(a),
        "x_t": np.ascontiguousarray(a["x"][0].T),
        "p_t": np.ascontiguousarray(a["p"][0, 0].T),
        "positions": np.ascontiguousarray(np.broadcast_to(a["positions"][0], (P, S))),
        "params": _params(a),
        "constants": cst,
        "sel16": sel,
    }
    nc = bacc.Bacc("TRN2", target_bir_lowering=False, num_devices=1)
    aps = [nc.dram_tensor(k, v.shape, mybir.dt.from_np(v.dtype), kind="ExternalInput").ap() for k, v in arrays.items()]
    w_scratch = nc.dram_tensor("w_scratch", (EXPERTS, S), F32, kind="Internal").ap()
    out = nc.dram_tensor("out_t", (D, S), F32, kind="ExternalOutput").ap()
    build(nc, *aps, w_scratch, out)
    r = run_bass_kernel_spmd(nc, [arrays], core_ids=[0])
    return np.ascontiguousarray(np.asarray(r.results[0]["out_t"]).T)[None]
```

```python
from contextlib import ExitStack

import numpy as np

import concourse.bass as bass
from concourse import mybir

F32 = mybir.dt.float32
I32 = mybir.dt.int32
ALU = mybir.AluOpType
ACT = mybir.ActivationFunctionType
AX = mybir.AxisListType

P = 128
S = 512
D = 1024
C8 = D // P
NT = S // P
NS = 4
SLAB = 8

POOL_W = (2, 4, 8, 16)
TAPS = 31
HEADS1, NOPE, ROPE, VH = 8, 64, 32, 64
QL, KVL = 384, 256
EXPERTS, FE, TOPK = 16, 512, 2
NB = EXPERTS + (TOPK * S - EXPERTS) // P
ALPHA1 = 2.0 ** 0.25
ALPHA2 = 4.0 ** 0.25
SSM_H, SSM_P, SSM_N = 16, 64, 128
FOX_H = 16
FF = 2816
FT = FF // P
NEG = -1e30
TWO_PI = 2.0 * np.pi
MAGIC = 1.5 * 2.0 ** 23

STAGES = [("in", 19, 19), ("uq", 3, 8), ("uk", 1, 4), ("uv", 1, 4), ("att", 0, 4 * HEADS1),
          ("branch", 36, 48), ("wout", 8, 8), ("pg", 8, 8), ("pp", 2, 8), ("moe", 12 * NB, 4 * NB),
          ("s_in", 44, 44), ("sout", 16, 8), ("up0", 44, 44), ("down0", 22, 8), ("fqk", 16, 16), ("fv", 8, 8),
          ("fatt", 0, 4 * FOX_H), ("fout", 8, 8), ("up1", 44, 44), ("down1", 22, 8)]
AUX = [("ln_in", 2), ("qrms", 1), ("kvrms", 1), ("poolw", 4), ("att", 4 * HEADS1), ("convln", 2), ("ln1", 2),
       ("route", 1), ("xtok1", 8), ("count", 1), ("moe", 4 * NB), ("mout", 8), ("ln2", 2), ("dt", 1), ("acst", 1), ("btok", 2), ("xtok", 8), ("cb", 2),
       ("state", 6), ("head", 24), ("grms0", 1), ("grms1", 1), ("lnm0", 2), ("lnf0", 2), ("f", 1),
       ("fatt", 4 * FOX_H), ("lnm1", 2), ("lnf1", 2)]


def starts(rows, k):
    out, at = {}, 0
    for row in rows:
        out[row[0]] = at
        at += row[k]
    return out, at


SLAB0, NSLABS = starts(STAGES, 1)
T0, _ = starts(STAGES, 2)
A0, _ = starts(AUX, 1)

PAR = [("ln_in_g", 8), ("ln_in_b", 8), ("b_gate", 24), ("pool_scale", 4), ("conv_dw", 4 * TAPS), ("conv_b", 4),
       ("conv_ln_g", 4), ("conv_ln_b", 4), ("q_norm_g", 3), ("kv_norm_g", 2), ("ln1_g", 8), ("ln1_b", 8),
       ("ln2_g", 8), ("ln2_b", 8), ("sc_conv", 24), ("ssm_conv", 48), ("ssm_conv_b", 12), ("ssm_d", 8),
       ("ssm_norm_g", 8), ("ffn_conv0", 132), ("ffn_conv1", 132), ("ffn_b0", 44), ("ffn_b1", 44),
       ("lnm0_g", 8), ("lnm0_b", 8), ("lnm1_g", 8), ("lnm1_b", 8), ("lnf0_g", 8), ("lnf0_b", 8),
       ("lnf1_g", 8), ("lnf1_b", 8), ("dt_bias", 1), ("a_log", 1), ("b_f", 1), ("router_bias", 16),
       ("router", 128), ("w_dt", 128), ("w_f", 128), ("pool_w", 512)]
PAR0, NPAR = starts(PAR, 1)
CST = [("ident", 128), ("ones", 128), ("mask_fox", 128), ("mask_mla", 128), ("mask_ssd", 128), ("invcnt", 64), ("before", 128), ("iota", NB), ("tokens", 4),
       ("invfreq", 1), ("sign", 1), ("ln_eps", 1), ("rms_eps", 1), ("zero", 1), ("one", 1), ("halfpi", 1)]
CST0, NCST = starts(CST, 1)

MIX = dict(ZB=0, ZP=6144, UP=8320, PW=10432, CQ=11488, CKV=13024, KT=14048, KR=15072, COS=15584,
           SIN=16096, QH=16608, KH=20704, V=24800, RT=26848, QB=27872, VB=28896, PTS=29408, SG=30688, MG=16608)
MOE = dict(XG=0, XST=2048, YO=4096, SGB=6144, ACTB=6656, ACTT=7168, PG=7680, XTK=11776, SEL=15872, YG=17920,
           MT=22016, PLE=31712)
SSM = dict(ZS=0, XBC=4096, Y=10240, T=18432, BT=18432, XDT=19456, ONE=23568, CB=25616, DT=26640,
           DTV=29712, DTE=30224, ACS=30736, TK=31248)
FFN = dict(G=0, PAD=11264, T=13320)
FOX = dict(QH=0, KH=8192, V=16384, O=20480, PTS=24576, QB=25856, VB=26880, F=27392)
ARENA = 32800


class Count:

    def __init__(self, sem):
        self.sem, self.n, self.i, self.per = sem, 0, None, 0

    def inc(self, ins):
        ins.then_inc(self.sem, 1)
        self.n += 1

    def now(self, back=0):
        return self.n - back if self.i is None else self.i * self.per + (self.n - back)

    def enter(self, i, per):
        self.i, self.per, self.base = i, per, self.n

    def leave(self, rounds):
        assert self.n == self.base + self.per, (self.n - self.base, self.per)
        self.n, self.i = self.base + self.per * rounds, None


def lin(i, per, base):
    return base if i is None else i * per + base


def one(ap):
    return ap.rearrange("p o n -> p (o n)")


def build(nc, w_stream, x, p, positions, par, cst, sel16, x_tok, slot_tok, y_slots, out):
    with ExitStack() as ctx:
        def sb(name, cols, dt=F32):
            return ctx.enter_context(nc.sbuf_tensor(name, [P, cols], dt))

        def sem(name):
            return ctx.enter_context(nc.semaphore(name))

        ring = sb("ring", NS * SLAB * P)
        Xt, Rt, SQt = sb("X", C8 * S), sb("R", C8 * S), sb("SQ", C8 * S)
        X, R, SQ = (t[:, :].rearrange("p (c s) -> p c s", s=S) for t in (Xt, Rt, SQt))
        part = sb("part", NPAR)
        cstt = sb("cstt", NCST)
        STD, RSTD = sb("STD", S), sb("RSTD", S)
        stat = sb("stat", 64)
        arena = sb("arena", ARENA)
        bank = [ctx.enter_context(nc.psum_tensor(f"bank{i}", [P, S], F32)) for i in range(8)]

        slab_full = [sem(f"slab_full{i}") for i in range(NS)]
        slab_used = sem("slab_used")
        m_full, a_full = sem("m_full"), sem("a_full")
        m_out = [sem(f"m_out{i}") for i in range(4)]
        a_out = [sem(f"a_out{i}") for i in range(4)]
        loaded, p_loaded, sel_loaded = sem("loaded"), sem("p_loaded"), sem("sel_loaded")
        dve_step, act_step, pool_step = sem("dve_step"), sem("act_step"), sem("pool_step")
        ln_centred, ln_rstd, ln_scaled = sem("ln_centred"), sem("ln_rstd"), sem("ln_scaled")
        ln_squared, ln_std, ln_done = sem("ln_squared"), sem("ln_std"), sem("ln_done")
        conv_in, pads_zero, pool_mixed, rope_q, k_rope, k_rope_in = (
            sem("conv_in"), sem("pads_zero"), sem("pool_mixed"), sem("rope_q"), sem("k_rope"), sem("k_rope_in"))
        att_q, att_v, att_masked, att_max, att_nm, att_rs, att_prob = (
            sem(n) for n in ("att_q", "att_v", "att_masked", "att_max", "att_nm", "att_rs", "att_prob"))
        merged, resid = sem("merged"), sem("resid")
        routed, xtok_sent, slots_known, experts_known, ints, table_zero, table_set, table_read = (
            sem(n) for n in ("routed", "xtok_sent", "slots_known", "experts_known", "ints", "table_zero", "table_set",
                             "table_read"))
        tok_sum = sem("tok_sum")
        xg_loaded, yo_sent = [sem(f"xg_loaded{n}") for n in range(2)], [sem(f"yo_sent{n}") for n in range(2)]
        yg_loaded = [sem(f"yg_loaded{n}") for n in range(4)]
        sc_y, xbc_conv, xbc_done, dt_e, dt_ln, a_neg, dt_ready = (
            sem(n) for n in ("sc_y", "xbc_conv", "xbc_done", "dt_e", "dt_ln", "a_neg", "dt_ready"))
        ssd_dx, ssd_prev, ssd_l, ssd_e, ssd_m, ssd_d, ssd_u, dte = (
            sem(n) for n in ("ssd_dx", "ssd_prev", "ssd_l", "ssd_e", "ssd_m", "ssd_d", "ssd_u", "dte"))
        ffn_conv, ffn_g, ffn_silu = sem("ffn_conv"), sem("ffn_g"), sem("ffn_silu")
        f_e, f_ln, f_cum, f_rows, f_ones = (sem(n) for n in ("f_e", "f_ln", "f_cum", "f_rows", "f_ones"))
        out_done = sem("out_done")

        def pc(name, j=0, rows=slice(0, P)):
            return part[rows, PAR0[name] + j:PAR0[name] + j + 1]

        def pmat(name, k, w):
            return part[:, PAR0[name] + k * w:PAR0[name] + (k + 1) * w]

        def cm(name, w=P, rows=slice(0, P)):
            return cstt[rows, CST0[name]:CST0[name] + w]

        def ar(at, n, w=S, rows=slice(0, P)):
            return arena[rows, at:at + n * w].rearrange("p (c s) -> p c s", s=w)

        ident, ones = cm("ident"), cm("ones")
        _m, _o, _s, _x, _f = MIX, MOE, SSM, FOX, FFN
        ZB = ar(_m["ZB"], 12)
        ZP = ar(_m["ZP"], 4, 544)
        UP = ar(_m["UP"], 4, 528)
        PW = ar(_m["PW"], 2, 528)
        CQ, CKV, KT = ar(_m["CQ"], 3), ar(_m["CKV"], 2), ar(_m["KT"], 2)
        KR, COS, SIN = (arena[:, _m[n]:_m[n] + S] for n in ("KR", "COS", "SIN"))
        RT, MSG, MG = ar(_m["RT"], 2), ar(_m["SG"], 2), ar(_m["MG"], 8)
        H0 = TAPS - 1
        XG, XST, YO = ar(_o["XG"], 2, D), ar(_o["XST"], 2 * C8, P), ar(_o["YO"], 2, D)
        SGB, ACTB, ACTT = (arena[:, _o[n]:_o[n] + S] for n in ("SGB", "ACTB", "ACTT"))
        PG, XTK, YG, MT = ar(_o["PG"], 8), ar(_o["XTK"], 4, D), ar(_o["YG"], 4, D), ar(_o["MT"], 4, D)
        PLE = ar(_o["PLE"], 2)
        SEL, AFF, CMP, RANK, KEEP, GSC, WTOK = (
            arena[:, _o["SEL"] + a:_o["SEL"] + b] for a, b in
            ((0, 128), (128, 256), (256, 512), (512, 576), (576, 640), (640, 656), (656, 720)))
        DEST, DTMP, CNT, BEND, BSTART, BCMP, BEXP = (
            arena[:, _o["SEL"] + a:_o["SEL"] + b] for a, b in
            ((720, 784), (784, 848), (848, 912), (912, 928), (928, 944), (944, 944 + 16 * NB),
             (944 + 16 * NB, 944 + 17 * NB)))
        MISC = _o["SEL"] + 944 + 17 * NB
        DMM, DWT, KIN = arena[:, MISC:MISC + 8], arena[:, MISC + 8:MISC + 16], arena[:, MISC + 16:MISC + 80]
        DI, TOKI, BEI, IDX, ZI = (
            arena[:, MISC + a:MISC + b].bitcast(I32) for a, b in
            ((80, 88), (88, 92), (92, 92 + NB), (92 + NB, 92 + 2 * NB), (92 + 2 * NB, 92 + 3 * NB)))

        def gate_tile(b):
            return T0["moe"] + (4 * b - 2 if b else 0)

        def down_tile(b):
            return T0["moe"] + (4 * b + 4 if b < NB - 1 else 4 * NB - 2)

        def xt_tile(b):
            return A0["moe"] + (4 * b - 1 if b >= 2 else 3 * b)

        def actt_tile(b):
            return A0["moe"] + (4 * b + 6 if b < NB - 1 else 4 * NB - 1)
        ZS, XBC, BT, CBS = ar(_s["ZS"], 8), ar(_s["XBC"], 12), ar(_s["BT"], 2), ar(_s["CB"], 2)
        XDT, DX, SEL16 = ar(_s["XDT"], 4, 1024), R[:, 0:6], arena[:, _s["ONE"]:_s["ONE"] + 2048]
        YY = ar(_s["Y"], 16)
        DTB = ar(_s["DT"], 6)
        DT, DTE, ACS, TK = (arena[:, _s[n]:_s[n] + S] for n in ("DTV", "DTE", "ACS", "TK"))
        CS, CHP, CT = ar(_s["T"], 2), ar(_s["T"] + 1024, 2, 514), ar(_s["T"] + 2052, 2)
        XP, XA = ar(_s["T"] + 3076, 2, 515), ar(_s["T"] + 4106, 2)
        EB, LB, MB, CSB = R[:, 0:2], R[:, 2:4], R[:, 4:6], R[:, 6:8]
        G, FP, TF = ar(_f["G"], FT), ar(_f["PAD"], 4, 514), ar(_f["T"], 4)
        FB, F8 = ar(_x["F"], 6), ar(_x["F"] + 3072, 2)

        def head_tile(h):
            return A0["head"] + (h if h < 2 else 3 * (h // 2) - 1 + h % 2)

        def pair_tile(j):
            return A0["head"] + (3 * j + 4 if j < 7 else 23)

        ATT = {
            "att": dict(n=HEADS1, K=NOPE + ROPE, QH=ar(_m["QH"], 8), KH=ar(_m["KH"], 8), V=ar(_m["V"], 4, 512),
                        O=ZB[:, 4:8], PR=R, PTS=arena[:, _m["PTS"]:_m["PTS"] + 1280],
                        QB=ar(_m["QB"], 2), VB=ar(_m["VB"], 8, 64), scale=float((NOPE + ROPE) ** -0.5),
                        mask=cm("mask_mla"), h0=0),
            "fatt": dict(n=FOX_H, K=66, QH=ar(_x["QH"], 16), KH=ar(_x["KH"], 16), V=ar(_x["V"], 4, 1024),
                         O=ar(_x["O"], 8), PR=R, PTS=arena[:, _x["PTS"]:_x["PTS"] + 1280],
                         QB=ar(_x["QB"], 2), VB=ar(_x["VB"], 8, 64), scale=0.125, mask=cm("mask_fox"), h0=HEADS1),
        }
        NORMS = {}
        total = dict(centred=0, n=0, scaled=0, squared=0)

        def norm(name, c, src, dst, g, b, eps, fn=ACT.Identity):
            NORMS[name] = dict(c=c, src=src, dst=dst, g=g, b=b, eps=eps, fn=fn, ln=b is not None, **total)
            total["centred"] += c if b is not None else 0
            total["n"] += 1
            total["scaled"] += c
            total["squared"] += c

        norm("ln_in", 8, X, X, "ln_in_g", "ln_in_b", "ln_eps")
        norm("qrms", 3, CQ, CQ, "q_norm_g", None, "rms_eps")
        norm("kvrms", 2, CKV, CKV, "kv_norm_g", None, "rms_eps")
        norm("convln", 4, ZB[:, 8:12], ZB[:, 8:12], "conv_ln_g", "conv_ln_b", "ln_eps", ACT.Silu)
        norm("ln1", 8, R, X, "ln1_g", "ln1_b", "ln_eps")
        norm("ln2", 8, R, X, "ln2_g", "ln2_b", "ln_eps")
        norm("grms0", 4, YY[:, 8:12], YY[:, 8:12], "ssm_norm_g", None, "ln_eps")
        norm("grms1", 4, YY[:, 12:16], YY[:, 12:16], "ssm_norm_g", None, "ln_eps")
        norm("lnm0", 8, R, X, "lnm0_g", "lnm0_b", "ln_eps")
        norm("lnf0", 8, R, X, "lnf0_g", "lnf0_b", "ln_eps")
        norm("lnm1", 8, R, X, "lnm1_g", "lnm1_b", "ln_eps")
        norm("lnf1", 8, R, X, "lnf1_g", "lnf1_b", "ln_eps")

        def norm_done(name):
            return NORMS[name]["scaled"] + NORMS[name]["c"]

        block = ctx.enter_context(nc.Block())

        def m_ready(eng, t, i=None, per=0):
            eng.wait_ge(m_full, lin(i, per, t + 1))

        def a_ready(eng, t, i=None, per=0):
            eng.wait_ge(a_full, lin(i, per, t + 1))

        def m_read(eng, t, i=None, per=0):
            eng.wait_ge(m_out[t % 4], lin(i, per // 4, t // 4 + 1))

        def a_read(eng, t, i=None, per=0):
            eng.wait_ge(a_out[t % 4], lin(i, per // 4, t // 4 + 1))

        def mbank(t):
            return bank[t % 4]

        def abank(t):
            return bank[4 + t % 4]

        @block.sync
        def _(sp):
            sp.dma_start(X, x.rearrange("(c p) s -> p c s", p=P)).then_inc(loaded, 16)
            sp.dma_start(part[:, :], par).then_inc(loaded, 16)
            sp.dma_start(cstt[:, :], cst).then_inc(loaded, 16)
            sp.dma_start(KR.bitcast(I32), positions).then_inc(loaded, 16)

            def load(slab, row, i=None, per=0):
                if slab >= NS:
                    sp.wait_ge(slab_used, lin(i, per, slab - NS + 1))
                src = w_stream[row] if isinstance(row, int) else w_stream[bass.ds(row, 1)].rearrange("o p n -> p (o n)")
                sp.dma_start(ring[:, (slab % NS) * SLAB * P:(slab % NS + 1) * SLAB * P], src)\
                    .then_inc(slab_full[slab % NS], 16)

            def run(first, last, back):
                rounds = (last - first) // NS
                with sp.Fori(0, rounds) as i:
                    for slab in range(first, first + NS):
                        load(slab, i * NS + (slab - back), i, NS)
                for slab in range(first + rounds * NS, last):
                    load(slab, slab - back)

            for slab in range(NS):
                load(slab, slab)
            sp.dma_start(PLE, p.rearrange("(c p) s -> p c s", p=P)).then_inc(p_loaded, 16)
            m0 = SLAB0["moe"]
            run(NS, m0, 0)

            def expert(b, i=None, k=0):
                col = BEI[0:1, b:b + 1] if i is None else BEI[0:1, bass.ds(i * 2 + k, 1)]
                return sp.value_load(col, min_val=0, max_val=EXPERTS - 1)

            def loads(b, e, part_, at, i=None):
                for j in range(8 if part_ == "up" else 4):
                    row = e * 12 + (m0 + j + (0 if part_ == "up" else 8))
                    load(m0 + at + j, row, i, 24)

            sp.wait_ge(experts_known, 1)
            loads(0, expert(0), "up", 0)
            with sp.Fori(0, (NB - 3) // 2) as i:
                for k in (1, 2):
                    loads(k, expert(k, i, k), "up", 8 + 12 * (k - 1), i)
                    loads(k - 1, expert(k - 1, i, k - 1), "down", 16 + 12 * (k - 1), i)
            for b in (NB - 2, NB - 1):
                loads(b, expert(b), "up", 12 * b - 4)
                loads(b - 1, expert(b - 1), "down", 12 * b + 4)
            loads(NB - 1, expert(NB - 1), "down", 12 * NB - 4)
            run(SLAB0["s_in"], NSLABS, 12 * (NB - EXPERTS))
            for k in range(C8):
                sp.wait_ge(ln_done, norm_done("lnf1") - C8 + k + 1)
                sp.dma_start(out[k * P:(k + 1) * P, :], X[:, k]).then_inc(out_done, 16)
            sp.wait_ge(out_done, 16 * C8)

        @block.tensor
        def _(pe):
            st = dict(n=0, b=0, pending=False)

            def weights(width=1, i=None, per=0):
                if st["b"] == 0:
                    slab = st["n"]
                    pe.wait_ge(slab_full[slab % NS], lin(i, 16 * per // NS, 16 * (slab // NS + 1)))
                    st["pending"] = slab > 0
                at = ((st["n"] % NS) * SLAB + st["b"]) * P
                st["b"] += width
                if st["b"] == SLAB:
                    st["b"], st["n"] = 0, st["n"] + 1
                return ring[:, at:at + width * P]

            def signal(ins, final=None):
                if final is not None:
                    ins.then_inc(final, 1)
                elif st["pending"]:
                    ins.then_inc(slab_used, 1)
                    st["pending"] = False

            def tile(t, rhs, i=None, per_t=0, per_s=0):
                if t >= 4:
                    m_read(pe, t - 4, i, per_t)
                for k, r in enumerate(rhs):
                    w = weights(1, i, per_s)
                    mm = pe.matmul(mbank(t)[:, :], w, r, start=(k == 0), stop=(k == len(rhs) - 1))
                    signal(mm, m_full if k == len(rhs) - 1 else None)

            def loop(rounds, tiles, slabs, body):
                n0 = st["n"]
                with pe.Fori(0, rounds) as i:
                    body(i)
                assert st["n"] == n0 + slabs and st["b"] == 0
                st["n"] = n0 + slabs * rounds

            def stats(name, waits=()):
                n = NORMS[name]
                t = A0[name]
                for s, v in waits:
                    pe.wait_ge(s, v)
                if n["ln"]:
                    if t >= 4:
                        a_read(pe, t - 4)
                    for k in range(n["c"]):
                        mm = pe.matmul(abank(t)[:, :], ones, n["src"][:, k], start=(k == 0), stop=(k == n["c"] - 1))
                    mm.then_inc(a_full, 1)
                    t += 1
                if t >= 4:
                    a_read(pe, t - 4)
                for k in range(n["c"]):
                    pe.wait_ge(ln_squared, n["squared"] + k + 1)
                    mm = pe.matmul(abank(t)[:, :], ones, SQ[:, k], start=(k == 0), stop=(k == n["c"] - 1))
                mm.then_inc(a_full, 1)

            def attention(name):
                a = ATT[name]
                K = a["K"]

                def scores(h, i=None):
                    per = 4 * 2
                    pe.wait_ge(att_q, lin(i, 2, a["h0"] + h + 1))
                    for q in range(NT):
                        t = T0[name] + 4 * h + q
                        m_read(pe, t - 4, i, per)
                        k = a["KH"][0:K, h, 0:(q + 1) * P] if i is None else \
                            one(a["KH"][0:K, bass.ds(i * 2 + h, 1), 0:(q + 1) * P])
                        pe.matmul(mbank(t)[:, 0:(q + 1) * P], a["QB"][0:K, h % 2, q * P:(q + 1) * P], k,
                                  start=True, stop=True).then_inc(m_full, 1)

                def values(h, i=None):
                    per = 4 * 2
                    pe.wait_ge(att_prob, lin(i, 8, 4 * (a["h0"] + h + 1)))
                    t = A0[name] + 4 * h
                    for n, blocks in enumerate((((0, 0), (1, 0), (2, 0), (3, 0)), ((1, 1), (2, 1), (3, 1)),
                                                ((2, 2), (3, 2), (3, 3)))):
                        a_read(pe, t + n - 4, i, per)
                        for m, (q, k) in enumerate(blocks):
                            tr = pe.transpose(abank(t + n)[:, m * P:(m + 1) * P],
                                              a["PR"][:, 4 * (h % 2) + q, k * P:(k + 1) * P], ident)
                        tr.then_inc(a_full, 1)
                    a_read(pe, t - 1, i, per)
                    pe.wait_ge(att_v, lin(i, 2, a["h0"] + h + 1))
                    for k, at in enumerate((0, 512, 896, 1152)):
                        if k < 3:
                            a_read(pe, t + k, i, per)
                        mm = pe.matmul(abank(t + 3)[0:64, k * P:S], a["VB"][:, 4 * (h % 2) + k, :],
                                       a["PTS"][:, at:at + (NT - k) * P], start=(k == 0), stop=(k == NT - 1))
                    mm.then_inc(a_full, 1)

                scores(0)
                with pe.Fori(0, a["n"] // 2 - 1) as i:
                    scores(1, i)
                    values(0, i)
                    scores(2, i)
                    values(1, i)
                scores(a["n"] - 1)
                values(a["n"] - 2)
                values(a["n"] - 1)

            Xr = [X[:, k] for k in range(C8)]
            pe.wait_ge(loaded, 64)
            stats("ln_in")
            for n in range(19):
                if n == 0:
                    pe.wait_ge(ln_done, norm_done("ln_in"))
                tile(T0["in"] + n, Xr)
            stats("qrms")
            for n in range(8):
                if n == 0:
                    pe.wait_ge(ln_done, norm_done("qrms"))
                tile(T0["uq"] + n, [CQ[:, k] for k in range(3)])
            stats("kvrms")
            pe.wait_ge(ln_done, norm_done("kvrms"))
            for n in range(4):
                tile(T0["uk"] + n, [CKV[:, k] for k in range(2)])
            for t in range(4):
                m_read(pe, T0["uv"] + t - 4)
            for k in range(2):
                w = weights(4)
                for t in range(NT):
                    mm = pe.matmul(mbank(T0["uv"] + t)[:, :], CKV[:, k, t * P:(t + 1) * P], w,
                                   start=(k == 0), stop=(k == 1))
                    signal(mm, m_full if k == 1 else None)
            for g in range(4):
                t = A0["poolw"] + g
                pe.wait_ge(pool_mixed, g + 1)
                a_read(pe, t - 4)
                pe.matmul(abank(t)[:, :], pmat("pool_w", g, P), UP[:, g, 16:16 + S], start=True, stop=True)\
                    .then_inc(a_full, 1)
            pe.wait_ge(k_rope, HEADS1)
            for j in range(4):
                m_read(pe, T0["uv"] + j)
            attention("att")
            def branch(i, b):
                for m in range(C8):
                    t = T0["branch"] + (16 * b if i is None else 0) + 2 * m
                    tile(t, Xr, i, 16, 12)
                    z = [one(ZB[:, bass.ds(i * 4 + k, 1), :]) if i is not None else ZB[:, 4 * b + k] for k in range(4)]
                    tile(t + 1, z, i, 16, 12)

            for t in range(A0["att"] + 4 * HEADS1 - 4, A0["att"] + 4 * HEADS1):
                a_read(pe, t)
            loop(2, 32, 12, lambda i: branch(i, 0))
            stats("convln", [(merged, 1)])
            pe.wait_ge(ln_done, norm_done("convln"))
            branch(None, 2)
            pe.wait_ge(merged, 2)
            for m in range(C8):
                tile(T0["wout"] + m, [MG[:, k] for k in range(C8)])
            stats("ln1", [(resid, 1)])
            pe.wait_ge(ln_done, norm_done("ln1"))
            t = A0["route"]
            a_read(pe, t - 4)
            for q in range(NT):
                for k in range(C8):
                    mm = pe.matmul(abank(t)[:, 16 * q:16 * q + 16], X[:, k, q * P:(q + 1) * P],
                                   pmat("router", k, 16), start=(k == 0), stop=(k == C8 - 1))
            mm.then_inc(a_full, 1)
            for q in range(NT):
                for half in range(2):
                    t = A0["xtok1"] + 2 * q + half
                    a_read(pe, t - 4)
                    for j in range(4):
                        tr = pe.transpose(abank(t)[:, j * P:(j + 1) * P], X[:, 4 * half + j, q * P:(q + 1) * P], ident)
                    tr.then_inc(a_full, 1)
            for m in range(C8):
                tile(T0["pg"] + m, Xr)
                if m == 2:
                    t = A0["count"]
                    pe.wait_ge(routed, 1)
                    a_read(pe, t - 4)
                    for q in range(NT):
                        for r in range(q + 1):
                            pe.matmul(abank(t)[:, 16 * q:16 * q + 16], cm("before") if r == q else ones,
                                      KIN[:, 16 * r:16 * r + 16], start=(r == 0), stop=(r == q))
                    for r in range(NT):
                        mm = pe.matmul(abank(t)[:, 64:80], ones, KIN[:, 16 * r:16 * r + 16],
                                       start=(r == 0), stop=(r == NT - 1))
                    mm.then_inc(a_full, 1)
            pe.wait_ge(p_loaded, 16)
            for m in range(C8):
                tile(T0["pp"] + m, [PLE[:, k] for k in range(2)])

            def wide(t, lhs, i=None):
                m_read(pe, t - 4, i, 8)
                for k, w_ in enumerate(lhs):
                    w = weights(4, i, 24)
                    mm = pe.matmul(mbank(t)[:, :], w_, w, start=(k == 0), stop=(k == len(lhs) - 1))
                    signal(mm, m_full if k == len(lhs) - 1 else None)

            def x_transposes(b, i=None):
                pe.wait_ge(xg_loaded[b % 2], lin(i, 16, 16 * (b // 2 + 1)))
                for n in range(3):
                    t = xt_tile(b) + n
                    a_read(pe, t - 4, i, 8)
                    for j in range(3 * n, min(3 * n + 3, C8)):
                        tr = pe.transpose(abank(t)[:, (j - 3 * n) * P:(j - 3 * n + 1) * P],
                                          XG[:, b % 2, j * P:(j + 1) * P], ident)
                    tr.then_inc(a_full, 1)

            def act_transposes(b, i=None):
                t = actt_tile(b)
                m_read(pe, gate_tile(b) + 1, i, 8)
                a_read(pe, t - 4, i, 8)
                for j in range(4):
                    tr = pe.transpose(abank(t)[:, j * P:(j + 1) * P], ACTB[:, j * P:(j + 1) * P], ident)
                tr.then_inc(a_full, 1)

            def up(b, half, i=None):
                if half == 0:
                    for n in range(3):
                        a_read(pe, xt_tile(b) + n, i, 8)
                wide(gate_tile(b) + half, [XST[:, C8 * (b % 2) + k] for k in range(C8)], i)

            def down(b, i=None):
                a_read(pe, actt_tile(b), i, 8)
                for half in range(2):
                    wide(down_tile(b) + half, [ACTT[:, k * P:(k + 1) * P] for k in range(4)], i)

            def block_of_slots(b, i=None):
                up(b, 0, i)
                act_transposes(b - 1, i)
                if b < NB - 1:
                    x_transposes(b + 1, i)
                up(b, 1, i)
                down(b - 1, i)

            x_transposes(0)
            up(0, 0)
            x_transposes(1)
            up(0, 1)
            block_of_slots(1)
            block_of_slots(2)
            n0 = st["n"]
            with pe.Fori(0, (NB - 3) // 2 - 1) as i:
                block_of_slots(3, i)
                block_of_slots(4, i)
            assert st["n"] == n0 + 24 and st["b"] == 0
            st["n"] = n0 + 12 * (NB - 5)
            block_of_slots(NB - 2)
            block_of_slots(NB - 1)
            act_transposes(NB - 1)
            down(NB - 1)
            for k in range(C8):
                t = A0["mout"] + k
                a_read(pe, t - 4)
                pe.wait_ge(tok_sum, NT)
                for q in range(NT):
                    tr = pe.transpose(abank(t)[:, q * P:(q + 1) * P], MT[:, q, k * P:(k + 1) * P], ident)
                tr.then_inc(a_full, 1)
            stats("ln2", [(resid, 2)])
            pe.wait_ge(ln_done, norm_done("ln2"))
            t = A0["dt"]
            a_read(pe, t - 4)
            for k in range(C8):
                mm = pe.matmul(abank(t)[0:16, :], pmat("w_dt", k, 16), X[:, k], start=(k == 0), stop=(k == C8 - 1))
            mm.then_inc(a_full, 1)

            def four(base, n):
                def body(i):
                    for j in range(4):
                        tile(base + j, Xr, i, 4, 4)
                loop(n // 4, 4, 4, body)

            def twelve(i):
                for j in range(12):
                    tile(T0["s_in"] + j, Xr, i, 12, 12)
            loop(2, 12, 12, twelve)
            four(T0["s_in"] + 24, 8)
            four(T0["s_in"] + 32, 12)
            t = A0["acst"]
            pe.wait_ge(dt_ready, 1)
            a_read(pe, t - 4)
            for n, src in enumerate((ACS, DT, DTE)):
                for c in range(NT):
                    tr = pe.transpose(abank(t)[:, 64 * n + 16 * c:64 * n + 16 * c + 16],
                                      src[0:16, c * P:(c + 1) * P], ident[0:16, 0:16])
            tr.then_inc(a_full, 1)
            pe.wait_ge(xbc_done, 12)
            for g in range(2):
                t = A0["btok"] + g
                a_read(pe, t - 4)
                for c in range(NT):
                    tr = pe.transpose(abank(t)[:, c * P:(c + 1) * P], XBC[:, 8 + g, c * P:(c + 1) * P], ident)
                tr.then_inc(a_full, 1)
            for c in range(NT):
                for g in range(2):
                    t = A0["xtok"] + 2 * c + g
                    a_read(pe, t - 4)
                    for j in range(4):
                        tr = pe.transpose(abank(t)[:, j * P:(j + 1) * P], XBC[:, 4 * g + j, c * P:(c + 1) * P], ident)
                    tr.then_inc(a_full, 1)
            for g in range(2):
                t = A0["cb"] + g
                a_read(pe, t - 4)
                for c in range(NT):
                    cs = slice(c * P, (c + 1) * P)
                    mm = pe.matmul(abank(t)[:, cs], XBC[:, 8 + g, cs], XBC[:, 10 + g, cs], start=True, stop=True)
                mm.then_inc(a_full, 1)
            a_read(pe, A0["btok"])
            a_read(pe, A0["btok"] + 1)
            for c in range(NT - 1):
                for g in range(2):
                    t = A0["state"] + 2 * c + g
                    pe.wait_ge(ssd_dx, 2 * c + g + 1)
                    a_read(pe, t - 4)
                    pe.matmul(abank(t)[:, :], BT[:, g, c * P:(c + 1) * P], DX[:, 2 * c + g],
                              start=True, stop=True).then_inc(a_full, 1)

            def decays(h):
                t = head_tile(h)
                a_read(pe, t - 4)
                pe.matmul(abank(t)[:, :], SEL16[0:16, h * P:(h + 1) * P], ACS[0:16, :], start=True, stop=True)\
                    .then_inc(a_full, 1)

            pe.wait_ge(sel_loaded, 16)
            decays(0)
            decays(1)
            for c in range(NT):
                for g in range(2):
                    a_read(pe, A0["xtok"] + 2 * c + g)
            for j in range(C8):
                if j < C8 - 1:
                    decays(2 * j + 2)
                    decays(2 * j + 3)
                t = pair_tile(j)
                a_read(pe, t - 4)
                pe.wait_ge(ssd_m, 2 * j + 2)
                pe.wait_ge(ssd_e, 2 * j + 2)
                pe.wait_ge(ssd_prev, 4 * j + 4)
                for h in (2 * j, 2 * j + 1):
                    r = slice(64 * (h % 2), 64 * (h % 2) + 64)
                    f = slice((h % 8) * 64, (h % 8) * 64 + 64)
                    for c in range(NT):
                        cs = slice(c * P, (c + 1) * P)
                        mm = pe.matmul(abank(t)[r, cs], XDT[:, c, h * 64:h * 64 + 64], MB[:, h % 2, cs],
                                       start=True, stop=(c == 0))
                        if c:
                            mm = pe.matmul(abank(t)[r, cs], SQ[:, 2 * (c - 1) + h // 8, f], CSB[:, h % 2, cs],
                                           start=False, stop=True)
                mm.then_inc(a_full, 1)
            stats("grms0")
            stats("grms1")
            for t in range(T0["sout"] - 4, T0["sout"]):
                m_read(pe, t)
            pe.wait_ge(ln_done, norm_done("grms1"))
            for m in range(C8):
                tile(T0["sout"] + m, [YY[:, k] for k in range(16)])
            stats("lnm0", [(resid, 3)])

            def ffn(layer, first, last, resid_n):
                pe.wait_ge(ln_done, norm_done(first))
                four(T0[f"up{layer}"], 2 * FT)
                pe.wait_ge(ffn_g, FT * (layer + 1))
                for m in range(C8):
                    tile(T0[f"down{layer}"] + m, [G[:, k] for k in range(FT)])
                stats(last, [(resid, resid_n)])

            ffn(0, "lnm0", "lnf0", 4)
            pe.wait_ge(ln_done, norm_done("lnf0"))
            t = A0["f"]
            a_read(pe, t - 4)
            for k in range(C8):
                mm = pe.matmul(abank(t)[0:16, :], pmat("w_f", k, 16), X[:, k], start=(k == 0), stop=(k == C8 - 1))
            mm.then_inc(a_full, 1)
            four(T0["fqk"], 16)
            for half in range(2):
                for q in range(NT):
                    m_read(pe, T0["fv"] + 4 * half + q - 4)
                for k in range(C8):
                    w = weights(4)
                    for q in range(NT):
                        mm = pe.matmul(mbank(T0["fv"] + 4 * half + q)[:, :], X[:, k, q * P:(q + 1) * P], w,
                                       start=(k == 0), stop=(k == C8 - 1))
                        signal(mm, m_full if k == C8 - 1 else None)
            pe.wait_ge(f_rows, 32)
            for q in range(NT):
                m_read(pe, T0["fv"] + 4 + q)
            attention("fatt")
            for t in range(A0["fatt"] + 4 * FOX_H - 4, A0["fatt"] + 4 * FOX_H):
                a_read(pe, t)
            for m in range(C8):
                tile(T0["fout"] + m, [ATT["fatt"]["O"][:, k] for k in range(C8)])
            stats("lnm1", [(resid, 5)])
            ffn(1, "lnm1", "lnf1", 6)

        @block.scalar
        def _(act):
            step = Count(act_step)

            def norm_act(name, waits=()):
                n = NORMS[name]
                t = A0[name] + n["ln"]
                for s, v in waits:
                    act.wait_ge(s, v)
                for k in range(n["c"]):
                    if n["ln"]:
                        act.wait_ge(ln_centred, n["centred"] + k + 1)
                    act.activation(SQ[:, k], n["src"][:, k], ACT.Square).then_inc(ln_squared, 1)
                a_ready(act, t)
                act.activation(STD[:, :], abank(t)[:, :], ACT.Sqrt, bias=cm(n["eps"], 1),
                               scale=1.0 / (n["c"] * P)).then_inc(a_out[t % 4], 1)
                for k in range(n["c"]):
                    act.wait_ge(ln_scaled, n["scaled"] + k + 1)
                    b = pc(n["b"], k) if n["ln"] else cm("zero", 1)
                    gk = k + (4 if name == "grms1" else 0)
                    act.activation(n["dst"][:, k], n["src"][:, k], n["fn"], bias=b, scale=pc(n["g"], gk))\
                        .then_inc(ln_done, 1)

            def attention(name):
                a = ATT[name]

                def exps(h, i=None):
                    act.wait_ge(att_nm, lin(i, 2, a["h0"] + h + 1))
                    if h >= 2:
                        a_ready(act, A0[name] + 4 * (h - 2) + 2, i, 8)
                    elif i is not None:
                        act.wait_ge(a_full, i * 8 + (A0[name] + 4 * (h - 2) + 3))
                    for q in range(NT):
                        t = T0[name] + 4 * h + q
                        c = 8 * (h % 2) + q
                        act.activation(a["PR"][:, 4 * (h % 2) + q, 0:(q + 1) * P], mbank(t)[:, 0:(q + 1) * P], ACT.Exp,
                                       bias=stat[:, c:c + 1], scale=a["scale"],
                                       accum_out=stat[:, c + 4:c + 5]).then_inc(m_out[t % 4], 1)

                def evacuate(h, i=None):
                    t = A0[name] + 4 * h
                    a_ready(act, t, i, 8)
                    act.activation(a["PTS"][:, 0:S], abank(t)[:, :], ACT.Copy).then_inc(a_out[t % 4], 1)
                    a_ready(act, t + 3, i, 8)
                    r = slice(64 * (h % 2), 64 * (h % 2) + 64)
                    o = a["O"][r, h // 2] if i is None else one(a["O"][r, bass.ds(i + h // 2, 1), :])
                    act.activation(o, abank(t + 3)[0:64, :], ACT.Copy).then_inc(a_out[(t + 3) % 4], 1)

                exps(0)
                with act.Fori(0, a["n"] // 2 - 1) as i:
                    exps(1, i)
                    evacuate(0, i)
                    exps(2, i)
                    evacuate(1, i)
                exps(a["n"] - 1)
                evacuate(a["n"] - 2)
                evacuate(a["n"] - 1)

            act.wait_ge(loaded, 64)
            norm_act("ln_in")
            act.wait_ge(rope_q, 1)
            act.activation(SIN, RT[:, 0], ACT.Sin, bias=cm("zero", 1)).then_inc(act_step, 1)
            act.activation(COS, RT[:, 1], ACT.Sin, bias=cm("zero", 1)).then_inc(act_step, 1)
            step.n = 2
            for k in range(4):
                t = T0["in"] + 2 * k + 1
                if k >= 2:
                    act.wait_ge(conv_in, k - 1)
                m_ready(act, t)
                act.activation(MSG[:, k % 2], mbank(t)[:, :], ACT.Sigmoid).then_inc(m_out[t % 4], 1)
            for k in range(3):
                t = T0["in"] + 8 + k
                m_ready(act, t)
                act.activation(CQ[:, k], mbank(t)[:, :], ACT.Copy).then_inc(m_out[t % 4], 1)
            for k in range(2):
                t = T0["in"] + 11 + k
                m_ready(act, t)
                act.activation(CKV[:, k], mbank(t)[:, :], ACT.Copy).then_inc(m_out[t % 4], 1)
            act.wait_ge(pads_zero, 2)
            for g in range(4):
                t = T0["in"] + 15 + g
                m_ready(act, t)
                act.activation(UP[:, g, 16:16 + S], mbank(t)[:, :], ACT.Copy).then_inc(m_out[t % 4], 1)
            m_read(act, T0["in"] + 8)
            m_read(act, T0["in"] + 9)
            m_read(act, T0["in"] + 10)
            norm_act("qrms")

            def split_heads(dst, t, j):
                m_ready(act, t)
                act.activation(dst[0:64, 2 * j], mbank(t)[0:64, :], ACT.Copy).then_inc(act_step, 1)
                act.activation(dst[0:64, 2 * j + 1], mbank(t)[64:128, :], ACT.Copy).then_inc(m_out[t % 4], 1)

            for j in range(4):
                split_heads(ATT["att"]["QH"], T0["uq"] + j, j)
            m_read(act, T0["in"] + 11)
            m_read(act, T0["in"] + 12)
            norm_act("kvrms")
            for j in range(4):
                split_heads(ATT["att"]["KH"], T0["uk"] + j, j)
            for k in range(4):
                t = T0["uv"] + k
                m_ready(act, t)
                act.activation(ATT["att"]["V"][:, k], mbank(t)[:, :], ACT.Copy).then_inc(m_out[t % 4], 1)
            for g in range(4):
                t = A0["poolw"] + g
                a_ready(act, t)
                act.activation(ZB[:, g], abank(t)[:, :], ACT.Identity, bias=cm("zero", 1),
                               scale=pc("pool_scale", g)).then_inc(a_out[t % 4], 1)
            attention("att")

            def branch(i, b):
                for m in range(C8):
                    t = T0["branch"] + (16 * b if i is None else 0) + 2 * m
                    m_read(act, t + 1 - 4, i, 16)
                    m_ready(act, t, i, 16)
                    bias = pc("b_gate", 8 * b + m) if i is None else \
                        part[:, bass.ds(i * 8 + (PAR0["b_gate"] + m), 1)]
                    act.activation(MSG[:, m % 2], mbank(t)[:, :], ACT.Sigmoid, bias=bias).then_inc(m_out[t % 4], 1)

            with act.Fori(0, 2) as i:
                branch(i, 0)
            norm_act("convln")
            branch(None, 2)
            norm_act("ln1")
            t = A0["route"]
            a_ready(act, t)
            act.activation(AFF[:, 0:64], abank(t)[:, 0:64], ACT.Sigmoid).then_inc(a_out[t % 4], 1)
            for q in range(NT):
                for half in range(2):
                    t = A0["xtok1"] + 2 * q + half
                    a_ready(act, t)
                    act.activation(XTK[:, q, half * S:(half + 1) * S], abank(t)[:, :], ACT.Copy)\
                        .then_inc(a_out[t % 4], 1)
            for n in range(4, 8):
                a_read(act, A0["xtok1"] + n)
            act.dma_start(x_tok.rearrange("(q p) d -> p q d", p=P), XTK).then_inc(xtok_sent, 16)
            for m in range(C8):
                t = T0["pg"] + m
                m_ready(act, t)
                act.activation(PG[:, m], mbank(t)[:, :], ACT.Sigmoid).then_inc(m_out[t % 4], 1)

            def silu(b, i=None):
                t = gate_tile(b)
                if b or i is not None:
                    m_read(act, gate_tile(b - 1) + 1, i, 8)
                m_ready(act, t, i, 8)
                act.activation(SGB, mbank(t)[:, :], ACT.Silu).then_inc(m_out[t % 4], 1)

            def finish(b, i=None):
                t = actt_tile(b)
                a_ready(act, t, i, 8)
                act.activation(ACTT, abank(t)[:, :], ACT.Copy).then_inc(a_out[t % 4], 1)
                t = down_tile(b)
                if b >= 2 or i is not None:
                    act.wait_ge(yo_sent[b % 2], lin(i, 16, 16 * (b // 2)) if b >= 2 else i * 16)
                m_ready(act, t, i, 8)
                act.activation(YO[:, b % 2, 0:S], mbank(t)[:, :], ACT.Copy).then_inc(m_out[t % 4], 1)
                m_read(act, t, i, 8)
                m_read(act, t + 1, i, 8)
                dst = y_slots[b] if i is None else y_slots[bass.ds(i * 2 + b, 1)].rearrange("o p d -> p (o d)")
                act.dma_start(dst, YO[:, b % 2]).then_inc(yo_sent[b % 2], 16)

            silu(0)
            silu(1)
            finish(0)
            silu(2)
            finish(1)
            with act.Fori(0, (NB - 3) // 2 - 1) as i:
                silu(3, i)
                finish(2, i)
                silu(4, i)
                finish(3, i)
            for b in (NB - 2, NB - 1):
                silu(b)
                finish(b - 1)
            finish(NB - 1)
            norm_act("ln2")
            def log1p_act(b, src_tile, bias):
                t = A0[src_tile]
                a_ready(act, t)
                act.activation(b[0:16, 0], abank(t)[0:16, :], ACT.Identity, bias=pc(bias, 0, slice(0, 16)))\
                    .then_inc(a_out[t % 4], 1)
                n = 1 if src_tile == "f" else 0
                act.wait_ge(dt_ln, 2 * n + 1)
                act.activation(b[0:16, 2], b[0:16, 1], ACT.Exp, scale=-1.0).then_inc(dt_e, 1)
                act.wait_ge(dt_ln, 2 * n + 2)
                act.activation(b[0:16, 4], b[0:16, 3], ACT.Ln).then_inc(dt_e, 1)

            act.activation(stat[0:16, 50:51], pc("a_log", 0, slice(0, 16)), ACT.Exp).then_inc(a_neg, 1)
            log1p_act(DTB, "dt", "dt_bias")
            act.wait_ge(dte, 1)
            for c in range(NT):
                last = ACS[0:16, (c + 1) * P - 1:(c + 1) * P]
                ins = act.activation(DTE[0:16, c * P:(c + 1) * P], ACS[0:16, c * P:(c + 1) * P], ACT.Exp,
                                     bias=last, scale=-1.0)
            ins.then_inc(a_neg, 1)
            with act.Fori(0, 2) as i:
                for m in range(4):
                    t = T0["s_in"] + 3 * m
                    m_read(act, t - 5, i, 12)
                    m_ready(act, t, i, 12)
                    act.activation(CS[:, m % 2], mbank(t)[:, :], ACT.Copy).then_inc(m_out[t % 4], 1)
            with act.Fori(0, 2) as i:
                for m in range(4):
                    t = T0["s_in"] + 24 + m
                    m_ready(act, t, i, 4)
                    act.activation(one(ZS[:, bass.ds(i * 4 + m, 1), :]), mbank(t)[:, :], ACT.Silu)\
                        .then_inc(m_out[t % 4], 1)
            with act.Fori(0, 3) as i:
                for m in range(4):
                    t = T0["s_in"] + 32 + m
                    m_ready(act, t, i, 4)
                    act.wait_ge(xbc_conv, i * 4 + (m + 1))
                    act.activation(XP[:, m % 2, 3:3 + S], mbank(t)[:, :], ACT.Copy).then_inc(m_out[t % 4], 1)
                    act.wait_ge(xbc_conv, i * 4 + (m + 3))
                    act.activation(one(XBC[:, bass.ds(i * 4 + m, 1), :]), XA[:, m % 2], ACT.Silu,
                                   bias=part[:, bass.ds(i * 4 + (PAR0["ssm_conv_b"] + m), 1)]).then_inc(xbc_done, 1)
            t = A0["acst"]
            a_ready(act, t)
            act.activation(TK[:, 0:192], abank(t)[:, 0:192], ACT.Copy).then_inc(a_out[t % 4], 1)
            for g in range(2):
                t = A0["btok"] + g
                a_ready(act, t)
                act.activation(BT[:, g], abank(t)[:, :], ACT.Copy).then_inc(a_out[t % 4], 1)
            for g in range(2):
                t = A0["cb"] + g
                a_ready(act, t)
                act.activation(CBS[:, g], abank(t)[:, :], ACT.Copy).then_inc(a_out[t % 4], 1)
            for n in range(6):
                t = A0["state"] + n
                a_ready(act, t)
                act.activation(SQ[:, n], abank(t)[:, :], ACT.Copy).then_inc(a_out[t % 4], 1)
            for h in range(SSM_H):
                t = head_tile(h)
                if h >= 2:
                    act.wait_ge(ssd_e, h - 1)
                    act.wait_ge(ssd_prev, 2 * (h - 2) + 2)
                a_ready(act, t)
                act.activation(EB[:, h % 2], abank(t)[:, :], ACT.Exp).then_inc(ssd_u, 1)
                act.wait_ge(ssd_d, 4 * h + 4)
                act.activation(LB[:, h % 2], LB[:, h % 2], ACT.Exp).then_inc(ssd_l, 1)
            norm_act("grms0", [(sc_y, 8)])
            norm_act("grms1")
            norm_act("lnm0")

            def ffn(layer, last):
                with act.Fori(0, FT // 2) as i:
                    for k in range(4):
                        t = T0[f"up{layer}"] + k
                        m_ready(act, t, i, 4)
                        act.wait_ge(ffn_conv, i * 4 + (48 * layer + k + 1))
                        act.activation(FP[:, k, 2:2 + S], mbank(t)[:, :], ACT.Copy).then_inc(m_out[t % 4], 1)
                        if k % 2:
                            act.wait_ge(ffn_conv, i * 4 + (48 * layer + k + 5))
                            act.activation(TF[:, k], TF[:, k], ACT.Silu).then_inc(ffn_silu, 1)
                norm_act(last)

            ffn(0, "lnf0")
            log1p_act(FB, "f", "b_f")
            QK = ar(_x["QH"], 32)
            with act.Fori(0, 4) as i:
                for j in range(4):
                    t = T0["fqk"] + j
                    m_ready(act, t, i, 4)
                    for h in range(2):
                        ins = act.activation(one(QK[0:64, bass.ds(i * 8 + (2 * j + h), 1), :]),
                                             mbank(t)[64 * h:64 * h + 64, :], ACT.Copy)
                    ins.then_inc(m_out[t % 4], 1)
            for half in range(2):
                for q in range(NT):
                    t = T0["fv"] + 4 * half + q
                    m_ready(act, t)
                    act.activation(ATT["fatt"]["V"][:, q, half * S:half * S + S], mbank(t)[:, :], ACT.Copy)\
                        .then_inc(m_out[t % 4], 1)
            attention("fatt")
            norm_act("lnm1")
            ffn(1, "lnf1")

        @block.vector
        def _(dve):
            step = Count(dve_step)

            def sync():
                dve.wait_ge(dve_step, step.now())

            def norm_dve(name):
                n = NORMS[name]
                t = A0[name]
                if n["ln"]:
                    a_ready(dve, t)
                    for k in range(n["c"]):
                        ins = dve.scalar_tensor_tensor(out=n["src"][:, k], in0=abank(t)[:, :],
                                                       scalar=-1.0 / (n["c"] * P), in1=n["src"][:, k],
                                                       op0=ALU.mult, op1=ALU.add)
                        ins.then_inc(ln_centred, 1)
                    dve.wait_ge(ln_centred, n["centred"] + n["c"])
                    dve.engine_nop().then_inc(a_out[t % 4], 1)
                    t += 1
                a_read(dve, t)
                dve.reciprocal(RSTD[:, :], STD[:, :]).then_inc(ln_rstd, 1)
                dve.wait_ge(ln_rstd, n["n"] + 1)
                for k in range(n["c"]):
                    if not n["ln"]:
                        dve.wait_ge(ln_squared, n["squared"] + k + 1)
                    dve.tensor_tensor(n["src"][:, k], n["src"][:, k], RSTD[:, :], ALU.mult).then_inc(ln_scaled, 1)

            def attention(name, h_nm):
                a = ATT[name]

                def maxima(h, i=None):
                    for q in range(NT):
                        t = T0[name] + 4 * h + q
                        m_ready(dve, t, i, 8)
                        dve.tensor_tensor(mbank(t)[:, q * P:(q + 1) * P], mbank(t)[:, q * P:(q + 1) * P],
                                          a["mask"], ALU.add).then_inc(att_masked, 1)
                    for q in range(NT):
                        t = T0[name] + 4 * h + q
                        c = 8 * (h % 2) + q
                        dve.wait_ge(att_masked, lin(i, 8, 4 * (a["h0"] + h) + q + 1))
                        dve.tensor_reduce(stat[:, 16 + c:17 + c], mbank(t)[:, 0:(q + 1) * P], AX.X, ALU.max,
                                          negate=True).then_inc(att_max, 1)
                    c = 8 * (h % 2)
                    dve.wait_ge(att_max, lin(i, 8, 4 * (a["h0"] + h + 1)))
                    dve.tensor_scalar(stat[:, c:c + 4], stat[:, 16 + c:20 + c], a["scale"], None, ALU.mult)\
                        .then_inc(att_nm, 1)

                def probabilities(h, i=None):
                    c = 8 * (h % 2) + 4
                    for q in range(NT):
                        m_read(dve, T0[name] + 4 * h + q, i, 8)
                    dve.reciprocal(stat[:, 28 + c:32 + c], stat[:, c:c + 4]).then_inc(att_rs, 1)
                    dve.wait_ge(att_rs, lin(i, 2, a["h0"] + h + 1))
                    for q in range(NT):
                        pr = a["PR"][:, 4 * (h % 2) + q, 0:(q + 1) * P]
                        dve.tensor_scalar(pr, pr, stat[:, 28 + c + q:29 + c + q], None, ALU.mult).then_inc(att_prob, 1)
                    t = A0[name] + 4 * h
                    for n, (at, w) in ((1, (512, 384)), (2, (896, 384))):
                        a_ready(dve, t + n, i, 8)
                        dve.tensor_copy(a["PTS"][:, at:at + w], abank(t + n)[:, 0:w]).then_inc(a_out[(t + n) % 4], 1)

                maxima(0)
                with dve.Fori(0, a["n"] // 2 - 1) as i:
                    maxima(1, i)
                    probabilities(0, i)
                    maxima(2, i)
                    probabilities(1, i)
                maxima(a["n"] - 1)
                probabilities(a["n"] - 2)
                probabilities(a["n"] - 1)

            def res_tiles(stage, alpha, n_done):
                for m in range(C8):
                    t = T0[stage] + m
                    m_ready(dve, t)
                    dve.scalar_tensor_tensor(out=R[:, m], in0=X[:, m], scalar=alpha, in1=mbank(t)[:, :],
                                             op0=ALU.mult, op1=ALU.add).then_inc(m_out[t % 4], 1)
                for t in range(T0[stage] + 4, T0[stage] + 8):
                    m_read(dve, t)
                dve.engine_nop().then_inc(resid, 1)

            dve.wait_ge(loaded, 64)
            norm_dve("ln_in")
            A, B = KT[:, 0], KT[:, 1]
            step.inc(dve.tensor_copy(A, KR.bitcast(I32)))
            sync()
            step.inc(dve.tensor_scalar(A, A, cm("invfreq", 1), None, ALU.mult))
            sync()
            step.inc(dve.tensor_scalar(B, A, float(1.0 / TWO_PI), MAGIC, ALU.mult, ALU.add))
            sync()
            step.inc(dve.tensor_scalar(B, B, MAGIC, None, ALU.subtract))
            c1 = 6.28125
            c2 = float(np.float32(TWO_PI - c1).view(np.uint32).__and__(0xFFFFF000).view(np.float32))
            c3 = float(TWO_PI - c1 - c2)
            for c in (c1, c2, c3):
                sync()
                step.inc(dve.scalar_tensor_tensor(out=A, in0=B, scalar=-c, in1=A, op0=ALU.mult, op1=ALU.add))
            sync()
            lim = 3.1415925
            step.inc(dve.tensor_scalar(RT[:, 1], A, float(np.pi / 2), None, ALU.add))
            sync()
            step.inc(dve.tensor_scalar(B, RT[:, 1], float(np.pi), -TWO_PI, ALU.is_gt, ALU.mult))
            sync()
            step.inc(dve.tensor_tensor(RT[:, 1], RT[:, 1], B, ALU.add))
            sync()
            step.inc(dve.tensor_scalar(RT[:, 1], RT[:, 1], lim, -lim, ALU.min, ALU.max))
            step.inc(dve.tensor_scalar(A, A, lim, -lim, ALU.min, ALU.max))
            sync()
            dve.tensor_scalar(RT[:, 0], A, cm("sign", 1), None, ALU.mult).then_inc(rope_q, 1)
            dve.memset(ZP[:, :, 0:H0], 0.0).then_inc(pads_zero, 1)
            dve.memset(UP[:, :, 0:16], 0.0).then_inc(pads_zero, 1)
            for k in range(4):
                t = T0["in"] + 2 * k
                m_read(dve, t + 1)
                dve.tensor_tensor(ZP[:, k, H0:H0 + S], mbank(t)[:, :], MSG[:, k % 2], ALU.mult).then_inc(conv_in, 1)
                dve.wait_ge(conv_in, k + 1)
                dve.engine_nop().then_inc(m_out[t % 4], 1)
            dve.wait_ge(act_step, 2)
            t = T0["in"] + 13
            m_ready(dve, t)
            dve.tensor_tensor(KT[:, 0], mbank(t)[:, :], COS, ALU.mult).then_inc(m_out[t % 4], 1)
            m_ready(dve, t + 1)
            dve.tensor_tensor(KT[:, 1], mbank(t + 1)[:, :], SIN, ALU.mult).then_inc(m_out[(t + 1) % 4], 1)
            m_read(dve, t)
            m_read(dve, t + 1)
            dve.tensor_tensor(KR, KT[:, 0], KT[:, 1], ALU.add).then_inc(k_rope_in, 1)
            for g in range(4):
                m_read(dve, T0["in"] + 15 + g)
                src = UP[:, g]
                lo = 0
                for r in range(g + 1):
                    w = 1 << r
                    lo += w
                    dst = PW[:, r % 2]
                    step.inc(dve.tensor_tensor(dst[:, lo:528], src[:, lo:528], src[:, lo - w:528 - w], ALU.add))
                    sync()
                    src = dst
                step.inc(dve.tensor_scalar(PW[:, (g + 1) % 2, 16:16 + S], src[:, 16:16 + S], 1.0 / POOL_W[g], None, ALU.mult))
                sync()
                mean = PW[:, (g + 1) % 2]
                ic = cstt[:, CST0["invcnt"] + 16 * g:CST0["invcnt"] + 16 * g + 16]
                step.inc(dve.tensor_tensor(mean[:, 16:32], src[:, 16:32], ic, ALU.mult))
                sync()
                dve.tensor_tensor(UP[:, g, 16:16 + S], mean[:, 16:16 + S], UP[:, g, 16:16 + S], ALU.subtract)\
                    .then_inc(pool_mixed, 1)
                dve.wait_ge(pool_mixed, g + 1)
            norm_dve("qrms")
            QH = ATT["att"]["QH"]
            for r in range(2):
                t = T0["uq"] + 4 + 2 * r
                m_ready(dve, t)
                dve.tensor_tensor(RT[:, 0], mbank(t)[:, :], COS, ALU.mult).then_inc(m_out[t % 4], 1)
                m_ready(dve, t + 1)
                dve.tensor_tensor(RT[:, 1], mbank(t + 1)[:, :], SIN, ALU.mult).then_inc(m_out[(t + 1) % 4], 1)
                m_read(dve, t)
                m_read(dve, t + 1)
                for j in range(4):
                    q = slice(32 * j, 32 * j + 32)
                    dve.tensor_tensor(QH[64:96, 4 * r + j], RT[q, 0], RT[q, 1], ALU.add).then_inc(rope_q, 1)
                dve.wait_ge(rope_q, 4 * r + 5)
            norm_dve("kvrms")
            attention("att", 0)
            dve.memset(MG, 0.0).then_inc(dve_step, 1)
            step.n += 1
            sync()

            def merge(i, b, conv):
                acc = ZB
                for m in range(C8):
                    t = T0["branch"] + (16 * b if i is None else 0) + 2 * m
                    m_ready(dve, t + 1, i, 16)
                    m_read(dve, t, i, 16)
                    sync()
                    dve.tensor_tensor(RT[:, m % 2], mbank(t + 1)[:, :], MSG[:, m % 2], ALU.mult)\
                        .then_inc(m_out[(t + 1) % 4], 1)
                    m_read(dve, t + 1, i, 16)
                    step.inc(dve.tensor_tensor(MG[:, m], MG[:, m], RT[:, m % 2], ALU.add))
                    if conv:
                        for j in range(4 * m, min(4 * m + 4, TAPS)):
                            for c in range(2):
                                o = one(acc[:, bass.ds(i * 2 + (8 + c), 1), :])
                                z = one(ZP[:, bass.ds(i * 2 + c, 1), j:j + S])
                                w = part[:, bass.ds(i * (2 * TAPS) + (PAR0["conv_dw"] + c * TAPS + j), 1)]
                                if j == 0:
                                    bb = part[:, bass.ds(i * 2 + (PAR0["conv_b"] + c), 1)]
                                    step.inc(dve.tensor_scalar(o, z, w, bb, ALU.mult, ALU.add))
                                else:
                                    dve.wait_ge(dve_step, step.now(1))
                                    step.inc(dve.scalar_tensor_tensor(out=o, in0=z, scalar=w, in1=o,
                                                                      op0=ALU.mult, op1=ALU.add))

            with dve.Fori(0, 2) as i:
                step.enter(i, C8 + 2 * TAPS)
                merge(i, 0, True)
            step.leave(2)
            sync()
            dve.engine_nop().then_inc(merged, 1)
            norm_dve("convln")
            merge(None, 2, False)
            sync()
            dve.engine_nop().then_inc(merged, 1)
            res_tiles("wout", ALPHA1, 1)
            norm_dve("ln1")
            dve.tensor_copy(TOKI, cm("tokens", 4)).then_inc(ints, 1)
            dve.memset(ZI, 0).then_inc(ints, 1)
            a_read(dve, A0["route"])
            rb = part[:, PAR0["router_bias"]:PAR0["router_bias"] + 16]
            for q in range(NT):
                c = slice(16 * q, 16 * q + 16)
                step.inc(dve.tensor_tensor(SEL[:, c], AFF[:, c], rb, ALU.add))
            step.inc(dve.memset(CMP[:, :], 0.0))

            def order(src, n):
                s4 = src.rearrange("p (g e) -> p g e", e=4)
                c4 = CMP[:, 0:16 * n].rearrange("p (g e j) -> p g e j", e=4, j=4)
                sync()
                for j in range(4):
                    for lo, hi, op in ((0, j, ALU.is_gt), (j + 1, 4, ALU.is_ge)):
                        if hi > lo:
                            b = s4[:, :, j:j + 1].to_broadcast([P, n, hi - lo])
                            step.inc(dve.tensor_tensor(c4[:, :, lo:hi, j], b, s4[:, :, lo:hi], op))
                sync()
                step.inc(dve.tensor_reduce(RANK[:, 0:4 * n], c4, AX.X, ALU.add))
                sync()

            order(SEL[:, 0:64], 16)
            KEEP2 = DTMP
            step.inc(dve.tensor_scalar(KEEP2, RANK[:, 0:64], 2.0, None, ALU.is_lt))
            sync()
            step.inc(dve.tensor_tensor(SEL[:, 64:128], SEL[:, 0:64], KEEP2, ALU.mult))
            step.inc(dve.tensor_tensor(AFF[:, 64:128], AFF[:, 0:64], KEEP2, ALU.mult))
            sync()
            step.inc(dve.tensor_reduce(GSC[:, 0:16], SEL[:, 64:128].rearrange("p (g e) -> p g e", e=4), AX.X, ALU.add))
            order(GSC[:, 0:16], 4)
            step.inc(dve.tensor_scalar(KEEP[:, 0:16], RANK[:, 0:16], 1.0, None, ALU.is_lt))
            sync()
            k3 = KEEP[:, 0:16].rearrange("p (g o) -> p g o", o=1).to_broadcast([P, 16, 4])
            step.inc(dve.tensor_tensor(AFF[:, 0:64].rearrange("p (g e) -> p g e", e=4),
                                       AFF[:, 64:128].rearrange("p (g e) -> p g e", e=4), k3, ALU.mult))
            sync()
            step.inc(dve.tensor_reduce(GSC[:, 0:4], AFF[:, 0:64].rearrange("p (q e) -> p q e", e=16), AX.X, ALU.add))
            sync()
            step.inc(dve.reciprocal(GSC[:, 4:8], GSC[:, 0:4]))
            sync()
            for q in range(NT):
                c = slice(16 * q, 16 * q + 16)
                step.inc(dve.tensor_scalar(WTOK[:, c], AFF[:, c], GSC[:, 4 + q:5 + q], None, ALU.mult))
            dve.tensor_tensor(KIN.rearrange("p (g e) -> p g e", e=4), KEEP2.rearrange("p (g e) -> p g e", e=4), k3,
                              ALU.mult).then_inc(routed, 1)
            t = A0["count"]
            a_ready(dve, t)
            for j in range(4):
                step.inc(dve.tensor_scalar(CNT[:, 16 * j:16 * j + 16], abank(t)[:, 64:80], float(P * j), None, ALU.is_gt))
            sync()
            step.inc(dve.tensor_reduce(DTMP[:, 0:16], CNT[:, 0:64].rearrange("p (j e) -> p e j", e=16), AX.X, ALU.add))
            sync()
            step.inc(dve.tensor_tensor_scan(BEND, ones[:, 0:16], DTMP[:, 0:16], 0.0, ALU.mult, ALU.add))
            sync()
            step.inc(dve.tensor_tensor(BSTART, BEND, DTMP[:, 0:16], ALU.subtract))
            step.inc(dve.tensor_tensor(BCMP.rearrange("p (b e) -> p b e", e=16),
                                       BEND.rearrange("p (o e) -> p o e", o=1).to_broadcast([P, NB, 16]),
                                       cm("iota", NB).rearrange("p (b o) -> p b o", o=1).to_broadcast([P, NB, 16]),
                                       ALU.is_le))
            sync()
            step.inc(dve.tensor_reduce(BEXP, BCMP.rearrange("p (b e) -> p b e", e=16), AX.X, ALU.add))
            for q in range(NT):
                c = slice(16 * q, 16 * q + 16)
                ins = dve.scalar_tensor_tensor(out=DEST[:, c], in0=BSTART, scalar=float(P), in1=abank(t)[:, c],
                                               op0=ALU.mult, op1=ALU.add)
                if q < NT - 1:
                    step.inc(ins)
            ins.then_inc(a_out[t % 4], 1)
            sync()
            a_read(dve, t)
            dve.tensor_scalar(BEI, BEXP, float(EXPERTS - 1), None, ALU.min).then_inc(experts_known, 1)
            step.inc(dve.tensor_scalar(DTMP, KIN, -8192.0, 8192.0, ALU.mult, ALU.add))
            step.inc(dve.tensor_tensor(SEL[:, 64:128], DEST, KIN, ALU.mult))
            sync()
            step.inc(dve.tensor_tensor(DTMP, DTMP, DEST, ALU.add))
            sync()
            step.inc(dve.tensor_reduce(DMM[:, 0:4], DTMP.rearrange("p (q e) -> p q e", e=16), AX.X, ALU.min))
            step.inc(dve.tensor_reduce(DMM[:, 4:8], SEL[:, 64:128].rearrange("p (q e) -> p q e", e=16), AX.X, ALU.max))
            sync()
            dve.tensor_copy(DI, DMM).then_inc(slots_known, 1)
            for n in range(2):
                for q in range(NT):
                    c = slice(16 * q, 16 * q + 16)
                    step.inc(dve.scalar_tensor_tensor(out=CMP[:, 64 * n + 16 * q:64 * n + 16 * q + 16], in0=DEST[:, c],
                                                      scalar=DMM[:, 4 * n + q:4 * n + q + 1], in1=WTOK[:, c],
                                                      op0=ALU.is_equal, op1=ALU.mult))
            sync()
            step.inc(dve.tensor_reduce(DWT, CMP[:, 0:128].rearrange("p (q e) -> p q e", e=16), AX.X, ALU.add))
            for m in range(C8):
                t = T0["pp"] + m
                m_read(dve, T0["pg"] + m)
                m_ready(dve, t)
                dve.tensor_tensor(PG[:, m], PG[:, m], mbank(t)[:, :], ALU.mult).then_inc(m_out[t % 4], 1)
                m_read(dve, t)
                step.inc(dve.scalar_tensor_tensor(out=R[:, m], in0=X[:, m], scalar=ALPHA1, in1=PG[:, m],
                                                  op0=ALU.mult, op1=ALU.add))

            def x_evacuate(b, i=None):
                for n in range(3):
                    t = xt_tile(b) + n
                    a_ready(dve, t, i, 8)
                    w = min(3, C8 - 3 * n)
                    at = C8 * (b % 2) + 3 * n
                    dve.tensor_copy(XST[:, at:at + w], abank(t)[:, 0:w * P].rearrange("p (k s) -> p k s", s=P))\
                        .then_inc(a_out[t % 4], 1)

            def product(b, i=None):
                t = gate_tile(b) + 1
                m_read(dve, t - 1, i, 8)
                m_ready(dve, t, i, 8)
                if b or i is not None:
                    a_ready(dve, actt_tile(b - 1), i, 8)
                dve.tensor_tensor(ACTB, mbank(t)[:, :], SGB, ALU.mult).then_inc(m_out[t % 4], 1)

            def half_out(b, i=None):
                t = down_tile(b) + 1
                if b >= 2:
                    dve.wait_ge(yo_sent[b % 2], lin(i, 16, 16 * (b // 2)))
                m_ready(dve, t, i, 8)
                dve.tensor_copy(YO[:, b % 2, S:D], mbank(t)[:, :]).then_inc(m_out[t % 4], 1)

            def block_of_slots(b, i=None):
                if b < NB - 1:
                    x_evacuate(b + 1, i)
                product(b, i)
                half_out(b - 1, i)

            x_evacuate(0)
            x_evacuate(1)
            product(0)
            block_of_slots(1)
            block_of_slots(2)
            with dve.Fori(0, (NB - 3) // 2 - 1) as i:
                block_of_slots(3, i)
                block_of_slots(4, i)
            block_of_slots(NB - 2)
            block_of_slots(NB - 1)
            half_out(NB - 1)
            for q in range(NT):
                for n in range(2):
                    g = (2 * q + n) % 4
                    dve.wait_ge(yg_loaded[g], 16 * ((2 * q + n) // 4 + 1))
                    w = DWT[:, 4 * n + q:4 * n + q + 1]
                    if n == 0:
                        step.inc(dve.tensor_scalar(MT[:, q], YG[:, g], w, None, ALU.mult))
                    else:
                        sync()
                        dve.scalar_tensor_tensor(out=MT[:, q], in0=YG[:, g], scalar=w, in1=MT[:, q],
                                                 op0=ALU.mult, op1=ALU.add).then_inc(tok_sum, 1)
            for k in range(C8):
                t = A0["mout"] + k
                a_ready(dve, t)
                dve.tensor_tensor(R[:, k], R[:, k], abank(t)[:, :], ALU.add).then_inc(a_out[t % 4], 1)
            for k in range(4, 8):
                a_read(dve, A0["mout"] + k)
            dve.engine_nop().then_inc(resid, 1)
            norm_dve("ln2")
            def log1p_dve(b, n):
                x_, ab, e, u, ln, o = (b[0:16, k] for k in range(6))
                a_read(dve, A0["f" if n else "dt"])
                step.inc(dve.tensor_scalar(ab, x_, -1.0, None, ALU.mult))
                sync()
                dve.tensor_tensor(ab, ab, x_, ALU.max).then_inc(dt_ln, 1)
                dve.wait_ge(dt_e, 2 * n + 1)
                dve.tensor_scalar(u, e, 1.0, None, ALU.add).then_inc(dt_ln, 1)
                dve.wait_ge(dt_ln, 2 * n + 2)
                step.inc(dve.tensor_scalar(o, u, -1.0, None, ALU.add))
                sync()
                step.inc(dve.tensor_tensor(o, e, o, ALU.subtract))
                step.inc(dve.reciprocal(ab, u))
                sync()
                step.inc(dve.tensor_tensor(o, o, ab, ALU.mult))
                sync()
                dve.wait_ge(dt_e, 2 * n + 2)
                step.inc(dve.tensor_tensor(o, o, ln, ALU.add))
                sync()

            x_, ab, e, u, ln, o = (DTB[0:16, k] for k in range(6))
            log1p_dve(DTB, 0)
            step.inc(dve.tensor_scalar(x_, x_, 0.0, None, ALU.max))
            sync()
            step.inc(dve.tensor_tensor(DT[0:16, :], x_, o, ALU.add))
            sync()
            dve.wait_ge(a_neg, 1)
            step.inc(dve.tensor_scalar(ab, DT[0:16, :], stat[0:16, 50:51], -1.0, ALU.mult, ALU.mult))
            sync()
            for c in range(NT):
                cs = slice(c * P, (c + 1) * P)
                ins = dve.tensor_tensor_scan(ACS[0:16, cs], ones[0:16, :], ab[:, cs], 0.0, ALU.mult, ALU.add)
            ins.then_inc(dte, 1)
            step.inc(dve.memset(CHP[:, :, 0:2], 0.0))
            for m in range(2):
                dve.memset(XP[:, m, 0:3], 0.0).then_inc(xbc_conv, 1)
            sync()
            dve.wait_ge(a_neg, 2)
            dve.tensor_tensor(DTE[0:16, :], DTE[0:16, :], DT[0:16, :], ALU.mult).then_inc(dt_ready, 1)

            with dve.Fori(0, 2) as i:
                step.enter(i, 4 * 3)
                for m in range(4):
                    t = T0["s_in"] + 3 * m
                    m_read(dve, t, i, 12)
                    m_ready(dve, t + 1, i, 12)
                    dve.tensor_tensor(CHP[:, m % 2, 2:2 + S], mbank(t + 1)[:, :], CS[:, m % 2], ALU.mult)\
                        .then_inc(m_out[(t + 1) % 4], 1)
                    m_read(dve, t + 1, i, 12)
                    if m == 0:
                        sync()

                    def w(j):
                        return part[:, bass.ds(i * 12 + (PAR0["sc_conv"] + 3 * m + j), 1)]
                    step.inc(dve.tensor_scalar(CT[:, m % 2], CHP[:, m % 2, 2:2 + S], w(2), None, ALU.mult))
                    for j in (1, 0):
                        sync()
                        step.inc(dve.scalar_tensor_tensor(out=CT[:, m % 2], in0=CHP[:, m % 2, j:j + S], scalar=w(j),
                                                          in1=CT[:, m % 2], op0=ALU.mult, op1=ALU.add))
                    sync()
                    m_ready(dve, t + 2, i, 12)
                    dve.tensor_tensor(one(YY[:, bass.ds(i * 4 + m, 1), :]), mbank(t + 2)[:, :], CT[:, m % 2],
                                      ALU.mult).then_inc(m_out[(t + 2) % 4], 1)
                    m_read(dve, t + 2, i, 12)
            step.leave(2)
            with dve.Fori(0, 3) as i:
                step.enter(i, 4 * 3)
                for m in range(4):
                    t = T0["s_in"] + 32 + m
                    m_read(dve, t, i, 4)

                    def w(j):
                        return part[:, bass.ds(i * 16 + (PAR0["ssm_conv"] + 4 * m + j), 1)]
                    step.inc(dve.tensor_scalar(XA[:, m % 2], XP[:, m % 2, 3:3 + S], w(3), None, ALU.mult))
                    for j in (2, 1, 0):
                        sync()
                        ins = dve.scalar_tensor_tensor(out=XA[:, m % 2], in0=XP[:, m % 2, j:j + S], scalar=w(j),
                                                       in1=XA[:, m % 2], op0=ALU.mult, op1=ALU.add)
                        if j:
                            step.inc(ins)
                        else:
                            ins.then_inc(xbc_conv, 1)
            step.leave(3)
            a_read(dve, A0["acst"])
            for c in range(NT):
                for g in range(2):
                    t = A0["xtok"] + 2 * c + g
                    a_ready(dve, t)
                    src = abank(t)[:, :].rearrange("p (h f) -> p h f", f=64)

                    def by_head(n):
                        a = 64 * n + 16 * c + 8 * g
                        return TK[:, a:a + 8].rearrange("p (h o) -> p h o", o=1).to_broadcast([P, 8, 64])
                    if c < NT - 1:
                        dve.tensor_tensor(DX[:, 2 * c + g].rearrange("p (h f) -> p h f", f=64), src, by_head(2),
                                          ALU.mult).then_inc(ssd_dx, 1)
                    dve.tensor_tensor(XDT[:, c, g * 512:g * 512 + 512].rearrange("p (h f) -> p h f", f=64), src,
                                      by_head(1), ALU.mult).then_inc(a_out[t % 4], 1)
            a_read(dve, A0["cb"])
            a_read(dve, A0["cb"] + 1)
            for n in range(6):
                a_read(dve, A0["state"] + n)

            def finish_pair(j):
                t = pair_tile(j)
                a_ready(dve, t)
                dve.scalar_tensor_tensor(out=YY[:, 8 + j], in0=XBC[:, j], scalar=pc("ssm_d", j), in1=abank(t)[:, :],
                                         op0=ALU.mult, op1=ALU.add).then_inc(a_out[t % 4], 1)
                a_read(dve, t)
                dve.tensor_tensor(YY[:, 8 + j], YY[:, 8 + j], ZS[:, j], ALU.mult).then_inc(sc_y, 1)

            for j in range(C8):
                for h in (2 * j, 2 * j + 1):
                    t = head_tile(h)
                    dve.wait_ge(ssd_u, h + 1)
                    for c in range(NT):
                        cs = slice(c * P, (c + 1) * P)
                        if h >= 2 and c == 0:
                            dve.wait_ge(ssd_m, h - 1)
                        dve.scalar_tensor_tensor(out=LB[:, h % 2, cs], in0=abank(t)[:, cs],
                                                 scalar=TK[:, 16 * c + h:16 * c + h + 1], in1=cm("mask_ssd"),
                                                 op0=ALU.subtract, op1=ALU.add).then_inc(ssd_d, 1)
                    dve.wait_ge(ssd_d, 4 * h + 4)
                    dve.engine_nop().then_inc(a_out[t % 4], 1)
                if j:
                    finish_pair(j - 1)
                for h in (2 * j, 2 * j + 1):
                    g = h // 8
                    dve.wait_ge(ssd_l, h + 1)
                    dve.tensor_tensor(MB[:, h % 2], LB[:, h % 2], CBS[:, g], ALU.mult).then_inc(ssd_m, 1)
                    f = slice((h % 8) * 64, (h % 8) * 64 + 64)
                    for c in (1, 2):
                        dve.scalar_tensor_tensor(out=SQ[:, 2 * c + g, f], in0=SQ[:, 2 * (c - 1) + g, f],
                                                 scalar=EB[:, h % 2, (c + 1) * P - 1:(c + 1) * P],
                                                 in1=SQ[:, 2 * c + g, f], op0=ALU.mult, op1=ALU.add)\
                            .then_inc(ssd_prev, 1)
                        dve.wait_ge(ssd_prev, 2 * h + c)
            finish_pair(C8 - 1)
            norm_dve("grms0")
            norm_dve("grms1")
            res_tiles("sout", ALPHA2, 1)
            norm_dve("lnm0")

            def ffn(layer, last):
                for k in range(4):
                    dve.memset(FP[:, k, 0:2], 0.0).then_inc(ffn_conv, 1)
                dve.wait_ge(ffn_conv, 48 * layer + 4)
                with dve.Fori(0, FT // 2) as i:
                    step.enter(i, 8)

                    def conv(k):
                        t = T0[f"up{layer}"] + k
                        m_read(dve, t, i, 4)
                        c = k // 2 + (FT if k % 2 else 0)

                        def w(j):
                            return part[:, bass.ds(i * 6 + (PAR0[f"ffn_conv{layer}"] + 3 * c + j), 1)]
                        b = part[:, bass.ds(i * 2 + (PAR0[f"ffn_b{layer}"] + c), 1)]
                        step.inc(dve.tensor_scalar(TF[:, k], FP[:, k, 2:2 + S], w(2), b, ALU.mult, ALU.add))
                        sync()
                        step.inc(dve.scalar_tensor_tensor(out=TF[:, k], in0=FP[:, k, 1:1 + S], scalar=w(1),
                                                          in1=TF[:, k], op0=ALU.mult, op1=ALU.add))
                        sync()
                        dve.scalar_tensor_tensor(out=TF[:, k], in0=FP[:, k, 0:S], scalar=w(0), in1=TF[:, k],
                                                 op0=ALU.mult, op1=ALU.add).then_inc(ffn_conv, 1)

                    def gate(r):
                        dve.wait_ge(ffn_silu, i * 2 + (FT * layer + r + 1))
                        dve.tensor_tensor(one(G[:, bass.ds(i * 2 + r, 1), :]), TF[:, 2 * r], TF[:, 2 * r + 1],
                                          ALU.mult).then_inc(ffn_g, 1)
                        dve.wait_ge(ffn_g, i * 2 + (FT * layer + r + 1))

                    conv(0)
                    conv(1)
                    conv(2)
                    gate(0)
                    conv(3)
                    gate(1)
                step.leave(FT // 2)
                res_tiles(f"down{layer}", ALPHA2, 1)
                norm_dve(last)

            ffn(0, "lnf0")
            dve.memset(ar(_x["QH"], 32)[64:66], 1.0).then_inc(f_ones, 1)
            log1p_dve(FB, 1)
            x_, ab, o = FB[0:16, 0], FB[0:16, 1], FB[0:16, 5]
            step.inc(dve.tensor_scalar(x_, x_, 0.0, None, ALU.min))
            sync()
            step.inc(dve.tensor_tensor(x_, x_, o, ALU.subtract))
            sync()
            for c in range(NT):
                cs = slice(c * P, (c + 1) * P)
                init = ab[:, c * P - 1:c * P] if c else 0.0
                step.inc(dve.tensor_tensor_scan(ab[:, cs], ones[0:16, :], x_[:, cs], init, ALU.mult, ALU.add))
                sync()
            dve.tensor_scalar(F8[0:16, 0], ab, 8.0, None, ALU.mult).then_inc(f_cum, 1)
            dve.tensor_scalar(F8[0:16, 1], ab, -8.0, None, ALU.mult).then_inc(f_cum, 1)
            attention("fatt", 0)
            res_tiles("fout", ALPHA2, 1)
            norm_dve("lnm1")
            ffn(1, "lnf1")

        @block.gpsimd
        def _(pool):
            def attention(name):
                a = ATT[name]

                def copies(h, i=None):
                    if h >= 2 or i is not None:
                        pool.wait_ge(m_full, lin(i, 8, T0[name] + 4 * (h - 2) + 4))
                    q = a["QH"][0:a["K"], h] if i is None else one(a["QH"][0:a["K"], bass.ds(i * 2 + h, 1), :])
                    pool.tensor_copy(a["QB"][0:a["K"], h % 2], q).then_inc(att_q, 1)
                    pool.wait_ge(att_q, lin(i, 2, a["h0"] + h + 1))
                    if h >= 2 or i is not None:
                        pool.wait_ge(a_full, lin(i, 8, A0[name] + 4 * (h - 2) + 4))
                    at = h * 64 if i is None else None
                    v = a["V"][:, :, at:at + 64] if i is None else a["V"][:, :, bass.ds(i * 128 + h * 64, 64)]
                    pool.tensor_copy(a["VB"][:, 4 * (h % 2):4 * (h % 2) + 4, :], v).then_inc(att_v, 1)
                    pool.wait_ge(att_v, lin(i, 2, a["h0"] + h + 1))

                for h in range(2):
                    copies(h)
                with pool.Fori(0, a["n"] // 2 - 1) as i:
                    copies(2, i)
                    copies(3, i)

            pool.wait_ge(k_rope_in, 1)
            for h in range(HEADS1):
                pool.tensor_copy(ATT["att"]["KH"][64:96, h], KR[64:96, :]).then_inc(k_rope, 1)
                pool.wait_ge(k_rope, h + 1)
            pool.wait_ge(rope_q, 9)
            for j in range(4):
                m_read(pool, T0["uv"] + j)
            attention("att")
            pool.wait_ge(ints, 2)
            pool.dma_start(slot_tok.rearrange("(p b) o -> p (b o)", p=P), ZI).then_inc(table_zero, 16)
            pool.wait_ge(table_zero, 16)
            pool.wait_ge(slots_known, 1)
            for n in range(2 * NT):
                pool.indirect_dma_start(slot_tok, bass.IndirectOffsetOnAxis(ap=DI[:, n:n + 1], axis=0),
                                        TOKI[:, n % NT:n % NT + 1], None).then_inc(table_set, 16)
            pool.wait_ge(table_set, 16 * 2 * NT)
            pool.dma_start(IDX, slot_tok.rearrange("(b p) o -> p (b o)", p=P), allow_slow_non_contiguous=True)\
                .then_inc(table_read, 16)
            pool.wait_ge(table_read, 16)
            pool.wait_ge(xtok_sent, 16)

            for b in range(NB):
                if b >= 2:
                    a_ready(pool, xt_tile(b - 2) + 2)
                pool.indirect_dma_start(XG[:, b % 2], None, x_tok,
                                        bass.IndirectOffsetOnAxis(ap=IDX[:, b:b + 1], axis=0))\
                    .then_inc(xg_loaded[b % 2], 16)
            for n in range(2):
                pool.wait_ge(yo_sent[n], 16 * ((NB + 1 - n) // 2))
            for q in range(NT):
                for n in range(2):
                    g = (2 * q + n) % 4
                    if q >= 2:
                        pool.wait_ge(tok_sum, q - 1)
                    pool.indirect_dma_start(YG[:, g], None, y_slots.rearrange("b p d -> (b p) d"),
                                            bass.IndirectOffsetOnAxis(ap=DI[:, 4 * n + q:4 * n + q + 1], axis=0))\
                        .then_inc(yg_loaded[g], 16)
            pool.wait_ge(a_full, A0["ln2"])
            pool.dma_start(SEL16[0:16, :], sel16).then_inc(sel_loaded, 16)
            pool.wait_ge(xbc_done, 12)
            for h in range(SSM_H):
                pool.wait_ge(ssd_u, h + 1)
                if h >= 2:
                    a_ready(pool, pair_tile(h // 2 - 1))
                pool.tensor_tensor(CSB[:, h % 2], EB[:, h % 2], XBC[:, 10 + h // 8], ALU.mult).then_inc(ssd_e, 1)
                pool.wait_ge(ssd_e, h + 1)
            pool.wait_ge(f_ones, 1)
            pool.wait_ge(f_cum, 2)
            pool.dma_start(ATT["fatt"]["QH"][65:66], F8[0:16, 0]).then_inc(f_rows, 16)
            pool.dma_start(ATT["fatt"]["KH"][64:65], F8[0:16, 1]).then_inc(f_rows, 16)
            for q in range(NT):
                m_read(pool, T0["fv"] + 4 + q)
            pool.wait_ge(f_rows, 32)
            attention("fatt")


def _blocks(w, cols):
    k = w.shape[0] // P
    return [w[i * P:(i + 1) * P, c:c + P] for c in cols for i in range(k)]


def _tiles(w, a=0, b=None):
    return _blocks(w, range(a, w.shape[1] if b is None else b, P))


def _wide(w, width):
    k = w.shape[0] // P
    return [w[i * P:(i + 1) * P, c + j:c + j + P]
            for c in range(0, w.shape[1], width) for i in range(k) for j in range(0, width, P)]


def _stream(a):
    w_in = a["w_in"][0]
    off = np.cumsum([0, 512, 512, 512, QL, KVL, ROPE])
    kr = w_in[:, off[5]:off[6]]
    krs = np.concatenate([kr[:, 16:], kr[:, :16]], 1)
    b = []
    for j in range(4):
        b += _blocks(w_in, [off[1] + j * P]) + _blocks(w_in, [off[2] + j * P])
    b += _tiles(w_in, off[3], off[5])
    b += _tiles(np.concatenate([kr] * 4, 1)) + _tiles(np.concatenate([krs] * 4, 1))
    b += _tiles(w_in, 0, 512)
    uq = a["w_uq"][0].reshape(QL, HEADS1, NOPE + ROPE)
    b += _tiles(uq[:, :, :NOPE].reshape(QL, -1))
    for r in range(2):
        rope = uq[:, 4 * r:4 * r + 4, NOPE:]
        b += _tiles(rope.reshape(QL, -1)) + _tiles(np.concatenate([rope[..., 16:], rope[..., :16]], -1).reshape(QL, -1))
    ukv = a["w_ukv"][0].reshape(KVL, HEADS1, NOPE + VH)
    b += _tiles(ukv[:, :, :NOPE].reshape(KVL, -1)) + _wide(ukv[:, :, NOPE:].reshape(KVL, -1), 512)
    for g, name in ((0, "pool_proj"), (2, "mla_proj"), (1, "conv_proj")):
        for m in range(C8):
            b += _blocks(w_in, [off[6] + g * D + m * P]) + _blocks(a[name][0], [m * P])
    b += _tiles(a["w_out"][0]) + _tiles(a["ple_gate"][0]) + _tiles(a["ple_proj"][0])
    for e in range(EXPERTS):
        b += _wide(a["exp_w_up"][0, e], FE) + _wide(a["exp_w_down"][0, e], 512)
    s = a["sc_ssm_w_in_2"][0]
    for m in range(C8):
        b += _blocks(s, [D + m * P, 2 * D + m * P, m * P])
    b += _tiles(s, 3 * D, 4 * D + 1536)
    b += _tiles(a["sc_ssm_w_out_2"][0])

    def ffn(i):
        up = a["ffn_w_up_2"][i]
        r = []
        for m in range(FT):
            r += _blocks(up, [m * P, FF + m * P])
        return r + _tiles(a["ffn_w_down_2"][i])

    b += ffn(0)
    fox = a["fox_w_in_2"][0]
    b += _tiles(fox, 0, 2 * D) + _wide(fox[:, 2 * D:3 * D], 512) + _tiles(a["fox_w_out_2"][0])
    b += ffn(1)
    rows = NSLABS - 12 * (NB - EXPERTS)
    assert len(b) == rows * SLAB, (len(b), rows * SLAB)
    out = np.empty((rows, P, SLAB, P), np.float32)
    for n, x in enumerate(b):
        out[n // SLAB, :, n % SLAB] = x
    return out.reshape(rows, P, SLAB * P)


def _params(a):
    part = np.zeros((P, NPAR), np.float32)

    def put(name, v):
        part[:v.shape[0], PAR0[name]:PAR0[name] + v.shape[1]] = v

    def col(v):
        return v.reshape(-1, P).T

    def taps(w):
        return w.T.reshape(w.shape[1] // P, P, w.shape[0]).transpose(1, 0, 2).reshape(P, -1)

    for name, key in (("ln_in_g", "ln_in_g"), ("ln_in_b", "ln_in_b")):
        put(name, col(a[key]))
    put("b_gate", col(a["b_gate"][0][[0, 2, 1]].reshape(-1)))
    for name, key in (("pool_scale", "pool_scale"), ("conv_b", "conv_b"), ("conv_ln_g", "conv_ln_g"),
                      ("conv_ln_b", "conv_ln_b"), ("q_norm_g", "q_norm_g"), ("kv_norm_g", "kv_norm_g"),
                      ("ln1_g", "ln1_g"), ("ln1_b", "ln1_b"), ("ln2_g", "ln2_g"), ("ln2_b", "ln2_b"),
                      ("ssm_conv_b", "ssm_conv_b_2"), ("ssm_norm_g", "ssm_norm_g_2")):
        put(name, col(a[key][0]))
    put("conv_dw", taps(a["conv_dw"][0]))
    put("sc_conv", taps(a["sc_conv_w_2"][0]))
    put("ssm_conv", taps(a["ssm_conv_w_2"][0]))
    put("ssm_d", col(np.repeat(a["ssm_d_2"][0], SSM_P)))
    for i in range(2):
        put(f"ffn_conv{i}", taps(a["ffn_conv_w_2"][i]))
        put(f"ffn_b{i}", col(a["ffn_conv_b_2"][i]))
        for k, key in (("lnm", "ln_mix"), ("lnf", "ln_ffn")):
            put(f"{k}{i}_g", col(a[f"{key}_g_2"][i]))
            put(f"{k}{i}_b", col(a[f"{key}_b_2"][i]))
    put("dt_bias", a["ssm_dt_bias_2"][0][:, None])
    put("a_log", a["ssm_a_log_2"][0][:, None])
    put("b_f", a["fox_b_f_2"][0][:, None])
    put("router_bias", np.broadcast_to(a["router_bias"], (P, EXPERTS)))

    def rows(w):
        return w.reshape(-1, P, w.shape[1]).transpose(1, 0, 2).reshape(P, -1)

    put("router", rows(a["w_router"]))
    put("w_dt", rows(a["sc_ssm_w_in_2"][0][:, 4 * D + 1536:]))
    put("w_f", rows(a["fox_w_in_2"][0][:, 3 * D:]))
    put("pool_w", a["pool_w"][0].transpose(1, 0, 2).reshape(P, -1))
    return part


def _constants():
    c = np.zeros((P, NCST), np.float32)
    q, k = np.meshgrid(np.arange(P), np.arange(P), indexing="ij")

    def put(name, v):
        c[:, CST0[name]:CST0[name] + v.shape[1]] = v

    put("ident", np.eye(P))
    put("ones", np.ones((P, P)))
    put("mask_fox", np.where(k <= q, 0, NEG))
    put("mask_mla", np.where(k // 64 <= q // 64, 0, NEG))
    put("mask_ssd", np.where(q <= k, 0, NEG))
    put("invcnt", np.broadcast_to(np.concatenate([1.0 / np.minimum(np.arange(16) + 1, w) for w in POOL_W]), (P, 64)))
    put("before", np.where(q < k, 1.0, 0.0))
    put("iota", np.broadcast_to(np.arange(NB), (P, NB)))
    put("tokens", np.arange(P)[:, None] + P * np.arange(NT)[None, :])
    j = np.arange(P) % 16
    put("invfreq", (np.float32(10000.0) ** (-(2 * j).astype(np.float32) / np.float32(ROPE)))[:, None])
    put("sign", np.where(np.arange(P) % 32 < 16, -1.0, 1.0)[:, None])
    for name, v in (("ln_eps", 1e-5), ("rms_eps", 1e-6), ("zero", 0.0), ("one", 1.0), ("halfpi", np.pi / 2)):
        put(name, np.full((P, 1), v))
    sel = np.zeros((16, 16, P), np.float32)
    sel[np.arange(16), np.arange(16)] = 1.0
    return c, sel.reshape(16, -1)


def kernel(**inputs):
    from concourse import bacc
    from concourse.bass_utils import run_bass_kernel_spmd

    a = {k: np.asarray(v) for k, v in inputs.items()}
    cst, sel = _constants()
    arrays = {
        "w_stream": _stream(a),
        "x_t": np.ascontiguousarray(a["x"][0].T),
        "p_t": np.ascontiguousarray(a["p"][0, 0].T),
        "positions": np.ascontiguousarray(np.broadcast_to(a["positions"][0], (P, S))),
        "params": _params(a),
        "constants": cst,
        "sel16": sel,
    }
    nc = bacc.Bacc("TRN2", target_bir_lowering=False, num_devices=1)
    aps = [nc.dram_tensor(k, v.shape, mybir.dt.from_np(v.dtype), kind="ExternalInput").ap() for k, v in arrays.items()]
    x_tok = nc.dram_tensor("x_tok", (S, D), F32, kind="Internal").ap()
    slot_tok = nc.dram_tensor("slot_tok", (NB * P, 1), I32, kind="Internal").ap()
    y_slots = nc.dram_tensor("y_slots", (NB, P, D), F32, kind="Internal").ap()
    out = nc.dram_tensor("out_t", (D, S), F32, kind="ExternalOutput").ap()
    build(nc, *aps, x_tok, slot_tok, y_slots, out)
    r = run_bass_kernel_spmd(nc, [arrays], core_ids=[0])
    return np.ascontiguousarray(np.asarray(r.results[0]["out_t"]).T)[None]
```

```python
from contextlib import ExitStack

import numpy as np

import concourse.bass as bass
from concourse import mybir

F32 = mybir.dt.float32
I32 = mybir.dt.int32
ALU = mybir.AluOpType
ACT = mybir.ActivationFunctionType
AX = mybir.AxisListType

P = 128
S = 512
D = 1024
C8 = D // P
NT = S // P
NS = 4
SLAB = 8

POOL_W = (2, 4, 8, 16)
TAPS = 31
HEADS1, NOPE, ROPE, VH = 8, 64, 32, 64
QL, KVL = 384, 256
EXPERTS, FE, TOPK = 16, 512, 2
NEEDED = EXPERTS + (TOPK * S - EXPERTS) // P
NB = (NEEDED + 1) // 2 * 2 + 2
MORE_ROUNDS = (NB - 4) // 2
LEAST = (TOPK * S // P + 1) // 2 * 2
ALPHA1 = 2.0 ** 0.25
ALPHA2 = 4.0 ** 0.25
SSM_H, SSM_P, SSM_N = 16, 64, 128
FOX_H = 16
FF = 2816
FT = FF // P
NEG = -1e30
TWO_PI = 2.0 * np.pi
MAGIC = 1.5 * 2.0 ** 23

STAGES = [("in", 19, 19), ("uq", 3, 8), ("uk", 1, 4), ("uv", 1, 4), ("att", 0, 4 * HEADS1),
          ("branch", 36, 48), ("wout", 8, 8), ("pg", 8, 8), ("moe", 12 * NB, 4 * NB), ("pp", 2, 8),
          ("s_in", 44, 44), ("sout", 16, 8), ("up0", 44, 44), ("down0", 22, 8), ("fqk", 16, 16), ("fv", 8, 8),
          ("fatt", 0, 4 * FOX_H), ("fout", 8, 8), ("up1", 44, 44), ("down1", 22, 8)]
AUX = [("ln_in", 2), ("qrms", 1), ("kvrms", 1), ("poolw", 4), ("att", 4 * HEADS1), ("convln", 2), ("ln1", 2),
       ("route", 1), ("xtok1", 8), ("count", 1), ("moe", 4 * NB + 3), ("mout", 8), ("ln2", 2),
       ("dt", 1), ("acst", 1), ("btok", 2), ("xtok", 8), ("cb", 2),
       ("state", 6), ("head", 24), ("grms0", 1), ("grms1", 1), ("lnm0", 2), ("lnf0", 2), ("f", 1),
       ("fatt", 4 * FOX_H), ("lnm1", 2), ("lnf1", 2)]


def starts(rows, k):
    out, at = {}, 0
    for row in rows:
        out[row[0]] = at
        at += row[k]
    return out, at


SLAB0, NSLABS = starts(STAGES, 1)
T0, _ = starts(STAGES, 2)
A0, _ = starts(AUX, 1)

PAR = [("ln_in_g", 8), ("ln_in_b", 8), ("b_gate", 24), ("pool_scale", 4), ("conv_dw", 4 * TAPS), ("conv_b", 4),
       ("conv_ln_g", 4), ("conv_ln_b", 4), ("q_norm_g", 3), ("kv_norm_g", 2), ("ln1_g", 8), ("ln1_b", 8),
       ("ln2_g", 8), ("ln2_b", 8), ("sc_conv", 24), ("ssm_conv", 48), ("ssm_conv_b", 12), ("ssm_d", 8),
       ("ssm_norm_g", 8), ("ffn_conv0", 132), ("ffn_conv1", 132), ("ffn_b0", 44), ("ffn_b1", 44),
       ("lnm0_g", 8), ("lnm0_b", 8), ("lnm1_g", 8), ("lnm1_b", 8), ("lnf0_g", 8), ("lnf0_b", 8),
       ("lnf1_g", 8), ("lnf1_b", 8), ("dt_bias", 1), ("a_log", 1), ("b_f", 1), ("router_bias", 16),
       ("router", 128), ("w_dt", 128), ("w_f", 128), ("pool_w", 512)]
PAR0, NPAR = starts(PAR, 1)
CST = [("ident", 128), ("ones", 128), ("mask_fox", 128), ("mask_mla", 128), ("mask_ssd", 128), ("invcnt", 64),
       ("before", 128), ("iota", NB), ("tokens", 4),
       ("invfreq", 1), ("sign", 1), ("ln_eps", 1), ("rms_eps", 1), ("zero", 1), ("one", 1), ("halfpi", 1)]
CST0, NCST = starts(CST, 1)

MIX = dict(ZB=0, ZP=6144, UP=8320, PW=10432, CQ=11488, CKV=13024, KT=14048, KR=15072, COS=15584,
           SIN=16096, QH=16608, KH=20704, V=24800, RT=26848, QB=27872, VB=28896, PTS=29408, SG=30688, MG=16608)
MOE = dict(XG=0, XST=2048, YO=4096, SGB=6144, ACTB=6656, ACTT=7168, PG=7680, XTK=11776, SEL=15872, MT=17920,
           YG=22016, PLE=31712)
SSM = dict(ZS=0, XBC=4096, Y=10240, T=18432, BT=18432, XDT=19456, ONE=23568, CB=25616, DT=26640,
           DTV=29712, DTE=30224, ACS=30736, TK=31248)
FFN = dict(G=0, PAD=11264, T=13320)
FOX = dict(QH=0, KH=8192, V=16384, O=20480, PTS=24576, QB=25856, VB=26880, F=27392)
ARENA = 32800


class Count:

    def __init__(self, sem):
        self.sem, self.n, self.i, self.per = sem, 0, None, 0

    def inc(self, ins):
        ins.then_inc(self.sem, 1)
        self.n += 1

    def now(self, back=0):
        return self.n - back if self.i is None else self.i * self.per + (self.n - back)

    def enter(self, i, per):
        self.i, self.per, self.base = i, per, self.n

    def leave(self, rounds):
        assert self.n == self.base + self.per, (self.n - self.base, self.per)
        self.n, self.i = self.base + self.per * rounds, None


def lin(i, per, base):
    return base if i is None else i * per + base


def one(ap):
    return ap.rearrange("p o n -> p (o n)")


def build(nc, w_stream, x, p, positions, par, cst, sel16, x_tok, slot_tok, y_slots, out):
    with ExitStack() as ctx:
        def sb(name, cols, dt=F32):
            return ctx.enter_context(nc.sbuf_tensor(name, [P, cols], dt))

        def sem(name):
            return ctx.enter_context(nc.semaphore(name))

        ring = sb("ring", NS * SLAB * P)
        Xt, Rt, SQt = sb("X", C8 * S), sb("R", C8 * S), sb("SQ", C8 * S)
        X, R, SQ = (t[:, :].rearrange("p (c s) -> p c s", s=S) for t in (Xt, Rt, SQt))
        part = sb("part", NPAR)
        cstt = sb("cstt", NCST)
        STD, RSTD = sb("STD", S), sb("RSTD", S)
        stat = sb("stat", 64)
        arena = sb("arena", ARENA)
        bank = [ctx.enter_context(nc.psum_tensor(f"bank{i}", [P, S], F32)) for i in range(8)]

        slab_full = [sem(f"slab_full{i}") for i in range(NS)]
        slab_used = sem("slab_used")
        m_full, a_full = sem("m_full"), sem("a_full")
        m_out = [sem(f"m_out{i}") for i in range(4)]
        a_out = [sem(f"a_out{i}") for i in range(4)]
        squares_added = sem("squares_added")
        constants_loaded, x_loaded = sem("constants_loaded"), [sem(f"x_loaded{h}") for h in range(2)]
        loaded, p_loaded, sel_loaded = sem("loaded"), sem("p_loaded"), sem("sel_loaded")
        dve_step, act_step = sem("dve_step"), sem("act_step")
        ln_centred, ln_rstd, ln_scaled = sem("ln_centred"), sem("ln_rstd"), sem("ln_scaled")
        ln_squared, ln_done = sem("ln_squared"), sem("ln_done")
        conv_in, pads_zero, pool_mixed, rope_q, k_rope, k_rope_in = (
            sem("conv_in"), sem("pads_zero"), sem("pool_mixed"), sem("rope_q"), sem("k_rope"), sem("k_rope_in"))
        att_q, att_v, att_masked, att_max, att_nm, att_rs, att_prob = (
            sem(n) for n in ("att_q", "att_v", "att_masked", "att_max", "att_nm", "att_rs", "att_prob"))
        merged, resid = sem("merged"), sem("resid")
        routed, xtok_sent, slots_known, experts_known, ints, table_zero, table_set, table_read = (
            sem(n) for n in ("routed", "xtok_sent", "slots_known", "experts_known", "ints", "table_zero", "table_set",
                             "table_read"))
        tok_sum, y_filled = sem("tok_sum"), sem("y_filled")
        xg_loaded, yo_sent = [sem(f"xg_loaded{n}") for n in range(2)], [sem(f"yo_sent{n}") for n in range(2)]
        yg_loaded = [sem(f"yg_loaded{n}") for n in range(2 * NT)]
        sc_y, xbc_conv, xbc_done, dt_e, dt_ln, a_neg, dt_ready = (
            sem(n) for n in ("sc_y", "xbc_conv", "xbc_done", "dt_e", "dt_ln", "a_neg", "dt_ready"))
        ssd_dx, ssd_prev, ssd_l, ssd_e, ssd_m, ssd_d, ssd_u, dte = (
            sem(n) for n in ("ssd_dx", "ssd_prev", "ssd_l", "ssd_e", "ssd_m", "ssd_d", "ssd_u", "dte"))
        ffn_conv, ffn_g, ffn_silu = sem("ffn_conv"), sem("ffn_g"), sem("ffn_silu")
        f_e, f_ln, f_cum, f_rows, f_ones = (sem(n) for n in ("f_e", "f_ln", "f_cum", "f_rows", "f_ones"))
        out_done = sem("out_done")

        def pc(name, j=0, rows=slice(0, P)):
            return part[rows, PAR0[name] + j:PAR0[name] + j + 1]

        def pmat(name, k, w):
            return part[:, PAR0[name] + k * w:PAR0[name] + (k + 1) * w]

        def cm(name, w=P, rows=slice(0, P)):
            return cstt[rows, CST0[name]:CST0[name] + w]

        def ar(at, n, w=S, rows=slice(0, P)):
            return arena[rows, at:at + n * w].rearrange("p (c s) -> p c s", s=w)

        ident, ones = cm("ident"), cm("ones")
        _m, _o, _s, _x, _f = MIX, MOE, SSM, FOX, FFN
        ZB = ar(_m["ZB"], 12)
        ZP = ar(_m["ZP"], 4, 544)
        UP = ar(_m["UP"], 4, 528)
        PW = ar(_m["PW"], 2, 528)
        CQ, CKV, KT = ar(_m["CQ"], 3), ar(_m["CKV"], 2), ar(_m["KT"], 2)
        KR, COS, SIN = (arena[:, _m[n]:_m[n] + S] for n in ("KR", "COS", "SIN"))
        RT, MSG, MG = ar(_m["RT"], 2), ar(_m["SG"], 2), ar(_m["MG"], 8)
        H0 = TAPS - 1
        XG, XST, YO = ar(_o["XG"], 2, D), ar(_o["XST"], 2 * C8, P), ar(_o["YO"], 2, D)
        SGB, ACTB, ACTT = (arena[:, _o[n]:_o[n] + S] for n in ("SGB", "ACTB", "ACTT"))
        PG, XTK, YG, MT = ar(_o["PG"], 8), ar(_o["XTK"], 4, D), ar(_o["YG"], 2 * NT, D), ar(_o["MT"], 4, D)
        PLE = ar(_o["PLE"], 2)
        SEL, AFF, CMP, RANK, KEEP, GSC, WTOK = (
            arena[:, _o["SEL"] + a:_o["SEL"] + b] for a, b in
            ((0, 128), (128, 256), (256, 512), (512, 576), (576, 640), (640, 656), (656, 720)))
        DEST, DTMP, CNT, BEND, BSTART, BCMP, BEXP = (
            arena[:, _o["SEL"] + a:_o["SEL"] + b] for a, b in
            ((720, 784), (784, 848), (848, 912), (912, 928), (928, 944), (944, 944 + 16 * NB),
             (944 + 16 * NB, 944 + 17 * NB)))
        RTMP = arena[:, _o["SEL"] + 944 + 17 * NB:_o["SEL"] + 944 + 17 * NB + MORE_ROUNDS]
        RCNT = arena[:, _o["SEL"] + 960 + 17 * NB:_o["SEL"] + 961 + 17 * NB]
        MISC = _o["SEL"] + 961 + 17 * NB
        DMM, DWT, KIN = arena[:, MISC:MISC + 8], arena[:, MISC + 8:MISC + 16], arena[:, MISC + 16:MISC + 80]
        DI, TOKI, BEI, ROUNDS, IDX, ZI = (
            arena[:, MISC + a:MISC + b].bitcast(I32) for a, b in
            ((80, 88), (88, 92), (92, 92 + NB), (92 + NB, 93 + NB), (93 + NB, 94 + 2 * NB),
             (94 + 2 * NB, 95 + 3 * NB)))

        def gate_tile(b):
            return T0["moe"] + (4 * b - 2 if b else 0)

        def down_tile(b):
            return T0["moe"] + (4 * b + 4 if b < NB - 1 else 4 * NB - 2)

        def xt_tile(b):
            return A0["moe"] + (4 * b - 1 if b >= 2 else 3 * b)

        def actt_tile(b):
            return A0["moe"] + 4 * b + 6

        def rounds_to_run(eng):
            eng.wait_ge(experts_known, 1)
            return eng.value_load(ROUNDS[0:1, 0:1], min_val=(LEAST - 4) // 2, max_val=MORE_ROUNDS - 1)

        def count_skipped(eng, rounds, counts):
            with eng.Fori(rounds, MORE_ROUNDS) as i:
                for s, each, base in counts:
                    eng.wait_ge(s, i * each + base)
                    eng.sem_inc(s, each)

        ZS, XBC, BT, CBS = ar(_s["ZS"], 8), ar(_s["XBC"], 12), ar(_s["BT"], 2), ar(_s["CB"], 2)
        XDT, DX, SEL16 = ar(_s["XDT"], 4, 1024), R[:, 0:6], arena[:, _s["ONE"]:_s["ONE"] + 2048]
        YY = ar(_s["Y"], 16)
        DTB = ar(_s["DT"], 6)
        DT, DTE, ACS, TK = (arena[:, _s[n]:_s[n] + S] for n in ("DTV", "DTE", "ACS", "TK"))
        CS, CHP, CT = ar(_s["T"], 2), ar(_s["T"] + 1024, 2, 514), ar(_s["T"] + 2052, 2)
        XP, XA = ar(_s["T"] + 3076, 2, 515), ar(_s["T"] + 4106, 2)
        EB, LB, MB, CSB = R[:, 0:2], R[:, 2:4], R[:, 4:6], R[:, 6:8]
        G, FP, TF = ar(_f["G"], FT), ar(_f["PAD"], 4, 514), ar(_f["T"], 4)
        FB, F8 = ar(_x["F"], 6), ar(_x["F"] + 3072, 2)

        def head_tile(h):
            return A0["head"] + (h if h < 2 else 3 * (h // 2) - 1 + h % 2)

        def pair_tile(j):
            return A0["head"] + (3 * j + 4 if j < 7 else 23)

        ATT = {
            "att": dict(n=HEADS1, K=NOPE + ROPE, QH=ar(_m["QH"], 8), KH=ar(_m["KH"], 8), V=ar(_m["V"], 4, 512),
                        O=ZB[:, 4:8], PR=R, PTS=arena[:, _m["PTS"]:_m["PTS"] + 1280],
                        QB=ar(_m["QB"], 2), VB=ar(_m["VB"], 8, 64), scale=float((NOPE + ROPE) ** -0.5),
                        mask=cm("mask_mla"), h0=0),
            "fatt": dict(n=FOX_H, K=66, QH=ar(_x["QH"], 16), KH=ar(_x["KH"], 16), V=ar(_x["V"], 4, 1024),
                         O=ar(_x["O"], 8), PR=R, PTS=arena[:, _x["PTS"]:_x["PTS"] + 1280],
                         QB=ar(_x["QB"], 2), VB=ar(_x["VB"], 8, 64), scale=0.125, mask=cm("mask_fox"), h0=HEADS1),
        }
        NORMS = {}
        total = dict(centred=0, n=0, scaled=0, squared=0)

        def norm(name, c, src, dst, g, b, eps, fn=ACT.Identity):
            last = {"ln1": T0["wout"], "ln2": A0["mout"], "lnm0": T0["sout"], "lnf0": T0["down0"],
                    "lnm1": T0["fout"], "lnf1": T0["down1"]}.get(name, 0) + C8 - 1
            index = sum(m["summed"] for m in NORMS.values()) + 1
            NORMS[name] = dict(last=last, index=index, c=c, src=src, dst=dst, g=g, b=b, eps=eps, fn=fn, ln=b is not None,
                               summed=src is R, **total)
            total["centred"] += c if b is not None else 0
            total["n"] += 1
            total["scaled"] += c
            total["squared"] += c

        norm("ln_in", 8, X, X, "ln_in_g", "ln_in_b", "ln_eps")
        norm("qrms", 3, CQ, CQ, "q_norm_g", None, "rms_eps")
        norm("kvrms", 2, CKV, CKV, "kv_norm_g", None, "rms_eps")
        norm("convln", 4, ZB[:, 8:12], ZB[:, 8:12], "conv_ln_g", "conv_ln_b", "ln_eps", ACT.Silu)
        norm("ln1", 8, R, X, "ln1_g", "ln1_b", "ln_eps")
        norm("ln2", 8, R, X, "ln2_g", "ln2_b", "ln_eps")
        norm("grms0", 4, YY[:, 8:12], YY[:, 8:12], "ssm_norm_g", None, "ln_eps")
        norm("grms1", 4, YY[:, 12:16], YY[:, 12:16], "ssm_norm_g", None, "ln_eps")
        norm("lnm0", 8, R, X, "lnm0_g", "lnm0_b", "ln_eps")
        norm("lnf0", 8, R, X, "lnf0_g", "lnf0_b", "ln_eps")
        norm("lnm1", 8, R, X, "lnm1_g", "lnm1_b", "ln_eps")
        norm("lnf1", 8, R, X, "lnf1_g", "lnf1_b", "ln_eps")

        def norm_done(name, k=None):
            return NORMS[name]["scaled"] + (NORMS[name]["c"] if k is None else k + 1)

        def conv_gate_tile(m):
            return T0["branch"] + 32 + (m if m < 2 else 2 * m)

        def conv_proj_tile(m):
            return T0["branch"] + 32 + (2 + m if m < 2 else 2 * m + 1)

        block = ctx.enter_context(nc.Block())

        def m_ready(eng, t, i=None, per=0):
            eng.wait_ge(m_full, lin(i, per, t + 1))

        def a_ready(eng, t, i=None, per=0):
            eng.wait_ge(a_full, lin(i, per, t + 1))

        def m_read(eng, t, i=None, per=0):
            eng.wait_ge(m_out[t % 4], lin(i, per // 4, t // 4 + 1))

        def a_read(eng, t, i=None, per=0):
            eng.wait_ge(a_out[t % 4], lin(i, per // 4, t // 4 + 1))

        def mbank(t):
            return bank[t % 4]

        def abank(t):
            return bank[4 + t % 4]

        @block.sync
        def _(sp):
            sp.dma_start(cstt[:, :], cst).then_inc(constants_loaded, 16)
            for h in range(2):
                sp.dma_start(X[:, 4 * h:4 * h + 4], x[h * S:(h + 1) * S].rearrange("(c p) s -> p c s", p=P))\
                    .then_inc(x_loaded[h], 16)
            sp.dma_start(part[:, :], par).then_inc(loaded, 16)
            sp.dma_start(KR.bitcast(I32), positions).then_inc(loaded, 16)

            def load(slab, row, i=None, per=0):
                if slab >= NS:
                    sp.wait_ge(slab_used, lin(i, per, slab - NS + 1))
                src = w_stream[row] if isinstance(row, int) else w_stream[bass.ds(row, 1)].rearrange("o p n -> p (o n)")
                sp.dma_start(ring[:, (slab % NS) * SLAB * P:(slab % NS + 1) * SLAB * P], src)\
                    .then_inc(slab_full[slab % NS], 16)

            def run(first, last, back):
                rounds = (last - first) // NS
                with sp.Fori(0, rounds) as i:
                    for slab in range(first, first + NS):
                        load(slab, i * NS + (slab - back), i, NS)
                for slab in range(first + rounds * NS, last):
                    load(slab, slab - back)

            for slab in range(NS):
                load(slab, slab)
            sp.dma_start(PLE, p.rearrange("(c p) s -> p c s", p=P)).then_inc(p_loaded, 16)
            m0 = SLAB0["moe"]
            run(NS, m0, 0)

            def expert(b, i=None, k=0):
                col = BEI[0:1, b:b + 1] if i is None else BEI[0:1, bass.ds(i * 2 + k, 1)]
                return sp.value_load(col, min_val=0, max_val=EXPERTS - 1)

            def loads(b, e, part_, at, i=None):
                for j in range(8 if part_ == "up" else 4):
                    row = e * 12 + (m0 + j + (0 if part_ == "up" else 8))
                    load(m0 + at + j, row, i, 24)

            rounds = rounds_to_run(sp)
            loads(0, expert(0), "up", 0)
            for b in (1, 2, 3):
                loads(b, expert(b), "up", 12 * b - 4)
                loads(b - 1, expert(b - 1), "down", 12 * b + 4)
            with sp.Fori(0, rounds) as i:
                for b in (4, 5):
                    loads(b, expert(b, i, b), "up", 12 * b - 4, i)
                    loads(b - 1, expert(b - 1, i, b - 1), "down", 12 * b + 4, i)
            before = m0 + 44
            count_skipped(sp, rounds, [(slab_full[n], 6 * 16, 16 * ((before - n + NS - 1) // NS)) for n in range(NS)])
            loads(NB - 1, expert(3, rounds, 3), "down", 12 * NB - 4)
            run(SLAB0["pp"], NSLABS, 12 * (NB - EXPERTS))
            for k in range(C8):
                sp.wait_ge(ln_done, norm_done("lnf1") - C8 + k + 1)
                sp.dma_start(out[k * P:(k + 1) * P, :], X[:, k]).then_inc(out_done, 16)
            sp.wait_ge(out_done, 16 * C8)

        @block.tensor
        def _(pe):
            st = dict(n=0, b=0, pending=False)

            def weights(width=1, i=None, per=0):
                if st["b"] == 0:
                    slab = st["n"]
                    pe.wait_ge(slab_full[slab % NS], lin(i, 16 * per // NS, 16 * (slab // NS + 1)))
                    st["pending"] = slab > 0
                at = ((st["n"] % NS) * SLAB + st["b"]) * P
                st["b"] += width
                if st["b"] == SLAB:
                    st["b"], st["n"] = 0, st["n"] + 1
                return ring[:, at:at + width * P]

            def signal(ins, final=None):
                if final is not None:
                    ins.then_inc(final, 1)
                elif st["pending"]:
                    ins.then_inc(slab_used, 1)
                    st["pending"] = False

            def tile(t, rhs, i=None, per_t=0, per_s=0, norm=None, ready=None):
                if t >= 4:
                    m_read(pe, t - 4, i, per_t)
                for k, r in enumerate(rhs):
                    w = weights(1, i, per_s)
                    if norm:
                        pe.wait_ge(ln_done, norm_done(norm, k))
                    if ready:
                        pe.wait_ge(ready[0], ready[1] + k + 1)
                    mm = pe.matmul(mbank(t)[:, :], w, r, start=(k == 0), stop=(k == len(rhs) - 1))
                    signal(mm, m_full if k == len(rhs) - 1 else None)

            def loop(rounds, tiles, slabs, body):
                n0 = st["n"]
                with pe.Fori(0, rounds) as i:
                    body(i)
                assert st["n"] == n0 + slabs and st["b"] == 0
                st["n"] = n0 + slabs * rounds

            def stats(name, waits=(), between=None):
                n = NORMS[name]
                t = A0[name]
                for s, v in waits:
                    pe.wait_ge(s, v)
                if n["ln"]:
                    if t >= 4:
                        a_read(pe, t - 4)
                    src = [SQ[:, 0], R[:, C8 - 1]] if n["summed"] else [n["src"][:, k] for k in range(n["c"])]
                    for k, v in enumerate(src):
                        if name == "ln_in":
                            pe.wait_ge(x_loaded[k // 4], 16)
                        if n["summed"] and k:
                            (a_read if name == "ln2" else m_read)(pe, n["last"])
                        mm = pe.matmul(abank(t)[:, :], ones, v, start=(k == 0), stop=(k == len(src) - 1))
                    mm.then_inc(a_full, 1)
                    t += 1
                    if between:
                        between()
                if t >= 4:
                    a_read(pe, t - 4)
                c = n["c"] - n["summed"]
                for k in range(c):
                    if n["summed"] and k == c - 1:
                        pe.wait_ge(squares_added, n["index"])
                    else:
                        pe.wait_ge(ln_squared, n["squared"] + k + 1)
                    mm = pe.matmul(abank(t)[:, :], ones, SQ[:, k], start=(k == 0), stop=(k == c - 1))
                mm.then_inc(a_full, 1)

            def attention(name):
                a = ATT[name]
                K = a["K"]

                def scores(h, i=None):
                    per = 4 * 2
                    pe.wait_ge(att_q, lin(i, 2, a["h0"] + h + 1))
                    for q in range(NT):
                        t = T0[name] + 4 * h + q
                        m_read(pe, t - 4, i, per)
                        k = a["KH"][0:K, h, 0:(q + 1) * P] if i is None else \
                            one(a["KH"][0:K, bass.ds(i * 2 + h, 1), 0:(q + 1) * P])
                        pe.matmul(mbank(t)[:, 0:(q + 1) * P], a["QB"][0:K, h % 2, q * P:(q + 1) * P], k,
                                  start=True, stop=True).then_inc(m_full, 1)

                def values(h, i=None):
                    per = 4 * 2
                    pe.wait_ge(att_prob, lin(i, 8, 4 * (a["h0"] + h + 1)))
                    t = A0[name] + 4 * h
                    for n, blocks in enumerate((((0, 0), (1, 0), (2, 0), (3, 0)), ((1, 1), (2, 1), (3, 1)),
                                                ((2, 2), (3, 2), (3, 3)))):
                        a_read(pe, t + n - 4, i, per)
                        for m, (q, k) in enumerate(blocks):
                            tr = pe.transpose(abank(t + n)[:, m * P:(m + 1) * P],
                                              a["PR"][:, 4 * (h % 2) + q, k * P:(k + 1) * P], ident)
                        tr.then_inc(a_full, 1)
                    a_read(pe, t - 1, i, per)
                    pe.wait_ge(att_v, lin(i, 2, a["h0"] + h + 1))
                    for k, at in enumerate((0, 512, 896, 1152)):
                        if k < 3:
                            a_read(pe, t + k, i, per)
                        mm = pe.matmul(abank(t + 3)[0:64, k * P:S], a["VB"][:, 4 * (h % 2) + k, :],
                                       a["PTS"][:, at:at + (NT - k) * P], start=(k == 0), stop=(k == NT - 1))
                    mm.then_inc(a_full, 1)

                scores(0)
                with pe.Fori(0, a["n"] // 2 - 1) as i:
                    scores(1, i)
                    values(0, i)
                    scores(2, i)
                    values(1, i)
                scores(a["n"] - 1)
                values(a["n"] - 2)
                values(a["n"] - 1)

            Xr = [X[:, k] for k in range(C8)]
            pe.wait_ge(constants_loaded, 16)
            stats("ln_in")
            pe.wait_ge(loaded, 32)
            for n in range(19):
                tile(T0["in"] + n, Xr, norm="ln_in" if n == 0 else None)
                if n == 14:
                    stats("qrms")
                if n == 16:
                    stats("kvrms")
            for n in range(8):
                tile(T0["uq"] + n, [CQ[:, k] for k in range(3)], norm="qrms" if n == 0 else None)
            for n in range(4):
                tile(T0["uk"] + n, [CKV[:, k] for k in range(2)], norm="kvrms" if n == 0 else None)
            for t in range(4):
                m_read(pe, T0["uv"] + t - 4)
            for k in range(2):
                w = weights(4)
                for t in range(NT):
                    mm = pe.matmul(mbank(T0["uv"] + t)[:, :], CKV[:, k, t * P:(t + 1) * P], w,
                                   start=(k == 0), stop=(k == 1))
                    signal(mm, m_full if k == 1 else None)
            for g in range(4):
                t = A0["poolw"] + g
                pe.wait_ge(pool_mixed, g + 1)
                a_read(pe, t - 4)
                pe.matmul(abank(t)[:, :], pmat("pool_w", g, P), UP[:, g, 16:16 + S], start=True, stop=True)\
                    .then_inc(a_full, 1)
            pe.wait_ge(k_rope, HEADS1)
            for j in range(4):
                m_read(pe, T0["uv"] + j)
            attention("att")
            def branch(i):
                for m in range(C8):
                    t = T0["branch"] + 2 * m
                    tile(t, Xr, i, 16, 12)
                    tile(t + 1, [one(ZB[:, bass.ds(i * 4 + k, 1), :]) for k in range(4)], i, 16, 12)

            for t in range(A0["att"] + 4 * HEADS1 - 4, A0["att"] + 4 * HEADS1):
                a_read(pe, t)
            loop(2, 32, 12, branch)
            gate, proj = conv_gate_tile, conv_proj_tile
            stats("convln", [(merged, 1)], lambda: tile(gate(0), Xr))
            tile(gate(1), Xr)
            tile(proj(0), [ZB[:, 8 + k] for k in range(4)], norm="convln")
            tile(proj(1), [ZB[:, 8 + k] for k in range(4)])
            for m in range(2, C8):
                tile(gate(m), Xr)
                tile(proj(m), [ZB[:, 8 + k] for k in range(4)])
            pe.wait_ge(merged, 2)
            for m in range(C8):
                tile(T0["wout"] + m, [MG[:, k] for k in range(C8)])
            stats("ln1", [(resid, 1)])
            t = A0["route"]
            a_read(pe, t - 4)
            for q in range(NT):
                for k in range(C8):
                    if q == 0:
                        pe.wait_ge(ln_done, norm_done("ln1", k))
                    mm = pe.matmul(abank(t)[:, 16 * q:16 * q + 16], X[:, k, q * P:(q + 1) * P],
                                   pmat("router", k, 16), start=(k == 0), stop=(k == C8 - 1))
            mm.then_inc(a_full, 1)
            for q in range(NT):
                for half in range(2):
                    t = A0["xtok1"] + 2 * q + half
                    a_read(pe, t - 4)
                    for j in range(4):
                        tr = pe.transpose(abank(t)[:, j * P:(j + 1) * P], X[:, 4 * half + j, q * P:(q + 1) * P], ident)
                    tr.then_inc(a_full, 1)
            for m in range(C8):
                tile(T0["pg"] + m, Xr)
                if m == 2:
                    t = A0["count"]
                    pe.wait_ge(routed, 1)
                    a_read(pe, t - 4)
                    for q in range(NT):
                        for r in range(q + 1):
                            pe.matmul(abank(t)[:, 16 * q:16 * q + 16], cm("before") if r == q else ones,
                                      KIN[:, 16 * r:16 * r + 16], start=(r == 0), stop=(r == q))
                    for r in range(NT):
                        mm = pe.matmul(abank(t)[:, 64:80], ones, KIN[:, 16 * r:16 * r + 16],
                                       start=(r == 0), stop=(r == NT - 1))
                    mm.then_inc(a_full, 1)
            def wide(t, lhs, i=None):
                m_read(pe, t - 4, i, 8)
                for k, w_ in enumerate(lhs):
                    w = weights(4, i, 24)
                    mm = pe.matmul(mbank(t)[:, :], w_, w, start=(k == 0), stop=(k == len(lhs) - 1))
                    signal(mm, m_full if k == len(lhs) - 1 else None)

            def x_transposes(b, i=None):
                pe.wait_ge(xg_loaded[b % 2], lin(i, 16, 16 * (b // 2 + 1)))
                for n in range(3):
                    t = xt_tile(b) + n
                    a_read(pe, t - 4, i, 8)
                    for j in range(3 * n, min(3 * n + 3, C8)):
                        tr = pe.transpose(abank(t)[:, (j - 3 * n) * P:(j - 3 * n + 1) * P],
                                          XG[:, b % 2, j * P:(j + 1) * P], ident)
                    tr.then_inc(a_full, 1)

            def act_transposes(b, i=None):
                t = actt_tile(b)
                m_read(pe, gate_tile(b) + 1, i, 8)
                a_read(pe, t - 4, i, 8)
                for j in range(4):
                    tr = pe.transpose(abank(t)[:, j * P:(j + 1) * P], ACTB[:, j * P:(j + 1) * P], ident)
                tr.then_inc(a_full, 1)

            def up(b, half, i=None):
                if half == 0:
                    for n in range(3):
                        a_read(pe, xt_tile(b) + n, i, 8)
                wide(gate_tile(b) + half, [XST[:, C8 * (b % 2) + k] for k in range(C8)], i)

            def down(b, i=None):
                a_read(pe, actt_tile(b), i, 8)
                for half in range(2):
                    wide(down_tile(b) + half, [ACTT[:, k * P:(k + 1) * P] for k in range(4)], i)

            def block_of_slots(b, i=None):
                up(b, 0, i)
                act_transposes(b - 1, i)
                x_transposes(b + 1, i)
                up(b, 1, i)
                down(b - 1, i)

            x_transposes(0)
            up(0, 0)
            x_transposes(1)
            up(0, 1)
            block_of_slots(1)
            block_of_slots(2)
            block_of_slots(3)
            n0 = st["n"]
            rounds = rounds_to_run(pe)
            with pe.Fori(0, rounds) as i:
                block_of_slots(4, i)
                block_of_slots(5, i)
            assert st["n"] == n0 + 24 and st["b"] == 0
            st["n"] = n0 + 24 * MORE_ROUNDS
            count_skipped(pe, rounds, [(m_full, 8, T0["moe"] + 14), (a_full, 8, A0["moe"] + 18),
                                       (slab_used, 24, SLAB0["moe"] + 43)])
            act_transposes(NB - 1)
            down(NB - 1)
            pe.wait_ge(p_loaded, 16)
            for m in range(C8):
                tile(T0["pp"] + m, [PLE[:, k] for k in range(2)])
            for k in range(C8):
                t = A0["mout"] + k
                a_read(pe, t - 4)
                for q in range(NT):
                    pe.wait_ge(tok_sum, q + 1)
                    tr = pe.transpose(abank(t)[:, q * P:(q + 1) * P], MT[:, q, k * P:(k + 1) * P], ident)
                tr.then_inc(a_full, 1)
            stats("ln2", [(resid, 2)])
            t = A0["dt"]
            a_read(pe, t - 4)
            for k in range(C8):
                pe.wait_ge(ln_done, norm_done("ln2", k))
                mm = pe.matmul(abank(t)[0:16, :], pmat("w_dt", k, 16), X[:, k], start=(k == 0), stop=(k == C8 - 1))
            mm.then_inc(a_full, 1)

            def four(base, n, norm=None):
                if norm:
                    for j in range(4):
                        tile(base + j, Xr, norm=norm if j == 0 else None)
                    base, n = base + 4, n - 4

                def body(i):
                    for j in range(4):
                        tile(base + j, Xr, i, 4, 4)
                loop(n // 4, 4, 4, body)

            def twelve(i):
                for j in range(12):
                    tile(T0["s_in"] + j, Xr, i, 12, 12)
            loop(2, 12, 12, twelve)
            four(T0["s_in"] + 24, 8)
            four(T0["s_in"] + 32, 12)
            def sout_half(m, half):
                t = T0["sout"] + m
                if half == 0:
                    m_read(pe, t - 4)
                for k in range(C8 * half, C8 * half + C8):
                    if half:
                        pe.wait_ge(ln_done, norm_done(f"grms{k // 4 - 2}", k % 4))
                    mm = pe.matmul(mbank(t)[:, :], weights(1), YY[:, k], start=(k == 0), stop=(k == 15))
                    signal(mm, m_full if k == 15 else None)

            t = A0["acst"]
            pe.wait_ge(dt_ready, 1)
            a_read(pe, t - 4)
            for n, src in enumerate((ACS, DT, DTE)):
                for c in range(NT):
                    tr = pe.transpose(abank(t)[:, 64 * n + 16 * c:64 * n + 16 * c + 16],
                                      src[0:16, c * P:(c + 1) * P], ident[0:16, 0:16])
            tr.then_inc(a_full, 1)
            sout_half(0, 0)
            pe.wait_ge(xbc_done, 12)
            for g in range(2):
                t = A0["btok"] + g
                a_read(pe, t - 4)
                for c in range(NT):
                    tr = pe.transpose(abank(t)[:, c * P:(c + 1) * P], XBC[:, 8 + g, c * P:(c + 1) * P], ident)
                tr.then_inc(a_full, 1)
            for c in range(NT):
                for g in range(2):
                    t = A0["xtok"] + 2 * c + g
                    a_read(pe, t - 4)
                    for j in range(4):
                        tr = pe.transpose(abank(t)[:, j * P:(j + 1) * P], XBC[:, 4 * g + j, c * P:(c + 1) * P], ident)
                    tr.then_inc(a_full, 1)
            for g in range(2):
                t = A0["cb"] + g
                a_read(pe, t - 4)
                for c in range(NT):
                    cs = slice(c * P, (c + 1) * P)
                    mm = pe.matmul(abank(t)[:, cs], XBC[:, 8 + g, cs], XBC[:, 10 + g, cs], start=True, stop=True)
                mm.then_inc(a_full, 1)
            a_read(pe, A0["btok"])
            a_read(pe, A0["btok"] + 1)
            for c in range(NT - 1):
                for g in range(2):
                    t = A0["state"] + 2 * c + g
                    pe.wait_ge(ssd_dx, 2 * c + g + 1)
                    a_read(pe, t - 4)
                    pe.matmul(abank(t)[:, :], BT[:, g, c * P:(c + 1) * P], DX[:, 2 * c + g],
                              start=True, stop=True).then_inc(a_full, 1)

            def decays(h):
                t = head_tile(h)
                a_read(pe, t - 4)
                pe.matmul(abank(t)[:, :], SEL16[0:16, h * P:(h + 1) * P], ACS[0:16, :], start=True, stop=True)\
                    .then_inc(a_full, 1)

            pe.wait_ge(sel_loaded, 16)
            decays(0)
            decays(1)
            for c in range(NT):
                for g in range(2):
                    a_read(pe, A0["xtok"] + 2 * c + g)
            for j in range(C8):
                if j < C8 - 1:
                    decays(2 * j + 2)
                    decays(2 * j + 3)
                t = pair_tile(j)
                a_read(pe, t - 4)
                pe.wait_ge(ssd_m, 2 * j + 2)
                pe.wait_ge(ssd_e, 2 * j + 2)
                pe.wait_ge(ssd_prev, 4 * j + 4)
                for h in (2 * j, 2 * j + 1):
                    r = slice(64 * (h % 2), 64 * (h % 2) + 64)
                    f = slice((h % 8) * 64, (h % 8) * 64 + 64)
                    for c in range(NT):
                        cs = slice(c * P, (c + 1) * P)
                        mm = pe.matmul(abank(t)[r, cs], XDT[:, c, h * 64:h * 64 + 64], MB[:, h % 2, cs],
                                       start=True, stop=(c == 0))
                        if c:
                            mm = pe.matmul(abank(t)[r, cs], SQ[:, 2 * (c - 1) + h // 8, f], CSB[:, h % 2, cs],
                                           start=False, stop=True)
                mm.then_inc(a_full, 1)
            sout_half(1, 0)
            stats("grms0")
            sout_half(2, 0)
            stats("grms1")
            sout_half(3, 0)
            for m in range(4):
                sout_half(m, 1)
            for m in range(4, C8):
                tile(T0["sout"] + m, [YY[:, k] for k in range(16)])
            stats("lnm0", [(resid, 3)])

            def ffn(layer, first, last, resid_n):
                four(T0[f"up{layer}"], 2 * FT, first)
                for m in range(C8):
                    tile(T0[f"down{layer}"] + m, [G[:, k] for k in range(FT)],
                         ready=(ffn_g, FT * layer) if m == 0 else None)
                stats(last, [(resid, resid_n)])

            ffn(0, "lnm0", "lnf0", 4)
            t = A0["f"]
            a_read(pe, t - 4)
            for k in range(C8):
                pe.wait_ge(ln_done, norm_done("lnf0", k))
                mm = pe.matmul(abank(t)[0:16, :], pmat("w_f", k, 16), X[:, k], start=(k == 0), stop=(k == C8 - 1))
            mm.then_inc(a_full, 1)
            four(T0["fqk"], 16)
            for half in range(2):
                for q in range(NT):
                    m_read(pe, T0["fv"] + 4 * half + q - 4)
                for k in range(C8):
                    w = weights(4)
                    for q in range(NT):
                        mm = pe.matmul(mbank(T0["fv"] + 4 * half + q)[:, :], X[:, k, q * P:(q + 1) * P], w,
                                       start=(k == 0), stop=(k == C8 - 1))
                        signal(mm, m_full if k == C8 - 1 else None)
            pe.wait_ge(f_rows, 32)
            for q in range(NT):
                m_read(pe, T0["fv"] + 4 + q)
            attention("fatt")
            for t in range(A0["fatt"] + 4 * FOX_H - 4, A0["fatt"] + 4 * FOX_H):
                a_read(pe, t)
            for m in range(C8):
                tile(T0["fout"] + m, [ATT["fatt"]["O"][:, k] for k in range(C8)])
            stats("lnm1", [(resid, 5)])
            ffn(1, "lnm1", "lnf1", 6)

        @block.scalar
        def _(act):
            step = Count(act_step)

            def norm_act(name, waits=(), between=None):
                n = NORMS[name]
                t = A0[name] + n["ln"]
                for s, v in waits:
                    act.wait_ge(s, v)
                for k in range(n["c"]):
                    if n["ln"]:
                        act.wait_ge(ln_centred, n["centred"] + k + 1)
                    act.activation(SQ[:, k], n["src"][:, k], ACT.Square).then_inc(ln_squared, 1)
                if between:
                    between()
                a_ready(act, t)
                act.activation(STD[:, :], abank(t)[:, :], ACT.Sqrt, bias=cm(n["eps"], 1),
                               scale=1.0 / (n["c"] * P)).then_inc(a_out[t % 4], 1)
                for k in range(n["c"]):
                    act.wait_ge(ln_scaled, n["scaled"] + k + 1)
                    b = pc(n["b"], k) if n["ln"] else cm("zero", 1)
                    gk = k + (4 if name == "grms1" else 0)
                    act.activation(n["dst"][:, k], n["src"][:, k], n["fn"], bias=b, scale=pc(n["g"], gk))\
                        .then_inc(ln_done, 1)

            def attention(name):
                a = ATT[name]

                def exps(h, i=None):
                    act.wait_ge(att_nm, lin(i, 2, a["h0"] + h + 1))
                    if h >= 2:
                        a_ready(act, A0[name] + 4 * (h - 2) + 2, i, 8)
                    elif i is not None:
                        act.wait_ge(a_full, i * 8 + (A0[name] + 4 * (h - 2) + 3))
                    for q in range(NT):
                        t = T0[name] + 4 * h + q
                        c = 8 * (h % 2) + q
                        act.activation(a["PR"][:, 4 * (h % 2) + q, 0:(q + 1) * P], mbank(t)[:, 0:(q + 1) * P], ACT.Exp,
                                       bias=stat[:, c:c + 1], scale=a["scale"],
                                       accum_out=stat[:, c + 4:c + 5]).then_inc(m_out[t % 4], 1)

                def transposed(h, i=None):
                    t = A0[name] + 4 * h
                    a_ready(act, t, i, 8)
                    act.activation(a["PTS"][:, 0:S], abank(t)[:, :], ACT.Copy).then_inc(a_out[t % 4], 1)

                def output(h, i=None):
                    t = A0[name] + 4 * h
                    a_ready(act, t + 3, i, 8)
                    r = slice(64 * (h % 2), 64 * (h % 2) + 64)
                    o = a["O"][r, h // 2] if i is None else one(a["O"][r, bass.ds(i + h // 2, 1), :])
                    act.activation(o, abank(t + 3)[0:64, :], ACT.Copy).then_inc(a_out[(t + 3) % 4], 1)

                def step_of_heads(h, i=None):
                    transposed(h - 1, i)
                    exps(h, i)
                    output(h - 1, i)

                exps(0)
                with act.Fori(0, a["n"] // 2 - 1) as i:
                    step_of_heads(1, i)
                    step_of_heads(2, i)
                step_of_heads(a["n"] - 1)
                transposed(a["n"] - 1)
                output(a["n"] - 1)

            act.wait_ge(constants_loaded, 16)
            act.wait_ge(loaded, 32)
            norm_act("ln_in")
            act.wait_ge(rope_q, 1)
            act.activation(SIN, RT[:, 0], ACT.Sin, bias=cm("zero", 1)).then_inc(act_step, 1)
            act.activation(COS, RT[:, 1], ACT.Sin, bias=cm("zero", 1)).then_inc(act_step, 1)
            step.n = 2
            for k in range(4):
                t = T0["in"] + 2 * k + 1
                if k >= 2:
                    act.wait_ge(conv_in, k - 1)
                m_ready(act, t)
                act.activation(MSG[:, k % 2], mbank(t)[:, :], ACT.Sigmoid).then_inc(m_out[t % 4], 1)
            for k in range(3):
                t = T0["in"] + 8 + k
                m_ready(act, t)
                act.activation(CQ[:, k], mbank(t)[:, :], ACT.Copy).then_inc(m_out[t % 4], 1)
            for k in range(2):
                t = T0["in"] + 11 + k
                m_ready(act, t)
                act.activation(CKV[:, k], mbank(t)[:, :], ACT.Copy).then_inc(m_out[t % 4], 1)
            m_read(act, T0["in"] + 8)
            m_read(act, T0["in"] + 9)
            m_read(act, T0["in"] + 10)
            norm_act("qrms")
            m_read(act, T0["in"] + 11)
            m_read(act, T0["in"] + 12)
            norm_act("kvrms")
            act.wait_ge(pads_zero, 2)
            for g in range(4):
                t = T0["in"] + 15 + g
                m_ready(act, t)
                act.activation(UP[:, g, 16:16 + S], mbank(t)[:, :], ACT.Copy).then_inc(m_out[t % 4], 1)

            def split_heads(dst, t, j):
                m_ready(act, t)
                act.activation(dst[0:64, 2 * j], mbank(t)[0:64, :], ACT.Copy).then_inc(act_step, 1)
                act.activation(dst[0:64, 2 * j + 1], mbank(t)[64:128, :], ACT.Copy).then_inc(m_out[t % 4], 1)

            for j in range(4):
                split_heads(ATT["att"]["QH"], T0["uq"] + j, j)
            for j in range(4):
                split_heads(ATT["att"]["KH"], T0["uk"] + j, j)
            for k in range(4):
                t = T0["uv"] + k
                m_ready(act, t)
                act.activation(ATT["att"]["V"][:, k], mbank(t)[:, :], ACT.Copy).then_inc(m_out[t % 4], 1)
            for g in range(4):
                t = A0["poolw"] + g
                a_ready(act, t)
                act.activation(ZB[:, g], abank(t)[:, :], ACT.Identity, bias=cm("zero", 1),
                               scale=pc("pool_scale", g)).then_inc(a_out[t % 4], 1)
            act.wait_ge(ln_done, norm_done("ln_in"))
            spare = NB - LEAST
            act.dma_start(y_slots[LEAST:NB].rearrange("b p (c s) -> p b c s", s=S),
                          X[:, 0:2].rearrange("p (o c) s -> p o c s", o=1).to_broadcast([P, spare, 2, S]))\
                .then_inc(y_filled, 16)
            attention("att")

            with act.Fori(0, 2) as i:
                for m in range(C8):
                    t = T0["branch"] + 2 * m
                    m_read(act, t + 1 - 4, i, 16)
                    m_ready(act, t, i, 16)
                    act.activation(MSG[:, m % 2], mbank(t)[:, :], ACT.Sigmoid,
                                   bias=part[:, bass.ds(i * 8 + (PAR0["b_gate"] + m), 1)]).then_inc(m_out[t % 4], 1)

            def conv_gate(m):
                t = conv_gate_tile(m)
                m_read(act, conv_proj_tile(m - 2) if m >= 2 else T0["branch"] + 29 + 2 * m)
                m_ready(act, t)
                act.activation(MSG[:, m % 2], mbank(t)[:, :], ACT.Sigmoid, bias=pc("b_gate", 16 + m))\
                    .then_inc(m_out[t % 4], 1)

            norm_act("convln", between=lambda: conv_gate(0))
            for m in range(1, C8):
                conv_gate(m)
            act.wait_ge(y_filled, 16)
            norm_act("ln1")
            t = A0["route"]
            a_ready(act, t)
            act.activation(AFF[:, 0:64], abank(t)[:, 0:64], ACT.Sigmoid).then_inc(a_out[t % 4], 1)
            for q in range(NT):
                for half in range(2):
                    t = A0["xtok1"] + 2 * q + half
                    a_ready(act, t)
                    act.activation(XTK[:, q, half * S:(half + 1) * S], abank(t)[:, :], ACT.Copy)\
                        .then_inc(a_out[t % 4], 1)
            for n in range(4, 8):
                a_read(act, A0["xtok1"] + n)
            act.dma_start(x_tok.rearrange("(q p) d -> p q d", p=P), XTK).then_inc(xtok_sent, 16)
            for m in range(C8):
                t = T0["pg"] + m
                m_ready(act, t)
                act.activation(PG[:, m], mbank(t)[:, :], ACT.Sigmoid).then_inc(m_out[t % 4], 1)

            def silu(b, i=None):
                t = gate_tile(b)
                if b or i is not None:
                    m_read(act, gate_tile(b - 1) + 1, i, 8)
                m_ready(act, t, i, 8)
                act.activation(SGB, mbank(t)[:, :], ACT.Silu).then_inc(m_out[t % 4], 1)

            def finish(b, i=None, rounds=None):
                t = actt_tile(b)
                a_ready(act, t, i, 8)
                act.activation(ACTT, abank(t)[:, :], ACT.Copy).then_inc(a_out[t % 4], 1)
                t = down_tile(b)
                if b >= 2 or i is not None:
                    act.wait_ge(yo_sent[b % 2], lin(i, 16, 16 * (b // 2)) if b >= 2 else i * 16)
                m_ready(act, t, i, 8)
                act.activation(YO[:, b % 2, 0:S], mbank(t)[:, :], ACT.Copy).then_inc(m_out[t % 4], 1)
                m_read(act, t, i, 8)
                m_read(act, t + 1, i, 8)
                if rounds is not None:
                    i, b = rounds, 3
                dst = y_slots[b] if i is None else y_slots[bass.ds(i * 2 + b, 1)].rearrange("o p d -> p (o d)")
                act.dma_start(dst, YO[:, b % 2]).then_inc(yo_sent[b % 2], 16)

            silu(0)
            silu(1)
            finish(0)
            silu(2)
            finish(1)
            silu(3)
            finish(2)
            rounds = rounds_to_run(act)
            with act.Fori(0, rounds) as i:
                silu(4, i)
                finish(3, i)
                silu(5, i)
                finish(4, i)
            count_skipped(act, rounds, [(m_out[t % 4], 2, t // 4 + 1) for t in (gate_tile(3), down_tile(2))] +
                          [(a_out[actt_tile(2) % 4], 2, actt_tile(2) // 4 + 1),
                           (yo_sent[0], 16, 32), (yo_sent[1], 16, 16)])
            finish(NB - 1, None, rounds)
            norm_act("ln2")
            def log1p_act(b, src_tile, bias):
                t = A0[src_tile]
                a_ready(act, t)
                act.activation(b[0:16, 0], abank(t)[0:16, :], ACT.Identity, bias=pc(bias, 0, slice(0, 16)))\
                    .then_inc(a_out[t % 4], 1)
                n = 1 if src_tile == "f" else 0
                act.wait_ge(dt_ln, 2 * n + 1)
                act.activation(b[0:16, 2], b[0:16, 1], ACT.Exp, scale=-1.0).then_inc(dt_e, 1)
                act.wait_ge(dt_ln, 2 * n + 2)
                act.activation(b[0:16, 4], b[0:16, 3], ACT.Ln).then_inc(dt_e, 1)

            act.activation(stat[0:16, 50:51], pc("a_log", 0, slice(0, 16)), ACT.Exp).then_inc(a_neg, 1)
            log1p_act(DTB, "dt", "dt_bias")
            act.wait_ge(dte, 1)
            for c in range(NT):
                last = ACS[0:16, (c + 1) * P - 1:(c + 1) * P]
                ins = act.activation(DTE[0:16, c * P:(c + 1) * P], ACS[0:16, c * P:(c + 1) * P], ACT.Exp,
                                     bias=last, scale=-1.0)
            ins.then_inc(a_neg, 1)
            with act.Fori(0, 2) as i:
                for m in range(4):
                    t = T0["s_in"] + 3 * m
                    m_read(act, t - 5, i, 12)
                    m_ready(act, t, i, 12)
                    act.activation(CS[:, m % 2], mbank(t)[:, :], ACT.Copy).then_inc(m_out[t % 4], 1)
            with act.Fori(0, 2) as i:
                for m in range(4):
                    t = T0["s_in"] + 24 + m
                    m_ready(act, t, i, 4)
                    act.activation(one(ZS[:, bass.ds(i * 4 + m, 1), :]), mbank(t)[:, :], ACT.Silu)\
                        .then_inc(m_out[t % 4], 1)
            with act.Fori(0, 3) as i:
                for m in range(4):
                    t = T0["s_in"] + 32 + m
                    m_ready(act, t, i, 4)
                    act.wait_ge(xbc_conv, i * 4 + (m + 1))
                    act.activation(XP[:, m % 2, 3:3 + S], mbank(t)[:, :], ACT.Copy).then_inc(m_out[t % 4], 1)
                    act.wait_ge(xbc_conv, i * 4 + (m + 3))
                    act.activation(one(XBC[:, bass.ds(i * 4 + m, 1), :]), XA[:, m % 2], ACT.Silu,
                                   bias=part[:, bass.ds(i * 4 + (PAR0["ssm_conv_b"] + m), 1)]).then_inc(xbc_done, 1)
            t = A0["acst"]
            a_ready(act, t)
            act.activation(TK[:, 0:192], abank(t)[:, 0:192], ACT.Copy).then_inc(a_out[t % 4], 1)
            for g in range(2):
                t = A0["btok"] + g
                a_ready(act, t)
                act.activation(BT[:, g], abank(t)[:, :], ACT.Copy).then_inc(a_out[t % 4], 1)
            for g in range(2):
                t = A0["cb"] + g
                a_ready(act, t)
                act.activation(CBS[:, g], abank(t)[:, :], ACT.Copy).then_inc(a_out[t % 4], 1)
            for n in range(6):
                t = A0["state"] + n
                a_ready(act, t)
                act.activation(SQ[:, n], abank(t)[:, :], ACT.Copy).then_inc(a_out[t % 4], 1)
            for h in range(SSM_H):
                t = head_tile(h)
                if h >= 2:
                    act.wait_ge(ssd_e, h - 1)
                    act.wait_ge(ssd_prev, 2 * (h - 2) + 2)
                a_ready(act, t)
                act.activation(EB[:, h % 2], abank(t)[:, :], ACT.Exp).then_inc(ssd_u, 1)
                act.wait_ge(ssd_d, 4 * h + 4)
                act.activation(LB[:, h % 2], LB[:, h % 2], ACT.Exp).then_inc(ssd_l, 1)
            norm_act("grms0", [(sc_y, 8)])
            norm_act("grms1")
            norm_act("lnm0")

            def ffn(layer, last):
                with act.Fori(0, FT // 2) as i:
                    for k in range(4):
                        t = T0[f"up{layer}"] + k
                        m_ready(act, t, i, 4)
                        act.wait_ge(ffn_conv, i * 4 + (48 * layer + k + 1))
                        act.activation(FP[:, k, 2:2 + S], mbank(t)[:, :], ACT.Copy).then_inc(m_out[t % 4], 1)
                        if k % 2:
                            act.wait_ge(ffn_conv, i * 4 + (48 * layer + k + 5))
                            act.activation(TF[:, k], TF[:, k], ACT.Silu).then_inc(ffn_silu, 1)
                norm_act(last)

            ffn(0, "lnf0")
            log1p_act(FB, "f", "b_f")
            QK = ar(_x["QH"], 32)
            with act.Fori(0, 4) as i:
                for j in range(4):
                    t = T0["fqk"] + j
                    m_ready(act, t, i, 4)
                    for h in range(2):
                        ins = act.activation(one(QK[0:64, bass.ds(i * 8 + (2 * j + h), 1), :]),
                                             mbank(t)[64 * h:64 * h + 64, :], ACT.Copy)
                    ins.then_inc(m_out[t % 4], 1)
            for half in range(2):
                for q in range(NT):
                    t = T0["fv"] + 4 * half + q
                    m_ready(act, t)
                    act.activation(ATT["fatt"]["V"][:, q, half * S:half * S + S], mbank(t)[:, :], ACT.Copy)\
                        .then_inc(m_out[t % 4], 1)
            attention("fatt")
            norm_act("lnm1")
            ffn(1, "lnf1")

        @block.vector
        def _(dve):
            step = Count(dve_step)

            def sync():
                dve.wait_ge(dve_step, step.now())

            def norm_dve(name):
                n = NORMS[name]
                t = A0[name]
                if n["ln"]:
                    a_ready(dve, t)
                    for k in range(n["c"]):
                        ins = dve.scalar_tensor_tensor(out=n["src"][:, k], in0=abank(t)[:, :],
                                                       scalar=-1.0 / (n["c"] * P), in1=n["src"][:, k],
                                                       op0=ALU.mult, op1=ALU.add)
                        ins.then_inc(ln_centred, 1)
                    dve.wait_ge(ln_centred, n["centred"] + n["c"])
                    dve.engine_nop().then_inc(a_out[t % 4], 1)
                    t += 1
                    if n["summed"]:
                        dve.wait_ge(ln_squared, n["squared"] + C8)
                        dve.tensor_tensor(SQ[:, C8 - 2], SQ[:, C8 - 2], SQ[:, C8 - 1], ALU.add)\
                            .then_inc(squares_added, 1)
                a_read(dve, t)
                dve.reciprocal(RSTD[:, :], STD[:, :]).then_inc(ln_rstd, 1)
                dve.wait_ge(ln_rstd, n["n"] + 1)
                for k in range(n["c"]):
                    if not n["ln"]:
                        dve.wait_ge(ln_squared, n["squared"] + k + 1)
                    dve.tensor_tensor(n["src"][:, k], n["src"][:, k], RSTD[:, :], ALU.mult).then_inc(ln_scaled, 1)

            def attention(name):
                a = ATT[name]

                def maxima(h, i=None):
                    for q in range(NT):
                        t = T0[name] + 4 * h + q
                        m_ready(dve, t, i, 8)
                        dve.tensor_tensor(mbank(t)[:, q * P:(q + 1) * P], mbank(t)[:, q * P:(q + 1) * P],
                                          a["mask"], ALU.add).then_inc(att_masked, 1)
                    for q in range(NT):
                        t = T0[name] + 4 * h + q
                        c = 8 * (h % 2) + q
                        dve.wait_ge(att_masked, lin(i, 8, 4 * (a["h0"] + h) + q + 1))
                        dve.tensor_reduce(stat[:, 16 + c:17 + c], mbank(t)[:, 0:(q + 1) * P], AX.X, ALU.max,
                                          negate=True).then_inc(att_max, 1)
                    c = 8 * (h % 2)
                    dve.wait_ge(att_max, lin(i, 8, 4 * (a["h0"] + h + 1)))
                    dve.tensor_scalar(stat[:, c:c + 4], stat[:, 16 + c:20 + c], a["scale"], None, ALU.mult)\
                        .then_inc(att_nm, 1)

                def probabilities(h, i=None):
                    c = 8 * (h % 2) + 4
                    for q in range(NT):
                        m_read(dve, T0[name] + 4 * h + q, i, 8)
                    dve.reciprocal(stat[:, 28 + c:32 + c], stat[:, c:c + 4]).then_inc(att_rs, 1)
                    dve.wait_ge(att_rs, lin(i, 2, a["h0"] + h + 1))
                    for q in range(NT):
                        pr = a["PR"][:, 4 * (h % 2) + q, 0:(q + 1) * P]
                        dve.tensor_scalar(pr, pr, stat[:, 28 + c + q:29 + c + q], None, ALU.mult).then_inc(att_prob, 1)

                def transposed(h, i=None):
                    t = A0[name] + 4 * h
                    for n, (at, w) in ((1, (512, 384)), (2, (896, 384))):
                        a_ready(dve, t + n, i, 8)
                        dve.tensor_copy(a["PTS"][:, at:at + w], abank(t + n)[:, 0:w]).then_inc(a_out[(t + n) % 4], 1)

                def step_of_heads(h, i=None):
                    probabilities(h - 1, i)
                    maxima(h, i)
                    transposed(h - 1, i)

                maxima(0)
                with dve.Fori(0, a["n"] // 2 - 1) as i:
                    step_of_heads(1, i)
                    step_of_heads(2, i)
                step_of_heads(a["n"] - 1)
                probabilities(a["n"] - 1)
                transposed(a["n"] - 1)

            def add_up(k):
                if k:
                    sync()
                    ins = dve.tensor_tensor(SQ[:, 0], R[:, 0] if k == 1 else SQ[:, 0], R[:, k], ALU.add)
                    if k < C8 - 2:
                        step.inc(ins)
                    else:
                        ins.then_inc(resid, 1)

            def res_tiles(stage, alpha):
                for m in range(C8):
                    t = T0[stage] + m
                    m_ready(dve, t)
                    dve.scalar_tensor_tensor(out=R[:, m], in0=X[:, m], scalar=alpha, in1=mbank(t)[:, :],
                                             op0=ALU.mult, op1=ALU.add).then_inc(m_out[t % 4], 1)
                    if m:
                        m_read(dve, t - 1)
                        add_up(m - 1)
                m_read(dve, T0[stage] + 7)

            dve.wait_ge(constants_loaded, 16)
            for h in range(2):
                dve.wait_ge(x_loaded[h], 16)
            norm_dve("ln_in")
            dve.wait_ge(loaded, 32)
            A, B = KT[:, 0], KT[:, 1]
            step.inc(dve.tensor_copy(A, KR.bitcast(I32)))
            sync()
            step.inc(dve.tensor_scalar(A, A, cm("invfreq", 1), None, ALU.mult))
            sync()
            step.inc(dve.tensor_scalar(B, A, float(1.0 / TWO_PI), MAGIC, ALU.mult, ALU.add))
            sync()
            step.inc(dve.tensor_scalar(B, B, MAGIC, None, ALU.subtract))
            c1 = 6.28125
            c2 = float(np.float32(TWO_PI - c1).view(np.uint32).__and__(0xFFFFF000).view(np.float32))
            c3 = float(TWO_PI - c1 - c2)
            for c in (c1, c2, c3):
                sync()
                step.inc(dve.scalar_tensor_tensor(out=A, in0=B, scalar=-c, in1=A, op0=ALU.mult, op1=ALU.add))
            sync()
            lim = 3.1415925
            step.inc(dve.tensor_scalar(RT[:, 1], A, float(np.pi / 2), None, ALU.add))
            sync()
            step.inc(dve.tensor_scalar(B, RT[:, 1], float(np.pi), -TWO_PI, ALU.is_gt, ALU.mult))
            sync()
            step.inc(dve.tensor_tensor(RT[:, 1], RT[:, 1], B, ALU.add))
            sync()
            step.inc(dve.tensor_scalar(RT[:, 1], RT[:, 1], lim, -lim, ALU.min, ALU.max))
            step.inc(dve.tensor_scalar(A, A, lim, -lim, ALU.min, ALU.max))
            sync()
            dve.tensor_scalar(RT[:, 0], A, cm("sign", 1), None, ALU.mult).then_inc(rope_q, 1)
            dve.memset(ZP[:, :, 0:H0], 0.0).then_inc(pads_zero, 1)
            dve.memset(UP[:, :, 0:16], 0.0).then_inc(pads_zero, 1)
            for k in range(4):
                t = T0["in"] + 2 * k
                m_read(dve, t + 1)
                dve.tensor_tensor(ZP[:, k, H0:H0 + S], mbank(t)[:, :], MSG[:, k % 2], ALU.mult).then_inc(conv_in, 1)
                dve.wait_ge(conv_in, k + 1)
                dve.engine_nop().then_inc(m_out[t % 4], 1)
            dve.wait_ge(act_step, 2)
            t = T0["in"] + 13
            m_ready(dve, t)
            dve.tensor_tensor(KT[:, 0], mbank(t)[:, :], COS, ALU.mult).then_inc(m_out[t % 4], 1)
            m_ready(dve, t + 1)
            dve.tensor_tensor(KT[:, 1], mbank(t + 1)[:, :], SIN, ALU.mult).then_inc(m_out[(t + 1) % 4], 1)
            m_read(dve, t)
            m_read(dve, t + 1)
            dve.tensor_tensor(KR, KT[:, 0], KT[:, 1], ALU.add).then_inc(k_rope_in, 1)
            norm_dve("qrms")
            norm_dve("kvrms")
            for g in range(4):
                m_read(dve, T0["in"] + 15 + g)
                src = UP[:, g]
                lo = 0
                for r in range(g + 1):
                    w = 1 << r
                    lo += w
                    dst = PW[:, r % 2]
                    step.inc(dve.tensor_tensor(dst[:, lo:528], src[:, lo:528], src[:, lo - w:528 - w], ALU.add))
                    sync()
                    src = dst
                step.inc(dve.tensor_scalar(PW[:, (g + 1) % 2, 16:16 + S], src[:, 16:16 + S], 1.0 / POOL_W[g], None, ALU.mult))
                sync()
                mean = PW[:, (g + 1) % 2]
                ic = cstt[:, CST0["invcnt"] + 16 * g:CST0["invcnt"] + 16 * g + 16]
                step.inc(dve.tensor_tensor(mean[:, 16:32], src[:, 16:32], ic, ALU.mult))
                sync()
                dve.tensor_tensor(UP[:, g, 16:16 + S], mean[:, 16:16 + S], UP[:, g, 16:16 + S], ALU.subtract)\
                    .then_inc(pool_mixed, 1)
                dve.wait_ge(pool_mixed, g + 1)
            QH = ATT["att"]["QH"]
            for r in range(2):
                t = T0["uq"] + 4 + 2 * r
                m_ready(dve, t)
                dve.tensor_tensor(RT[:, 0], mbank(t)[:, :], COS, ALU.mult).then_inc(m_out[t % 4], 1)
                m_ready(dve, t + 1)
                dve.tensor_tensor(RT[:, 1], mbank(t + 1)[:, :], SIN, ALU.mult).then_inc(m_out[(t + 1) % 4], 1)
                m_read(dve, t)
                m_read(dve, t + 1)
                for j in range(4):
                    q = slice(32 * j, 32 * j + 32)
                    dve.tensor_tensor(QH[64:96, 4 * r + j], RT[q, 0], RT[q, 1], ALU.add).then_inc(rope_q, 1)
                dve.wait_ge(rope_q, 4 * r + 5)
            attention("att")
            dve.memset(MG, 0.0).then_inc(dve_step, 1)
            step.n += 1
            sync()

            def merge(i, conv):
                acc = ZB
                for m in range(C8):
                    gate, t = T0["branch"] + 2 * m, T0["branch"] + 2 * m + 1
                    if i is None:
                        gate, t = conv_gate_tile(m), conv_proj_tile(m)
                    m_ready(dve, t, i, 16)
                    m_read(dve, gate, i, 16)
                    sync()
                    dve.tensor_tensor(RT[:, m % 2], mbank(t)[:, :], MSG[:, m % 2], ALU.mult)\
                        .then_inc(m_out[t % 4], 1)
                    m_read(dve, t, i, 16)
                    step.inc(dve.tensor_tensor(MG[:, m], MG[:, m], RT[:, m % 2], ALU.add))
                    if conv:
                        for j in range(4 * m, min(4 * m + 4, TAPS)):
                            for c in range(2):
                                o = one(acc[:, bass.ds(i * 2 + (8 + c), 1), :])
                                z = one(ZP[:, bass.ds(i * 2 + c, 1), j:j + S])
                                w = part[:, bass.ds(i * (2 * TAPS) + (PAR0["conv_dw"] + c * TAPS + j), 1)]
                                if j == 0:
                                    bb = part[:, bass.ds(i * 2 + (PAR0["conv_b"] + c), 1)]
                                    step.inc(dve.tensor_scalar(o, z, w, bb, ALU.mult, ALU.add))
                                else:
                                    dve.wait_ge(dve_step, step.now(1))
                                    step.inc(dve.scalar_tensor_tensor(out=o, in0=z, scalar=w, in1=o,
                                                                      op0=ALU.mult, op1=ALU.add))

            with dve.Fori(0, 2) as i:
                step.enter(i, C8 + 2 * TAPS)
                merge(i, True)
            step.leave(2)
            sync()
            dve.engine_nop().then_inc(merged, 1)
            norm_dve("convln")
            merge(None, False)
            sync()
            dve.engine_nop().then_inc(merged, 1)
            res_tiles("wout", ALPHA1)
            norm_dve("ln1")
            dve.tensor_copy(TOKI, cm("tokens", 4)).then_inc(ints, 1)
            dve.memset(ZI, 0).then_inc(ints, 1)
            a_read(dve, A0["route"])
            rb = part[:, PAR0["router_bias"]:PAR0["router_bias"] + 16]
            for q in range(NT):
                c = slice(16 * q, 16 * q + 16)
                step.inc(dve.tensor_tensor(SEL[:, c], AFF[:, c], rb, ALU.add))
            step.inc(dve.memset(CMP[:, :], 0.0))

            def order(src, n):
                s4 = src.rearrange("p (g e) -> p g e", e=4)
                c4 = CMP[:, 0:16 * n].rearrange("p (g e j) -> p g e j", e=4, j=4)
                sync()
                for j in range(4):
                    for lo, hi, op in ((0, j, ALU.is_gt), (j + 1, 4, ALU.is_ge)):
                        if hi > lo:
                            b = s4[:, :, j:j + 1].to_broadcast([P, n, hi - lo])
                            step.inc(dve.tensor_tensor(c4[:, :, lo:hi, j], b, s4[:, :, lo:hi], op))
                sync()
                step.inc(dve.tensor_reduce(RANK[:, 0:4 * n], c4, AX.X, ALU.add))
                sync()

            order(SEL[:, 0:64], 16)
            KEEP2 = DTMP
            step.inc(dve.tensor_scalar(KEEP2, RANK[:, 0:64], 2.0, None, ALU.is_lt))
            sync()
            step.inc(dve.tensor_tensor(SEL[:, 64:128], SEL[:, 0:64], KEEP2, ALU.mult))
            step.inc(dve.tensor_tensor(AFF[:, 64:128], AFF[:, 0:64], KEEP2, ALU.mult))
            sync()
            step.inc(dve.tensor_reduce(GSC[:, 0:16], SEL[:, 64:128].rearrange("p (g e) -> p g e", e=4), AX.X, ALU.add))
            order(GSC[:, 0:16], 4)
            step.inc(dve.tensor_scalar(KEEP[:, 0:16], RANK[:, 0:16], 1.0, None, ALU.is_lt))
            sync()
            k3 = KEEP[:, 0:16].rearrange("p (g o) -> p g o", o=1).to_broadcast([P, 16, 4])
            step.inc(dve.tensor_tensor(AFF[:, 0:64].rearrange("p (g e) -> p g e", e=4),
                                       AFF[:, 64:128].rearrange("p (g e) -> p g e", e=4), k3, ALU.mult))
            sync()
            step.inc(dve.tensor_reduce(GSC[:, 0:4], AFF[:, 0:64].rearrange("p (q e) -> p q e", e=16), AX.X, ALU.add))
            sync()
            step.inc(dve.reciprocal(GSC[:, 4:8], GSC[:, 0:4]))
            sync()
            for q in range(NT):
                c = slice(16 * q, 16 * q + 16)
                step.inc(dve.tensor_scalar(WTOK[:, c], AFF[:, c], GSC[:, 4 + q:5 + q], None, ALU.mult))
            dve.tensor_tensor(KIN.rearrange("p (g e) -> p g e", e=4), KEEP2.rearrange("p (g e) -> p g e", e=4), k3,
                              ALU.mult).then_inc(routed, 1)
            t = A0["count"]
            a_ready(dve, t)
            for j in range(4):
                step.inc(dve.tensor_scalar(CNT[:, 16 * j:16 * j + 16], abank(t)[:, 64:80], float(P * j), None, ALU.is_gt))
            sync()
            step.inc(dve.tensor_reduce(DTMP[:, 0:16], CNT[:, 0:64].rearrange("p (j e) -> p e j", e=16), AX.X, ALU.add))
            sync()
            step.inc(dve.tensor_tensor_scan(BEND, ones[:, 0:16], DTMP[:, 0:16], 0.0, ALU.mult, ALU.add))
            sync()
            step.inc(dve.tensor_tensor(BSTART, BEND, DTMP[:, 0:16], ALU.subtract))
            step.inc(dve.tensor_tensor(BCMP.rearrange("p (b e) -> p b e", e=16),
                                       BEND.rearrange("p (o e) -> p o e", o=1).to_broadcast([P, NB, 16]),
                                       cm("iota", NB).rearrange("p (b o) -> p b o", o=1).to_broadcast([P, NB, 16]),
                                       ALU.is_le))
            sync()
            step.inc(dve.tensor_reduce(BEXP, BCMP.rearrange("p (b e) -> p b e", e=16), AX.X, ALU.add))
            step.inc(dve.tensor_scalar(RTMP, cm("iota", MORE_ROUNDS), 2.0, 5.0, ALU.mult, ALU.add))
            sync()
            step.inc(dve.tensor_scalar(RTMP, RTMP, BEND[:, 15:16], None, ALU.is_le))
            sync()
            step.inc(dve.tensor_reduce(RCNT, RTMP, AX.X, ALU.add))
            sync()
            step.inc(dve.tensor_copy(ROUNDS, RCNT))
            for q in range(NT):
                c = slice(16 * q, 16 * q + 16)
                ins = dve.scalar_tensor_tensor(out=DEST[:, c], in0=BSTART, scalar=float(P), in1=abank(t)[:, c],
                                               op0=ALU.mult, op1=ALU.add)
                if q < NT - 1:
                    step.inc(ins)
            ins.then_inc(a_out[t % 4], 1)
            sync()
            a_read(dve, t)
            dve.tensor_scalar(BEI, BEXP, float(EXPERTS - 1), None, ALU.min).then_inc(experts_known, 1)
            step.inc(dve.tensor_scalar(DTMP, KIN, -8192.0, 8192.0, ALU.mult, ALU.add))
            step.inc(dve.tensor_tensor(SEL[:, 64:128], DEST, KIN, ALU.mult))
            sync()
            step.inc(dve.tensor_tensor(DTMP, DTMP, DEST, ALU.add))
            sync()
            step.inc(dve.tensor_reduce(DMM[:, 0:4], DTMP.rearrange("p (q e) -> p q e", e=16), AX.X, ALU.min))
            step.inc(dve.tensor_reduce(DMM[:, 4:8], SEL[:, 64:128].rearrange("p (q e) -> p q e", e=16), AX.X, ALU.max))
            sync()
            dve.tensor_copy(DI, DMM).then_inc(slots_known, 1)
            for n in range(2):
                for q in range(NT):
                    c = slice(16 * q, 16 * q + 16)
                    step.inc(dve.scalar_tensor_tensor(out=CMP[:, 64 * n + 16 * q:64 * n + 16 * q + 16], in0=DEST[:, c],
                                                      scalar=DMM[:, 4 * n + q:4 * n + q + 1], in1=WTOK[:, c],
                                                      op0=ALU.is_equal, op1=ALU.mult))
            sync()
            step.inc(dve.tensor_reduce(DWT, CMP[:, 0:128].rearrange("p (q e) -> p q e", e=16), AX.X, ALU.add))
            def x_evacuate(b, i=None):
                for n in range(3):
                    t = xt_tile(b) + n
                    a_ready(dve, t, i, 8)
                    w = min(3, C8 - 3 * n)
                    at = C8 * (b % 2) + 3 * n
                    dve.tensor_copy(XST[:, at:at + w], abank(t)[:, 0:w * P].rearrange("p (k s) -> p k s", s=P))\
                        .then_inc(a_out[t % 4], 1)

            def product(b, i=None):
                t = gate_tile(b) + 1
                m_read(dve, t - 1, i, 8)
                m_ready(dve, t, i, 8)
                if b or i is not None:
                    a_ready(dve, actt_tile(b - 1), i, 8)
                dve.tensor_tensor(ACTB, mbank(t)[:, :], SGB, ALU.mult).then_inc(m_out[t % 4], 1)

            def half_out(b, i=None):
                t = down_tile(b) + 1
                if b >= 2:
                    dve.wait_ge(yo_sent[b % 2], lin(i, 16, 16 * (b // 2)))
                m_ready(dve, t, i, 8)
                dve.tensor_copy(YO[:, b % 2, S:D], mbank(t)[:, :]).then_inc(m_out[t % 4], 1)

            def block_of_slots(b, i=None):
                x_evacuate(b + 1, i)
                product(b, i)
                half_out(b - 1, i)

            x_evacuate(0)
            x_evacuate(1)
            product(0)
            block_of_slots(1)
            block_of_slots(2)
            block_of_slots(3)
            rounds = rounds_to_run(dve)
            with dve.Fori(0, rounds) as i:
                block_of_slots(4, i)
                block_of_slots(5, i)
            count_skipped(dve, rounds, [(m_out[t % 4], 2, t // 4 + 1) for t in (gate_tile(3) + 1, down_tile(2) + 1)] +
                          [(a_out[t % 4], 2, t // 4 + 1) for t in range(xt_tile(4), xt_tile(4) + 3)])
            half_out(NB - 1)
            def ple(m):
                t = T0["pp"] + m
                m_read(dve, T0["pg"] + m)
                m_ready(dve, t)
                dve.tensor_tensor(PG[:, m], PG[:, m], mbank(t)[:, :], ALU.mult).then_inc(m_out[t % 4], 1)
                m_read(dve, t)
                step.inc(dve.scalar_tensor_tensor(out=R[:, m], in0=X[:, m], scalar=ALPHA1, in1=PG[:, m],
                                                  op0=ALU.mult, op1=ALU.add))

            def token_outputs(q):
                for n in range(2):
                    dve.wait_ge(yg_loaded[2 * q + n], 16)
                    y, w = YG[:, 2 * q + n], DWT[:, 4 * n + q:4 * n + q + 1]
                    if n == 0:
                        step.inc(dve.tensor_scalar(MT[:, q], y, w, None, ALU.mult))
                    else:
                        sync()
                        dve.scalar_tensor_tensor(out=MT[:, q], in0=y, scalar=w, in1=MT[:, q],
                                                 op0=ALU.mult, op1=ALU.add).then_inc(tok_sum, 1)

            for m in range(C8):
                ple(m)
                if m in (5, 6):
                    token_outputs(m - 5)
            for q in range(2, NT):
                token_outputs(q)
            for k in range(C8):
                t = A0["mout"] + k
                a_ready(dve, t)
                dve.tensor_tensor(R[:, k], R[:, k], abank(t)[:, :], ALU.add).then_inc(a_out[t % 4], 1)
                if k:
                    a_read(dve, t - 1)
                    add_up(k - 1)
            a_read(dve, A0["mout"] + 7)
            norm_dve("ln2")
            def log1p_dve(b, n):
                x_, ab, e, u, ln, o = (b[0:16, k] for k in range(6))
                a_read(dve, A0["f" if n else "dt"])
                step.inc(dve.tensor_scalar(ab, x_, -1.0, None, ALU.mult))
                sync()
                dve.tensor_tensor(ab, ab, x_, ALU.max).then_inc(dt_ln, 1)
                dve.wait_ge(dt_e, 2 * n + 1)
                dve.tensor_scalar(u, e, 1.0, None, ALU.add).then_inc(dt_ln, 1)
                dve.wait_ge(dt_ln, 2 * n + 2)
                step.inc(dve.tensor_scalar(o, u, -1.0, None, ALU.add))
                sync()
                step.inc(dve.tensor_tensor(o, e, o, ALU.subtract))
                step.inc(dve.reciprocal(ab, u))
                sync()
                step.inc(dve.tensor_tensor(o, o, ab, ALU.mult))
                sync()
                dve.wait_ge(dt_e, 2 * n + 2)
                step.inc(dve.tensor_tensor(o, o, ln, ALU.add))
                sync()

            x_, ab, e, u, ln, o = (DTB[0:16, k] for k in range(6))
            log1p_dve(DTB, 0)
            step.inc(dve.tensor_scalar(x_, x_, 0.0, None, ALU.max))
            sync()
            step.inc(dve.tensor_tensor(DT[0:16, :], x_, o, ALU.add))
            sync()
            dve.wait_ge(a_neg, 1)
            step.inc(dve.tensor_scalar(ab, DT[0:16, :], stat[0:16, 50:51], -1.0, ALU.mult, ALU.mult))
            sync()
            for c in range(NT):
                cs = slice(c * P, (c + 1) * P)
                ins = dve.tensor_tensor_scan(ACS[0:16, cs], ones[0:16, :], ab[:, cs], 0.0, ALU.mult, ALU.add)
            ins.then_inc(dte, 1)
            step.inc(dve.memset(CHP[:, :, 0:2], 0.0))
            for m in range(2):
                dve.memset(XP[:, m, 0:3], 0.0).then_inc(xbc_conv, 1)
            sync()
            dve.wait_ge(a_neg, 2)
            dve.tensor_tensor(DTE[0:16, :], DTE[0:16, :], DT[0:16, :], ALU.mult).then_inc(dt_ready, 1)

            with dve.Fori(0, 2) as i:
                step.enter(i, 4 * 3)
                for m in range(4):
                    t = T0["s_in"] + 3 * m
                    m_read(dve, t, i, 12)
                    m_ready(dve, t + 1, i, 12)
                    dve.tensor_tensor(CHP[:, m % 2, 2:2 + S], mbank(t + 1)[:, :], CS[:, m % 2], ALU.mult)\
                        .then_inc(m_out[(t + 1) % 4], 1)
                    m_read(dve, t + 1, i, 12)
                    if m == 0:
                        sync()

                    def w(j):
                        return part[:, bass.ds(i * 12 + (PAR0["sc_conv"] + 3 * m + j), 1)]
                    step.inc(dve.tensor_scalar(CT[:, m % 2], CHP[:, m % 2, 2:2 + S], w(2), None, ALU.mult))
                    for j in (1, 0):
                        sync()
                        step.inc(dve.scalar_tensor_tensor(out=CT[:, m % 2], in0=CHP[:, m % 2, j:j + S], scalar=w(j),
                                                          in1=CT[:, m % 2], op0=ALU.mult, op1=ALU.add))
                    sync()
                    m_ready(dve, t + 2, i, 12)
                    dve.tensor_tensor(one(YY[:, bass.ds(i * 4 + m, 1), :]), mbank(t + 2)[:, :], CT[:, m % 2],
                                      ALU.mult).then_inc(m_out[(t + 2) % 4], 1)
                    m_read(dve, t + 2, i, 12)
            step.leave(2)
            with dve.Fori(0, 3) as i:
                step.enter(i, 4 * 3)
                for m in range(4):
                    t = T0["s_in"] + 32 + m
                    m_read(dve, t, i, 4)

                    def w(j):
                        return part[:, bass.ds(i * 16 + (PAR0["ssm_conv"] + 4 * m + j), 1)]
                    step.inc(dve.tensor_scalar(XA[:, m % 2], XP[:, m % 2, 3:3 + S], w(3), None, ALU.mult))
                    for j in (2, 1, 0):
                        sync()
                        ins = dve.scalar_tensor_tensor(out=XA[:, m % 2], in0=XP[:, m % 2, j:j + S], scalar=w(j),
                                                       in1=XA[:, m % 2], op0=ALU.mult, op1=ALU.add)
                        if j:
                            step.inc(ins)
                        else:
                            ins.then_inc(xbc_conv, 1)
            step.leave(3)
            a_read(dve, A0["acst"])
            for c in range(NT):
                for g in range(2):
                    t = A0["xtok"] + 2 * c + g
                    a_ready(dve, t)
                    src = abank(t)[:, :].rearrange("p (h f) -> p h f", f=64)

                    def by_head(n):
                        a = 64 * n + 16 * c + 8 * g
                        return TK[:, a:a + 8].rearrange("p (h o) -> p h o", o=1).to_broadcast([P, 8, 64])
                    if c < NT - 1:
                        dve.tensor_tensor(DX[:, 2 * c + g].rearrange("p (h f) -> p h f", f=64), src, by_head(2),
                                          ALU.mult).then_inc(ssd_dx, 1)
                    dve.tensor_tensor(XDT[:, c, g * 512:g * 512 + 512].rearrange("p (h f) -> p h f", f=64), src,
                                      by_head(1), ALU.mult).then_inc(a_out[t % 4], 1)
            a_read(dve, A0["cb"])
            a_read(dve, A0["cb"] + 1)
            for n in range(6):
                a_read(dve, A0["state"] + n)

            def finish_pair(j):
                t = pair_tile(j)
                a_ready(dve, t)
                dve.scalar_tensor_tensor(out=YY[:, 8 + j], in0=XBC[:, j], scalar=pc("ssm_d", j), in1=abank(t)[:, :],
                                         op0=ALU.mult, op1=ALU.add).then_inc(a_out[t % 4], 1)
                a_read(dve, t)
                dve.tensor_tensor(YY[:, 8 + j], YY[:, 8 + j], ZS[:, j], ALU.mult).then_inc(sc_y, 1)

            for j in range(C8):
                for h in (2 * j, 2 * j + 1):
                    t = head_tile(h)
                    dve.wait_ge(ssd_u, h + 1)
                    for c in range(NT):
                        cs = slice(c * P, (c + 1) * P)
                        if h >= 2 and c == 0:
                            dve.wait_ge(ssd_m, h - 1)
                        dve.scalar_tensor_tensor(out=LB[:, h % 2, cs], in0=abank(t)[:, cs],
                                                 scalar=TK[:, 16 * c + h:16 * c + h + 1], in1=cm("mask_ssd"),
                                                 op0=ALU.subtract, op1=ALU.add).then_inc(ssd_d, 1)
                    dve.wait_ge(ssd_d, 4 * h + 4)
                    dve.engine_nop().then_inc(a_out[t % 4], 1)
                if j:
                    finish_pair(j - 1)
                for h in (2 * j, 2 * j + 1):
                    g = h // 8
                    dve.wait_ge(ssd_l, h + 1)
                    dve.tensor_tensor(MB[:, h % 2], LB[:, h % 2], CBS[:, g], ALU.mult).then_inc(ssd_m, 1)
                    f = slice((h % 8) * 64, (h % 8) * 64 + 64)
                    for c in (1, 2):
                        dve.scalar_tensor_tensor(out=SQ[:, 2 * c + g, f], in0=SQ[:, 2 * (c - 1) + g, f],
                                                 scalar=EB[:, h % 2, (c + 1) * P - 1:(c + 1) * P],
                                                 in1=SQ[:, 2 * c + g, f], op0=ALU.mult, op1=ALU.add)\
                            .then_inc(ssd_prev, 1)
                        dve.wait_ge(ssd_prev, 2 * h + c)
            finish_pair(C8 - 1)
            norm_dve("grms0")
            norm_dve("grms1")
            res_tiles("sout", ALPHA2)
            norm_dve("lnm0")

            def ffn(layer, last):
                for k in range(4):
                    dve.memset(FP[:, k, 0:2], 0.0).then_inc(ffn_conv, 1)
                dve.wait_ge(ffn_conv, 48 * layer + 4)
                with dve.Fori(0, FT // 2) as i:
                    step.enter(i, 8)

                    def conv(k):
                        t = T0[f"up{layer}"] + k
                        m_read(dve, t, i, 4)
                        c = k // 2 + (FT if k % 2 else 0)

                        def w(j):
                            return part[:, bass.ds(i * 6 + (PAR0[f"ffn_conv{layer}"] + 3 * c + j), 1)]
                        b = part[:, bass.ds(i * 2 + (PAR0[f"ffn_b{layer}"] + c), 1)]
                        step.inc(dve.tensor_scalar(TF[:, k], FP[:, k, 2:2 + S], w(2), b, ALU.mult, ALU.add))
                        sync()
                        step.inc(dve.scalar_tensor_tensor(out=TF[:, k], in0=FP[:, k, 1:1 + S], scalar=w(1),
                                                          in1=TF[:, k], op0=ALU.mult, op1=ALU.add))
                        sync()
                        dve.scalar_tensor_tensor(out=TF[:, k], in0=FP[:, k, 0:S], scalar=w(0), in1=TF[:, k],
                                                 op0=ALU.mult, op1=ALU.add).then_inc(ffn_conv, 1)

                    def gate(r):
                        dve.wait_ge(ffn_silu, i * 2 + (FT * layer + r + 1))
                        dve.tensor_tensor(one(G[:, bass.ds(i * 2 + r, 1), :]), TF[:, 2 * r], TF[:, 2 * r + 1],
                                          ALU.mult).then_inc(ffn_g, 1)
                        dve.wait_ge(ffn_g, i * 2 + (FT * layer + r + 1))

                    conv(0)
                    conv(1)
                    conv(2)
                    gate(0)
                    conv(3)
                    gate(1)
                step.leave(FT // 2)
                res_tiles(f"down{layer}", ALPHA2)
                norm_dve(last)

            ffn(0, "lnf0")
            dve.memset(ar(_x["QH"], 32)[64:66], 1.0).then_inc(f_ones, 1)
            log1p_dve(FB, 1)
            x_, ab, o = FB[0:16, 0], FB[0:16, 1], FB[0:16, 5]
            step.inc(dve.tensor_scalar(x_, x_, 0.0, None, ALU.min))
            sync()
            step.inc(dve.tensor_tensor(x_, x_, o, ALU.subtract))
            sync()
            for c in range(NT):
                cs = slice(c * P, (c + 1) * P)
                init = ab[:, c * P - 1:c * P] if c else 0.0
                step.inc(dve.tensor_tensor_scan(ab[:, cs], ones[0:16, :], x_[:, cs], init, ALU.mult, ALU.add))
                sync()
            dve.tensor_scalar(F8[0:16, 0], ab, 8.0, None, ALU.mult).then_inc(f_cum, 1)
            dve.tensor_scalar(F8[0:16, 1], ab, -8.0, None, ALU.mult).then_inc(f_cum, 1)
            attention("fatt")
            res_tiles("fout", ALPHA2)
            norm_dve("lnm1")
            ffn(1, "lnf1")

        @block.gpsimd
        def _(pool):
            def attention(name):
                a = ATT[name]

                def copies(h, i=None):
                    if h >= 2 or i is not None:
                        pool.wait_ge(m_full, lin(i, 8, T0[name] + 4 * (h - 2) + 4))
                    q = a["QH"][0:a["K"], h] if i is None else one(a["QH"][0:a["K"], bass.ds(i * 2 + h, 1), :])
                    pool.tensor_copy(a["QB"][0:a["K"], h % 2], q).then_inc(att_q, 1)
                    pool.wait_ge(att_q, lin(i, 2, a["h0"] + h + 1))
                    if h >= 2 or i is not None:
                        pool.wait_ge(a_full, lin(i, 8, A0[name] + 4 * (h - 2) + 4))
                    at = h * 64 if i is None else None
                    v = a["V"][:, :, at:at + 64] if i is None else a["V"][:, :, bass.ds(i * 128 + h * 64, 64)]
                    pool.tensor_copy(a["VB"][:, 4 * (h % 2):4 * (h % 2) + 4, :], v).then_inc(att_v, 1)
                    pool.wait_ge(att_v, lin(i, 2, a["h0"] + h + 1))

                for h in range(2):
                    copies(h)
                with pool.Fori(0, a["n"] // 2 - 1) as i:
                    copies(2, i)
                    copies(3, i)

            pool.wait_ge(k_rope_in, 1)
            for h in range(HEADS1):
                pool.tensor_copy(ATT["att"]["KH"][64:96, h], KR[64:96, :]).then_inc(k_rope, 1)
                pool.wait_ge(k_rope, h + 1)
            pool.wait_ge(rope_q, 9)
            for j in range(4):
                m_read(pool, T0["uv"] + j)
            attention("att")
            pool.wait_ge(ints, 2)
            pool.dma_start(slot_tok.rearrange("(p b) o -> p (b o)", p=P), ZI).then_inc(table_zero, 16)
            pool.wait_ge(table_zero, 16)
            pool.wait_ge(slots_known, 1)
            for n in range(2 * NT):
                pool.indirect_dma_start(slot_tok, bass.IndirectOffsetOnAxis(ap=DI[:, n:n + 1], axis=0),
                                        TOKI[:, n % NT:n % NT + 1], None).then_inc(table_set, 16)
            pool.wait_ge(table_set, 16 * 2 * NT)
            pool.dma_start(IDX, slot_tok.rearrange("(b p) o -> p (b o)", p=P), allow_slow_non_contiguous=True)\
                .then_inc(table_read, 16)
            pool.wait_ge(table_read, 16)
            pool.wait_ge(xtok_sent, 16)

            for b in range(NB - 1):
                if b >= 2:
                    a_ready(pool, xt_tile(b - 2) + 2)
                    pool.wait_ge(xg_loaded[b % 2], 16 * (b // 2))
                pool.indirect_dma_start(XG[:, b % 2], None, x_tok,
                                        bass.IndirectOffsetOnAxis(ap=IDX[:, b:b + 1], axis=0))\
                    .then_inc(xg_loaded[b % 2], 16)
            pool.wait_ge(y_filled, 16)
            for n in range(2):
                pool.wait_ge(yo_sent[n], 16 * ((NB + 1 - n) // 2))
            for q in range(NT):
                for n in range(2):
                    g = 2 * q + n
                    pool.indirect_dma_start(YG[:, g], None, y_slots.rearrange("b p d -> (b p) d"),
                                            bass.IndirectOffsetOnAxis(ap=DI[:, 4 * n + q:4 * n + q + 1], axis=0))\
                        .then_inc(yg_loaded[g], 16)
            pool.wait_ge(a_full, A0["ln2"])
            pool.dma_start(SEL16[0:16, :], sel16).then_inc(sel_loaded, 16)
            pool.wait_ge(xbc_done, 12)
            for h in range(SSM_H):
                pool.wait_ge(ssd_u, h + 1)
                if h >= 2:
                    a_ready(pool, pair_tile(h // 2 - 1))
                pool.tensor_tensor(CSB[:, h % 2], EB[:, h % 2], XBC[:, 10 + h // 8], ALU.mult).then_inc(ssd_e, 1)
                pool.wait_ge(ssd_e, h + 1)
            pool.wait_ge(f_ones, 1)
            pool.wait_ge(f_cum, 2)
            pool.dma_start(ATT["fatt"]["QH"][65:66], F8[0:16, 0]).then_inc(f_rows, 16)
            pool.dma_start(ATT["fatt"]["KH"][64:65], F8[0:16, 1]).then_inc(f_rows, 16)
            for q in range(NT):
                m_read(pool, T0["fv"] + 4 + q)
            pool.wait_ge(f_rows, 32)
            attention("fatt")


def _blocks(w, cols):
    k = w.shape[0] // P
    return [w[i * P:(i + 1) * P, c:c + P] for c in cols for i in range(k)]


def _tiles(w, a=0, b=None):
    return _blocks(w, range(a, w.shape[1] if b is None else b, P))


def _wide(w, width):
    k = w.shape[0] // P
    return [w[i * P:(i + 1) * P, c + j:c + j + P]
            for c in range(0, w.shape[1], width) for i in range(k) for j in range(0, width, P)]


def _stream(a):
    w_in = a["w_in"][0]
    off = np.cumsum([0, 512, 512, 512, QL, KVL, ROPE])
    kr = w_in[:, off[5]:off[6]]
    krs = np.concatenate([kr[:, 16:], kr[:, :16]], 1)
    b = []
    for j in range(4):
        b += _blocks(w_in, [off[1] + j * P]) + _blocks(w_in, [off[2] + j * P])
    b += _tiles(w_in, off[3], off[5])
    b += _tiles(np.concatenate([kr] * 4, 1)) + _tiles(np.concatenate([krs] * 4, 1))
    b += _tiles(w_in, 0, 512)
    uq = a["w_uq"][0].reshape(QL, HEADS1, NOPE + ROPE)
    b += _tiles(uq[:, :, :NOPE].reshape(QL, -1))
    for r in range(2):
        rope = uq[:, 4 * r:4 * r + 4, NOPE:]
        b += _tiles(rope.reshape(QL, -1)) + _tiles(np.concatenate([rope[..., 16:], rope[..., :16]], -1).reshape(QL, -1))
    ukv = a["w_ukv"][0].reshape(KVL, HEADS1, NOPE + VH)
    b += _tiles(ukv[:, :, :NOPE].reshape(KVL, -1)) + _wide(ukv[:, :, NOPE:].reshape(KVL, -1), 512)
    for g, name in ((0, "pool_proj"), (2, "mla_proj"), (1, "conv_proj")):
        gates = [_blocks(w_in, [off[6] + g * D + m * P]) for m in range(C8)]
        proj = [_blocks(a[name][0], [m * P]) for m in range(C8)]
        if g == 1:
            b += gates[0] + gates[1] + proj[0] + proj[1]
            gates, proj = gates[2:], proj[2:]
        for u, v in zip(gates, proj):
            b += u + v
    b += _tiles(a["w_out"][0]) + _tiles(a["ple_gate"][0])
    for e in range(EXPERTS):
        b += _wide(a["exp_w_up"][0, e], FE) + _wide(a["exp_w_down"][0, e], 512)
    b += _tiles(a["ple_proj"][0])
    s = a["sc_ssm_w_in_2"][0]
    for m in range(C8):
        b += _blocks(s, [D + m * P, 2 * D + m * P, m * P])
    b += _tiles(s, 3 * D, 4 * D + 1536)
    w = _tiles(a["sc_ssm_w_out_2"][0])
    for half in range(2):
        for m in range(4):
            b += w[16 * m + 8 * half:16 * m + 8 * half + 8]
    b += w[64:]

    def ffn(i):
        up = a["ffn_w_up_2"][i]
        r = []
        for m in range(FT):
            r += _blocks(up, [m * P, FF + m * P])
        return r + _tiles(a["ffn_w_down_2"][i])

    b += ffn(0)
    fox = a["fox_w_in_2"][0]
    b += _tiles(fox, 0, 2 * D) + _wide(fox[:, 2 * D:3 * D], 512) + _tiles(a["fox_w_out_2"][0])
    b += ffn(1)
    rows = NSLABS - 12 * (NB - EXPERTS)
    assert len(b) == rows * SLAB, (len(b), rows * SLAB)
    out = np.empty((rows, P, SLAB, P), np.float32)
    for n, x in enumerate(b):
        out[n // SLAB, :, n % SLAB] = x
    return out.reshape(rows, P, SLAB * P)


def _params(a):
    part = np.zeros((P, NPAR), np.float32)

    def put(name, v):
        part[:v.shape[0], PAR0[name]:PAR0[name] + v.shape[1]] = v

    def col(v):
        return v.reshape(-1, P).T

    def taps(w):
        return w.T.reshape(w.shape[1] // P, P, w.shape[0]).transpose(1, 0, 2).reshape(P, -1)

    for name, key in (("ln_in_g", "ln_in_g"), ("ln_in_b", "ln_in_b")):
        put(name, col(a[key]))
    put("b_gate", col(a["b_gate"][0][[0, 2, 1]].reshape(-1)))
    for name, key in (("pool_scale", "pool_scale"), ("conv_b", "conv_b"), ("conv_ln_g", "conv_ln_g"),
                      ("conv_ln_b", "conv_ln_b"), ("q_norm_g", "q_norm_g"), ("kv_norm_g", "kv_norm_g"),
                      ("ln1_g", "ln1_g"), ("ln1_b", "ln1_b"), ("ln2_g", "ln2_g"), ("ln2_b", "ln2_b"),
                      ("ssm_conv_b", "ssm_conv_b_2"), ("ssm_norm_g", "ssm_norm_g_2")):
        put(name, col(a[key][0]))
    put("conv_dw", taps(a["conv_dw"][0]))
    put("sc_conv", taps(a["sc_conv_w_2"][0]))
    put("ssm_conv", taps(a["ssm_conv_w_2"][0]))
    put("ssm_d", col(np.repeat(a["ssm_d_2"][0], SSM_P)))
    for i in range(2):
        put(f"ffn_conv{i}", taps(a["ffn_conv_w_2"][i]))
        put(f"ffn_b{i}", col(a["ffn_conv_b_2"][i]))
        for k, key in (("lnm", "ln_mix"), ("lnf", "ln_ffn")):
            put(f"{k}{i}_g", col(a[f"{key}_g_2"][i]))
            put(f"{k}{i}_b", col(a[f"{key}_b_2"][i]))
    put("dt_bias", a["ssm_dt_bias_2"][0][:, None])
    put("a_log", a["ssm_a_log_2"][0][:, None])
    put("b_f", a["fox_b_f_2"][0][:, None])
    put("router_bias", np.broadcast_to(a["router_bias"], (P, EXPERTS)))

    def rows(w):
        return w.reshape(-1, P, w.shape[1]).transpose(1, 0, 2).reshape(P, -1)

    put("router", rows(a["w_router"]))
    put("w_dt", rows(a["sc_ssm_w_in_2"][0][:, 4 * D + 1536:]))
    put("w_f", rows(a["fox_w_in_2"][0][:, 3 * D:]))
    put("pool_w", a["pool_w"][0].transpose(1, 0, 2).reshape(P, -1))
    return part


def _constants():
    c = np.zeros((P, NCST), np.float32)
    q, k = np.meshgrid(np.arange(P), np.arange(P), indexing="ij")

    def put(name, v):
        c[:, CST0[name]:CST0[name] + v.shape[1]] = v

    put("ident", np.eye(P))
    put("ones", np.ones((P, P)))
    put("mask_fox", np.where(k <= q, 0, NEG))
    put("mask_mla", np.where(k // 64 <= q // 64, 0, NEG))
    put("mask_ssd", np.where(q <= k, 0, NEG))
    put("invcnt", np.broadcast_to(np.concatenate([1.0 / np.minimum(np.arange(16) + 1, w) for w in POOL_W]), (P, 64)))
    put("before", np.where(q < k, 1.0, 0.0))
    put("iota", np.broadcast_to(np.arange(NB), (P, NB)))
    put("tokens", np.arange(P)[:, None] + P * np.arange(NT)[None, :])
    j = np.arange(P) % 16
    put("invfreq", (np.float32(10000.0) ** (-(2 * j).astype(np.float32) / np.float32(ROPE)))[:, None])
    put("sign", np.where(np.arange(P) % 32 < 16, -1.0, 1.0)[:, None])
    for name, v in (("ln_eps", 1e-5), ("rms_eps", 1e-6), ("zero", 0.0), ("one", 1.0), ("halfpi", np.pi / 2)):
        put(name, np.full((P, 1), v))
    sel = np.zeros((16, 16, P), np.float32)
    sel[np.arange(16), np.arange(16)] = 1.0
    return c, sel.reshape(16, -1)


def kernel(**inputs):
    from concourse import bacc
    from concourse.bass_utils import run_bass_kernel_spmd

    a = {k: np.asarray(v) for k, v in inputs.items()}
    cst, sel = _constants()
    arrays = {
        "w_stream": _stream(a),
        "x_t": np.ascontiguousarray(a["x"][0].T),
        "p_t": np.ascontiguousarray(a["p"][0, 0].T),
        "positions": np.ascontiguousarray(np.broadcast_to(a["positions"][0], (P, S))),
        "params": _params(a),
        "constants": cst,
        "sel16": sel,
    }
    nc = bacc.Bacc("TRN2", target_bir_lowering=False, num_devices=1)
    aps = [nc.dram_tensor(k, v.shape, mybir.dt.from_np(v.dtype), kind="ExternalInput").ap() for k, v in arrays.items()]
    x_tok = nc.dram_tensor("x_tok", (S, D), F32, kind="Internal").ap()
    slot_tok = nc.dram_tensor("slot_tok", ((NB + 1) * P, 1), I32, kind="Internal").ap()
    y_slots = nc.dram_tensor("y_slots", (NB, P, D), F32, kind="Internal").ap()
    out = nc.dram_tensor("out_t", (D, S), F32, kind="ExternalOutput").ap()
    build(nc, *aps, x_tok, slot_tok, y_slots, out)
    r = run_bass_kernel_spmd(nc, [arrays], core_ids=[0])
    return np.ascontiguousarray(np.asarray(r.results[0]["out_t"]).T)[None]
```
